# Optimizing a Trainium2 kernel written in Bass

```python
import math
import jax, jax.numpy as jnp
from jax import lax
import numpy as np

D_MODEL = 1024
BATCH = 1
SEQ = 512
DEPTH = 2

HEAD_DIM = 64
NSA_HEADS = 4
NSA_KV_HEADS = 1
CMP_LEN = 32
CMP_STRIDE = 16
CMP_HIDDEN = 128
SEL_BLOCK = 64
SEL_TOP = 16
NSA_WINDOW = 512
MLA_HEADS = 4
MLA_Q_RANK = 256
MLA_KV_RANK = 128
MLA_NOPE = 64
MLA_ROPE = 32
MLA_V = 64
ROPE_THETA = 10000.0
SWA_HEADS = 8
SWA_KV_HEADS = 1
SWA_WINDOW = 128
REL_BUCKETS = 32
REL_MAX_DIST = 512
N_BIAS_HEADS = NSA_HEADS + SWA_HEADS

Q_BLOCK = 128
NORM_EPS = 1e-6
NEG = -1e30
BIG = 1e9

W_A = NSA_HEADS * HEAD_DIM
W_B = MLA_HEADS * MLA_V
W_C = SWA_HEADS * HEAD_DIM
D_MIX = W_A + W_B + W_C

A_Q = NSA_HEADS * HEAD_DIM
A_KV = 6 * NSA_KV_HEADS * HEAD_DIM
A_GATE = 3 * NSA_HEADS
B_CQ = MLA_Q_RANK
B_CKV = MLA_KV_RANK
B_KR = MLA_ROPE
C_Q = SWA_HEADS * HEAD_DIM
C_KV = 2 * SWA_KV_HEADS * HEAD_DIM
IN_SIZES = (A_Q, A_KV, A_GATE, B_CQ, B_CKV, B_KR, C_Q, C_KV, D_MIX)
D_IN = A_Q + A_KV + A_GATE + B_CQ + B_CKV + B_KR + C_Q + C_KV + D_MIX


def rms_norm(x, g):
    xf = x.astype(jnp.float32)
    y = xf * lax.rsqrt(jnp.mean(xf * xf, axis=-1, keepdims=True) + NORM_EPS)
    return (y * g.astype(jnp.float32)).astype(x.dtype)

def split_cols(h):
    outs, o = [], 0
    for s in IN_SIZES:
        outs.append(h[..., o:o + s])
        o += s
    return outs

def t5_bucket(dist):
    dist = jnp.maximum(dist, 0)
    exact = REL_BUCKETS // 2
    large = exact + (jnp.log(jnp.maximum(dist, 1).astype(jnp.float32) / exact)
                     / math.log(REL_MAX_DIST / exact) * (REL_BUCKETS - exact)).astype(jnp.int32)
    large = jnp.minimum(large, REL_BUCKETS - 1)
    return jnp.where(dist < exact, dist, large)

def rope(x, pos):
    half = x.shape[-1] // 2
    inv = ROPE_THETA ** (-jnp.arange(half, dtype=jnp.float32) / half)
    ang = pos.astype(jnp.float32)[:, None] * inv[None, :]
    cos, sin = jnp.cos(ang)[:, None, :], jnp.sin(ang)[:, None, :]
    x1, x2 = x[..., :half].astype(jnp.float32), x[..., half:].astype(jnp.float32)
    return jnp.concatenate([x1 * cos - x2 * sin, x2 * cos + x1 * sin], axis=-1).astype(x.dtype)

def banded_attention(q, k, v, window, bias_heads, sinks):
    B, T, H, dh = q.shape
    G = k.shape[2]
    hpg = H // G
    nq = T // Q_BLOCK
    nb = window // Q_BLOCK
    K = (nb + 1) * Q_BLOCK
    pad = ((0, 0), (nb * Q_BLOCK, 0), (0, 0), (0, 0))

    def band(t):
        tp = jnp.pad(t, pad).reshape(B, nq + nb, Q_BLOCK, G, dh)
        return jnp.concatenate([tp[:, i:i + nq] for i in range(nb + 1)], axis=2)

    kb, vb = band(k), band(v)
    qb = q.reshape(B, nq, Q_BLOCK, G, hpg, dh)
    logits = jnp.einsum('bnqghd,bnkgd->bnghqk', qb, kb).astype(jnp.float32) * (dh ** -0.5)
    i = jnp.arange(Q_BLOCK)[:, None]
    j = jnp.arange(K)[None, :]
    dist = nb * Q_BLOCK + i - j
    kpos = (jnp.arange(nq)[:, None, None] - nb) * Q_BLOCK + j[None]
    mask = (dist >= 0) & (dist < window) & (kpos >= 0)
    bias = bias_heads[:, t5_bucket(dist)].reshape(G, hpg, Q_BLOCK, K)
    logits = jnp.where(mask[None, :, None, None], logits + bias, NEG)
    if sinks is None:
        p = jax.nn.softmax(logits, axis=-1)
    else:
        s = jnp.broadcast_to(sinks.reshape(G, hpg, 1, 1).astype(jnp.float32), logits.shape[:-1] + (1,))
        p = jax.nn.softmax(jnp.concatenate([logits, s], axis=-1), axis=-1)[..., :-1]
    out = jnp.einsum('bnghqk,bnkgd->bnqghd', p.astype(v.dtype), vb)
    return out.reshape(B, T, H, dh)

def causal_block_attention(q, k, v, scale):
    B, T, H, dk = q.shape
    nq = T // Q_BLOCK
    qb = q.reshape(B, nq, Q_BLOCK, H, dk).transpose(1, 0, 2, 3, 4)
    kpos = jnp.arange(T)

    def one(args):
        qc, n = args
        logits = jnp.einsum('bqhd,bkhd->bhqk', qc, k).astype(jnp.float32) * scale
        qpos = n * Q_BLOCK + jnp.arange(Q_BLOCK)
        mask = kpos[None, :] <= qpos[:, None]
        p = jax.nn.softmax(jnp.where(mask, logits, NEG), axis=-1)
        return jnp.einsum('bhqk,bkhd->bqhd', p.astype(v.dtype), v)

    out = lax.map(one, (qb, jnp.arange(nq)))
    return out.transpose(1, 0, 2, 3, 4).reshape(B, T, H, v.shape[-1])

def nsa_attention(q, kv, gates, cmp_pos, cmp_w1, cmp_w2, bias_heads):
    B, T, H, dh = q.shape
    G = kv.shape[3]
    hpg = H // G
    scale = dh ** -0.5
    k_cmp, v_cmp, k_slc, v_slc, k_win, v_win = [kv[:, :, i] for i in range(6)]
    pos = jnp.arange(T)
    qg = q.reshape(B, T, G, hpg, dh)

    nc = T // CMP_STRIDE - 1

    def compress(t, pe, w1, w2):
        ch = t.reshape(B, T // CMP_STRIDE, CMP_STRIDE, G, dh)
        blk = jnp.concatenate([ch[:, :-1], ch[:, 1:]], axis=2) + pe[:, None, :]
        blk = blk.transpose(0, 1, 3, 2, 4).reshape(B, nc, G, CMP_LEN * dh)
        return jax.nn.silu(blk @ w1) @ w2

    kc = compress(k_cmp, cmp_pos[0], cmp_w1[0], cmp_w2[0])
    vc = compress(v_cmp, cmp_pos[1], cmp_w1[1], cmp_w2[1])
    lc = jnp.einsum('btghd,bcgd->bghtc', qg, kc).astype(jnp.float32) * scale
    cend = jnp.arange(nc) * CMP_STRIDE + CMP_LEN - 1
    dist_c = pos[:, None] - cend[None, :]
    valid_c = dist_c >= 0
    lc = lc + bias_heads[:, t5_bucket(dist_c)].reshape(G, hpg, T, nc)
    p_c = jax.nn.softmax(jnp.where(valid_c, lc, NEG), axis=-1) * valid_c
    o_cmp = jnp.einsum('bghtc,bcgd->btghd', p_c.astype(vc.dtype), vc)

    ns = T // SEL_BLOCK
    n_top = min(SEL_TOP, ns)
    sstart = np.arange(ns) * SEL_BLOCK
    cstart = np.arange(nc) * CMP_STRIDE
    overlap = (np.clip(np.minimum(cstart[:, None] + CMP_LEN, sstart[None, :] + SEL_BLOCK)
                       - np.maximum(cstart[:, None], sstart[None, :]), 0, None) / CMP_STRIDE).astype(np.float32)
    imp = jnp.einsum('bghtc,cs->bgts', p_c, jnp.asarray(overlap))
    blk = jnp.arange(ns)[None, :]
    cur = (pos // SEL_BLOCK)[:, None]
    forced = (blk == 0) | (blk == cur) | (blk == cur - 1)
    imp = jnp.where(forced, BIG, jnp.where(blk <= cur, imp, -BIG))
    _, idx = lax.top_k(imp, n_top)

    ksb = k_slc.reshape(B, ns, SEL_BLOCK, G, dh).transpose(0, 3, 1, 2, 4)
    vsb = v_slc.reshape(B, ns, SEL_BLOCK, G, dh).transpose(0, 3, 1, 2, 4)
    nq = T // Q_BLOCK
    qch = qg.reshape(B, nq, Q_BLOCK, G, hpg, dh).transpose(1, 0, 3, 4, 2, 5)
    ich = idx.reshape(B, G, nq, Q_BLOCK, n_top).transpose(2, 0, 1, 3, 4)
    gather = jax.vmap(jax.vmap(lambda blocks, ids: blocks[ids]))
    tok = jnp.arange(SEL_BLOCK)
    bias_g = bias_heads.reshape(G, hpg, REL_BUCKETS)
    group_bias = jax.vmap(lambda tab, bk: jnp.moveaxis(tab[:, bk], 0, 1), in_axes=(0, 1), out_axes=1)
    nk = n_top * SEL_BLOCK

    def sel_block(args):
        qc, ic, n = args
        kg = gather(ksb, ic).reshape(B, G, Q_BLOCK, nk, dh)
        vg = gather(vsb, ic).reshape(B, G, Q_BLOCK, nk, dh)
        kpos = (ic[..., None] * SEL_BLOCK + tok).reshape(B, G, Q_BLOCK, nk)
        qpos = n * Q_BLOCK + jnp.arange(Q_BLOCK)
        dist = qpos[:, None] - kpos
        l = jnp.einsum('bghqd,bgqkd->bghqk', qc, kg).astype(jnp.float32) * scale
        l = l + group_bias(bias_g, t5_bucket(dist))
        p = jax.nn.softmax(jnp.where((dist >= 0)[:, :, None], l, NEG), axis=-1)
        return jnp.einsum('bghqk,bgqkd->bqghd', p.astype(vg.dtype), vg)

    o_slc = lax.map(sel_block, (qch, ich, jnp.arange(nq)))
    o_slc = o_slc.transpose(1, 0, 2, 3, 4, 5).reshape(B, T, H, dh)

    o_win = banded_attention(q, k_win, v_win, NSA_WINDOW, bias_heads, None)

    g = jax.nn.sigmoid(gates.astype(jnp.float32)).astype(q.dtype)
    o = (g[..., 0:1] * o_cmp.reshape(B, T, H, dh) + g[..., 1:2] * o_slc + g[..., 2:3] * o_win)
    return o.reshape(B, T, H * dh)

def hybrid_layer(x, w_in, w_out, g_pre, g_post, cmp_pos, cmp_w1, cmp_w2,
                 q_norm, w_uq, kv_norm, w_ukv, sinks, rel_bias):
    B, T, _ = x.shape
    pos = jnp.arange(T)
    h = rms_norm(x, g_pre)
    a_q, a_kv, a_g, b_cq, b_ckv, b_kr, c_q, c_kv, z = split_cols(h @ w_in)

    o_a = nsa_attention(a_q.reshape(B, T, NSA_HEADS, HEAD_DIM),
                        a_kv.reshape(B, T, 6, NSA_KV_HEADS, HEAD_DIM),
                        a_g.reshape(B, T, NSA_HEADS, 3),
                        cmp_pos, cmp_w1, cmp_w2, rel_bias[:NSA_HEADS])

    qb = (rms_norm(b_cq, q_norm) @ w_uq).reshape(B, T, MLA_HEADS, MLA_NOPE + MLA_ROPE)
    q_full = jnp.concatenate([qb[..., :MLA_NOPE], rope(qb[..., MLA_NOPE:], pos)], axis=-1)
    kvb = (rms_norm(b_ckv, kv_norm) @ w_ukv).reshape(B, T, MLA_HEADS, MLA_NOPE + MLA_V)
    k_rope = rope(b_kr.reshape(B, T, 1, MLA_ROPE), pos)
    k_full = jnp.concatenate([kvb[..., :MLA_NOPE],
                              jnp.broadcast_to(k_rope, (B, T, MLA_HEADS, MLA_ROPE))], axis=-1)
    o_b = causal_block_attention(q_full, k_full, kvb[..., MLA_NOPE:], (MLA_NOPE + MLA_ROPE) ** -0.5)

    ckv = c_kv.reshape(B, T, 2, SWA_KV_HEADS, HEAD_DIM)
    o_c = banded_attention(c_q.reshape(B, T, SWA_HEADS, HEAD_DIM), ckv[:, :, 0], ckv[:, :, 1],
                           SWA_WINDOW, rel_bias[NSA_HEADS:], sinks)

    mixed = jnp.concatenate([o_a, o_b.reshape(B, T, W_B), o_c.reshape(B, T, W_C)], axis=-1) * jax.nn.silu(z)
    return x + rms_norm(mixed @ w_out, g_post)

def first_inputs(seed: int = 0) -> dict:
    key = jax.random.key(seed)
    ks = jax.random.split(key, 14)
    f32 = jnp.float32

    def nrm(k, shape, scale):
        return jax.random.normal(k, shape, f32) * scale

    return {
        'x': nrm(ks[0], (BATCH, SEQ, D_MODEL), 1.0),
        'w_in': nrm(ks[1], (DEPTH, D_MODEL, D_IN), D_MODEL ** -0.5),
        'w_out': nrm(ks[2], (DEPTH, D_MIX, D_MODEL), D_MIX ** -0.5),
        'norm_pre': 1.0 + nrm(ks[3], (DEPTH, D_MODEL), 0.05),
        'norm_post': 1.0 + nrm(ks[4], (DEPTH, D_MODEL), 0.05),
        'cmp_pos': nrm(ks[5], (DEPTH, 2, CMP_LEN, HEAD_DIM), 0.1),
        'cmp_w1': nrm(ks[6], (DEPTH, 2, CMP_LEN * HEAD_DIM, CMP_HIDDEN), (CMP_LEN * HEAD_DIM) ** -0.5),
        'cmp_w2': nrm(ks[7], (DEPTH, 2, CMP_HIDDEN, HEAD_DIM), CMP_HIDDEN ** -0.5),
        'mla_q_norm': 1.0 + nrm(ks[8], (DEPTH, MLA_Q_RANK), 0.05),
        'mla_w_uq': nrm(ks[9], (DEPTH, MLA_Q_RANK, MLA_HEADS * (MLA_NOPE + MLA_ROPE)), MLA_Q_RANK ** -0.5),
        'mla_kv_norm': 1.0 + nrm(ks[10], (DEPTH, MLA_KV_RANK), 0.05),
        'mla_w_ukv': nrm(ks[11], (DEPTH, MLA_KV_RANK, MLA_HEADS * (MLA_NOPE + MLA_V)), MLA_KV_RANK ** -0.5),
        'swa_sinks': nrm(ks[12], (DEPTH, SWA_HEADS), 0.5),
        'rel_bias': nrm(ks[13], (N_BIAS_HEADS, REL_BUCKETS), 0.5),
    }

def first_block(x, w_in, w_out, norm_pre, norm_post, cmp_pos, cmp_w1, cmp_w2,
              mla_q_norm, mla_w_uq, mla_kv_norm, mla_w_ukv, swa_sinks, rel_bias):
    for l in range(DEPTH):
        x = hybrid_layer(x, w_in[l], w_out[l], norm_pre[l], norm_post[l],
                         cmp_pos[l], cmp_w1[l], cmp_w2[l],
                         mla_q_norm[l], mla_w_uq[l], mla_kv_norm[l], mla_w_ukv[l],
                         swa_sinks[l], rel_bias)
    return x


D_MIX_2 = D_MODEL
D_POOL = D_MIX_2 // 2
D_HGRN = D_MIX_2 - D_POOL
POOL_WINDOWS = (2, 4, 8, 16)
N_POOL_GROUPS = len(POOL_WINDOWS)
POOL_GROUP_DIM = D_POOL // N_POOL_GROUPS
HGRN_HEADS = 4
HGRN_HEAD_DIM = D_HGRN // HGRN_HEADS
CHUNK = 64
D_IN_2 = D_POOL + 4 * D_HGRN
D_FF = ((8 * D_MODEL // 3 + 127) // 128) * 128
ALPHA = (2.0 * DEPTH) ** 0.25
BETA = (8.0 * DEPTH) ** -0.25
LN_EPS = 1e-5
RMS_EPS = 1e-6


def layer_norm(x, g, b):
    x32 = x.astype(jnp.float32)
    mu = jnp.mean(x32, axis=-1, keepdims=True)
    var = jnp.mean(jnp.square(x32 - mu), axis=-1, keepdims=True)
    y = (x32 - mu) * lax.rsqrt(var + LN_EPS) * g.astype(jnp.float32) + b.astype(jnp.float32)
    return y.astype(x.dtype)

def swiglu(x, w_gate, w_up, w_down):
    return (jax.nn.silu(x @ w_gate) * (x @ w_up)) @ w_down

def multiscale_pool(u, pool_w, pool_scale):
    B, S, _ = u.shape
    u32 = u.astype(jnp.float32).reshape(B, S, N_POOL_GROUPS, POOL_GROUP_DIM)
    c = jnp.cumsum(u32, axis=1)
    pos = jnp.arange(S)
    means = []
    for g, w in enumerate(POOL_WINDOWS):
        cg = c[:, :, g]
        lag = jnp.pad(cg, ((0, 0), (w, 0), (0, 0)))[:, :S]
        cnt = jnp.minimum(pos + 1, w).astype(jnp.float32)[None, :, None]
        means.append((cg - lag) / cnt)
    pooled = jnp.stack(means, axis=2) - u32
    y = jnp.einsum('bsgc,gcd->bsgd', pooled.astype(u.dtype), pool_w)
    return y.reshape(B, S, D_POOL) * pool_scale

def hgrn2_recurrence(q, f_raw, v, lb):
    B, S, _ = q.shape
    n = S // CHUNK
    log_f = jnp.logaddexp(jnp.log(lb), jnp.log1p(-lb) + jax.nn.log_sigmoid(f_raw))
    k = (1.0 - lb) * jax.nn.sigmoid(-f_raw)
    q = q * (HGRN_HEAD_DIM ** -0.5)

    def heads(t):
        return t.reshape(B, n, CHUNK, HGRN_HEADS, HGRN_HEAD_DIM).transpose(1, 0, 3, 2, 4)

    causal = jnp.tril(jnp.ones((CHUNK, CHUNK), dtype=bool))[:, :, None]

    def step(state, inp):
        q_c, k_c, v_c, g_c = inp
        b = jnp.cumsum(g_c, axis=2)
        o_inter = jnp.einsum('bhtd,bhdv->bhtv', q_c * jnp.exp(b), state)
        rel = b[:, :, :, None, :] - b[:, :, None, :, :]
        decay = jnp.exp(jnp.where(causal, rel, -jnp.inf))
        scores = jnp.einsum('bhtd,bhsd,bhtsd->bhts', q_c, k_c, decay)
        o_intra = jnp.einsum('bhts,bhsv->bhtv', scores, v_c)
        b_last = b[:, :, -1:, :]
        k_dec = k_c * jnp.exp(b_last - b)
        new_state = jnp.exp(b_last[:, :, 0, :])[..., None] * state + jnp.einsum('bhsd,bhsv->bhdv', k_dec, v_c)
        return new_state, o_inter + o_intra

    s0 = jnp.zeros((B, HGRN_HEADS, HGRN_HEAD_DIM, HGRN_HEAD_DIM), jnp.float32)
    _, o = lax.scan(step, s0, (heads(q), heads(k), heads(v), heads(log_f)))
    return o.transpose(1, 0, 3, 2, 4).reshape(B, S, D_HGRN)

def head_rms_norm(o, g):
    B, S, _ = o.shape
    o = o.reshape(B, S, HGRN_HEADS, HGRN_HEAD_DIM)
    o = o * lax.rsqrt(jnp.mean(jnp.square(o), axis=-1, keepdims=True) + RMS_EPS) * g.astype(jnp.float32)
    return o.reshape(B, S, D_HGRN)

def second_inputs(seed: int = 0) -> dict:
    key = jax.random.key(seed)
    ks = jax.random.split(key, 16)
    nrm = jax.random.normal
    f32 = jnp.float32
    x = nrm(ks[0], (BATCH, SEQ, D_MODEL), f32)
    w_in = nrm(ks[1], (DEPTH, D_MODEL, D_IN_2), f32) * D_MODEL ** -0.5
    pool_w = nrm(ks[2], (DEPTH, N_POOL_GROUPS, POOL_GROUP_DIM, POOL_GROUP_DIM), f32) * POOL_GROUP_DIM ** -0.5
    pool_scale = 1.0 + 0.02 * nrm(ks[3], (DEPTH, D_POOL), f32)
    lb_param = 0.5 * nrm(ks[4], (DEPTH, D_HGRN), f32)
    hgrn_norm_g = 1.0 + 0.02 * nrm(ks[5], (DEPTH, HGRN_HEAD_DIM), f32)
    w_out = nrm(ks[6], (DEPTH, D_MIX_2, D_MODEL), f32) * (D_MIX_2 ** -0.5 * BETA)
    ffn1_gate = nrm(ks[7], (DEPTH, D_MODEL, D_FF), f32) * D_MODEL ** -0.5
    ffn1_up = nrm(ks[8], (DEPTH, D_MODEL, D_FF), f32) * D_MODEL ** -0.5
    ffn1_down = nrm(ks[9], (DEPTH, D_FF, D_MODEL), f32) * (D_FF ** -0.5 * BETA)
    ffn2_gate = nrm(ks[10], (DEPTH, D_MODEL, D_FF), f32) * D_MODEL ** -0.5
    ffn2_up = nrm(ks[11], (DEPTH, D_MODEL, D_FF), f32) * D_MODEL ** -0.5
    ffn2_down = nrm(ks[12], (DEPTH, D_FF, D_MODEL), f32) * (D_FF ** -0.5 * BETA)
    ln_g = 1.0 + 0.02 * nrm(ks[13], (DEPTH, 3, D_MODEL), f32)
    ln_b = 0.02 * nrm(ks[14], (DEPTH, 3, D_MODEL), f32)
    return {"x": x, "w_in": w_in, "pool_w": pool_w, "pool_scale": pool_scale, "lb_param": lb_param,
            "hgrn_norm_g": hgrn_norm_g, "w_out": w_out, "ffn1_gate": ffn1_gate, "ffn1_up": ffn1_up,
            "ffn1_down": ffn1_down, "ffn2_gate": ffn2_gate, "ffn2_up": ffn2_up, "ffn2_down": ffn2_down,
            "ln_g": ln_g, "ln_b": ln_b}

def second_block(x, w_in, pool_w, pool_scale, lb_param, hgrn_norm_g, w_out, ffn1_gate, ffn1_up, ffn1_down,
              ffn2_gate, ffn2_up, ffn2_down, ln_g, ln_b):
    f32 = jnp.float32
    lb_all = jnp.cumsum(jax.nn.softmax(lb_param.astype(f32), axis=0), axis=0)
    lb_all = lb_all - lb_all[0:1]
    for l in range(DEPTH):
        x = layer_norm(ALPHA * x + 0.5 * swiglu(x, ffn1_gate[l], ffn1_up[l], ffn1_down[l]), ln_g[l, 0], ln_b[l, 0])
        h = x @ w_in[l]
        u = h[..., :D_POOL]
        q, f_raw, v, g = jnp.split(h[..., D_POOL:], 4, axis=-1)
        y_pool = multiscale_pool(u, pool_w[l], pool_scale[l])
        o = hgrn2_recurrence(q.astype(f32), f_raw.astype(f32), v.astype(f32), lb_all[l])
        y_hgrn = head_rms_norm(o, hgrn_norm_g[l]) * jax.nn.silu(g.astype(f32))
        mix = jnp.concatenate([y_pool.astype(x.dtype), y_hgrn.astype(x.dtype)], axis=-1) @ w_out[l]
        x = layer_norm(ALPHA * x + mix, ln_g[l, 1], ln_b[l, 1])
        x = layer_norm(ALPHA * x + 0.5 * swiglu(x, ffn2_gate[l], ffn2_up[l], ffn2_down[l]), ln_g[l, 2], ln_b[l, 2])
    return x


def setup_inputs(seed=0):
    out = dict(first_inputs(seed))
    for name, value in second_inputs(seed + 1).items():
        if name != "x":
            out[name + "_2"] = value
    return out


def reference(
    x, w_in, w_out, norm_pre, norm_post, cmp_pos, cmp_w1, cmp_w2, mla_q_norm, mla_w_uq,
    mla_kv_norm, mla_w_ukv, swa_sinks, rel_bias, w_in_2, pool_w_2, pool_scale_2, lb_param_2,
    hgrn_norm_g_2, w_out_2, ffn1_gate_2, ffn1_up_2, ffn1_down_2, ffn2_gate_2, ffn2_up_2,
    ffn2_down_2, ln_g_2, ln_b_2,
):
    x = first_block(
        x, w_in, w_out, norm_pre, norm_post, cmp_pos, cmp_w1, cmp_w2, mla_q_norm, mla_w_uq,
        mla_kv_norm, mla_w_ukv, swa_sinks, rel_bias,
    )
    return second_block(
        x, w_in_2, pool_w_2, pool_scale_2, lb_param_2, hgrn_norm_g_2, w_out_2, ffn1_gate_2,
        ffn1_up_2, ffn1_down_2, ffn2_gate_2, ffn2_up_2, ffn2_down_2, ln_g_2, ln_b_2,
    )


_drawn_inputs = setup_inputs


def setup_inputs(seed=0):
    import zlib

    import numpy as np

    out = dict(_drawn_inputs(seed))
    spreads = {}
    factors = {'swa_sinks': 4.89, 'pool_scale_2': 8.0, 'hgrn_norm_g_2': 8.0}
    for name, (base, spread) in spreads.items():
        noise = np.random.default_rng([zlib.crc32(name.encode()), seed]).standard_normal(out[name].shape)
        drawn = base * np.exp(spread * noise) if base else spread * noise
        out[name] = __import__('jax').numpy.asarray(drawn.astype(out[name].dtype))
    for name, factor in factors.items():
        out[name] = (out[name] * factor).astype(out[name].dtype)
    return out
```

```python
import math
from contextlib import ExitStack

import numpy as np

import concourse.bass as bass
from concourse import mybir

ALU = mybir.AluOpType
ACT = mybir.ActivationFunctionType
AX_X = mybir.AxisListType.X
F32 = mybir.dt.float32
F32R = mybir.dt.float32r

P = 128
T = 512
D = 1024
DC = D // P
NT = T // P
DEPTH = 2
HD = 64
A_HEADS, B_HEADS, C_HEADS = 4, 4, 8
CMP_LEN, CMP_STRIDE = 32, 16
NCMP = T // CMP_STRIDE - 1
ROPE = 32
BKT = 32
SWA_WINDOW = 128
NEG = -1e30
NORM_EPS = 1e-6
LN_EPS = 1e-5
RMS_EPS = 1e-6
FF = ((8 * D // 3 + 127) // 128) * 128
FC = FF // P
KH = FC // 2
ALPHA = (2.0 * DEPTH) ** 0.25
HH = 4
POOL_WINDOWS = (2, 4, 8, 16)
PADT = max(POOL_WINDOWS)

(C_QA, C_KSLC, C_KWIN, C_V, C_CMP, C_CQ, C_CKV, C_KR, C_QC, C_KC, C_GATE, C_Z, N_IN) = (
    0, 2, 3, 4, 5, 6, 8, 9, 10, 14, 15, 16, 24)
D_U, D_Q, D_F, D_V, D_G, N_IN2 = 0, 4, 8, 12, 16, 20

S_GPRE, S_GPOST, S_QN, S_KVN, S_SINK, S_PE = 0, 8, 16, 18, 19, 27
S_UQ = S_PE + CMP_LEN
S_UK = S_UQ + 2 * B_HEADS * P
S_UV = S_UK + B_HEADS * HD
S_W2K = S_UV + B_HEADS * HD
S_W2V = S_W2K + P
N_S1 = S_W2V + HD
Q_LNG, Q_LNB, Q_PS, Q_HG, Q_LB, Q_FIRST, Q_NOTFIRST, Q_PW = 0, 24, 48, 52, 53, 61, 62, 63
N_S2 = Q_PW + HH * P
K_ID, K_EX, K_TRIG, K_CAUSAL, K_ROWOK = 0, P, 2 * P, 2 * P + T, 2 * P + 2 * T
N_K1 = K_ROWOK + 1
MASKED = (16, 8, 4, 2, 1, 0)
M_MASK = P
M_INV = M_MASK + 32 * len(MASKED)
N_K2 = M_INV + HH * T

RAW_RING = 4
HL_RING = 2
UNROLL = 4



class Stream:

    def __init__(self, nc, ctx, tag, kp):
        self.kp = kp
        self.raw = ctx.enter_context(nc.sbuf_tensor(f"{tag}_raw", [P, RAW_RING, kp * P], F32))
        self.hi = ctx.enter_context(nc.sbuf_tensor(f"{tag}_hi", [P, HL_RING, kp * P], F32R))
        self.lo = ctx.enter_context(nc.sbuf_tensor(f"{tag}_lo", [P, HL_RING, kp * P], F32R))


def load_weights(sp, st, sems, dram, base, n):
    w_loaded, w_split = sems["w_loaded"], sems["w_split"]
    with sp.Fori(0, n // UNROLL) as j:
        for u in range(UNROLL):
            sp.wait_ge(w_split, j * UNROLL + u + 1)
            sp.dma_start(st.raw[:, u, :], dram[bass.ds(base + j * UNROLL + u, 1)].rearrange("o p k -> (o p) k")
                         ).then_inc(w_loaded[u], 16)


def split_weights(v, st, sems, n):
    w_loaded, hi_made, w_split, mm_done = (sems[k] for k in ("w_loaded", "hi_made", "w_split", "mm_done"))
    with v.Fori(0, n // UNROLL) as j:
        for u in range(UNROLL):
            s = u % HL_RING
            v.wait_ge(w_loaded[u], j * 16 + 16)
            v.wait_ge(mm_done, j * UNROLL + u + 1)
            v.tensor_copy(st.hi[:, s, :], st.raw[:, u, :]).then_inc(hi_made, 1)
            v.wait_ge(hi_made, j * UNROLL + u + 1)
            v.tensor_tensor(st.lo[:, s, :], st.raw[:, u, :], st.hi[:, s, :].bitcast(F32), ALU.subtract
                            ).then_inc(w_split, 1)


def dense_products(pe, st, sems, n, xh, xl, banks, pieces=1):
    w_split, mm_done, out_taken = (sems[k] for k in ("w_split", "mm_done", "out_taken"))
    per = UNROLL // pieces
    with pe.Fori(0, n // UNROLL) as j:
        for u in range(UNROLL):
            out = banks[(u // pieces) % len(banks)]
            h = u % pieces
            pe.wait_ge(w_split, j * UNROLL + u + 1 + RAW_RING)
            if h == 0:
                pe.wait_ge(out_taken, j * per + u // pieces + 1)
            for k in range(st.kp):
                wh = st.hi[:, u % HL_RING, k * P:(k + 1) * P]
                wl = st.lo[:, u % HL_RING, k * P:(k + 1) * P]
                kx = h * st.kp + k
                pe.matmul(out[:], wh, xh[:, kx, :], start=kx == 0, stop=False)
                pe.matmul(out[:], wh, xl[:, kx, :], start=False, stop=False)
                mm = pe.matmul(out[:], wl, xh[:, kx, :], start=False, stop=kx == pieces * st.kp - 1)
            mm.then_inc(mm_done, 1)


def linker(eng, sem):
    count = [0]

    def link(ins):
        count[0] += 1
        ins.then_inc(sem, 1)
        eng.wait_ge(sem, count[0])
    return link


class Kit:

    def __init__(self, nc, ctx, dram):
        self.nc, self.sem_ctx, self.d = nc, ctx, dram
        self.groups = {}

    def sems(self, tag, names, ring=()):
        if tag not in self.groups:
            g, nums = {}, []
            for n in names:
                if n in ring:
                    g[n] = [self.sem_ctx.enter_context(self.nc.semaphore(f"{tag}_{n}{u}")) for u in range(RAW_RING)]
                    nums += [s.num for s in g[n]]
                else:
                    g[n] = self.sem_ctx.enter_context(self.nc.semaphore(f"{tag}_{n}"))
                    nums.append(g[n].num)
            runs = []
            for n in sorted(nums):
                if runs and runs[-1].stop == n:
                    runs[-1] = range(runs[-1].start, n + 1)
                else:
                    runs.append(range(n, n + 1))
            self.groups[tag] = (g, runs)
        return self.groups[tag][0]

    def clear(self, pool, tag):
        for run in self.groups[tag][1]:
            pool.sem_clear(run)


DENSE = ("w_loaded", "hi_made", "w_split", "mm_done", "out_taken")
OUT1_SEMS = DENSE + ("mhi_made", "mlo_made", "sq_made", "sq_summed", "ln_made", "rstd_made", "scaled", "x_made")
LN_SEMS = DENSE + ("alpha", "r_made", "summed", "mean_made", "cent_made", "sq_made", "sq_summed", "ln_made",
                   "rstd_made", "norm_made", "x_made", "xhi_made", "xlo_made")



def phase_start(kit):
    nc, d = kit.nc, kit.d
    bank = kit.bank
    with ExitStack() as ctx:
        def sb(name, shape):
            return ctx.enter_context(nc.sbuf_tensor(name, shape, F32))
        rel = sb("rel", [BKT, A_HEADS + C_HEADS])
        hot = sb("hot", [BKT, 2 * T])
        msk = sb("msk", [A_HEADS + C_HEADS, 2 * T])
        vec = sb("vec", [A_HEADS + C_HEADS, 2 * T])
        ha = sb("ha", [P, A_HEADS, 896])
        hc = sb("hc", [P, C_HEADS, 256])
        s = kit.sems("start", ("loaded", "x_loaded", "vec_mm", "vec_made", "stored", "read_a", "read_c",
                               "turned", "kept", "set"))
        block = ctx.enter_context(nc.Block())

        @block.sync
        def _(sp):
            for dst, src in ((rel, "rel"), (hot, "hot"), (msk, "msk"), (kit.k1, "k1")):
                sp.dma_start(dst[:], d[src]).then_inc(s["loaded"], 16)
            sp.dma_start(kit.x[:], d["x"]).then_inc(s["x_loaded"], 16)
            sp.wait_ge(s["vec_made"], 2)
            sp.dma_start(d["scratch"], vec[:]).then_inc(s["stored"], 16)
            sp.wait_ge(s["stored"], 16)
            src = d["scratch"]
            sp.dma_start(ha[:], bass.AP(src.tensor, src.offset, [[1, P], [2 * T, A_HEADS], [1, 896]])
                         ).then_inc(s["read_a"], 16)
            sp.dma_start(hc[:], bass.AP(src.tensor, src.offset + A_HEADS * 2 * T + 256,
                                        [[1, P], [2 * T, C_HEADS], [1, 256]])).then_inc(s["read_c"], 16)
            sp.wait_ge(s["x_loaded"], 16)

        @block.tensor
        def _(pe):
            pe.wait_ge(s["loaded"], 64)
            for i in range(2):
                pe.matmul(bank[i][0:A_HEADS + C_HEADS, :], rel[:], hot[:, i * T:(i + 1) * T], start=True, stop=True
                          ).then_inc(s["vec_mm"], 1)
            ex = kit.k1[:, K_EX:K_EX + P]
            pe.wait_ge(s["read_a"], 16)
            for h in range(A_HEADS):
                pe.matmul(bank[2 + h % 2][:], ex, ha[:, h, 0:T], start=True, stop=True).then_inc(s["turned"], 1)
                for n in range(NT):
                    at = 415 - P * n
                    mm = pe.matmul(bank[4 + h % 2][:, n * 32:n * 32 + NCMP], ex,
                                   ha[:, h, at:at + CMP_STRIDE * (NCMP - 1) + 1:CMP_STRIDE], start=True, stop=True)
                mm.then_inc(s["turned"], 1)
                pe.wait_ge(s["kept"], 2 * h + 2)
            pe.wait_ge(s["read_c"], 16)
            for h in range(0, C_HEADS, 2):
                pe.matmul(bank[6 + h // 2 % 2][:], ex, hc[:, h:h + 2, :], start=True, stop=True).then_inc(s["turned"], 1)
                pe.wait_ge(s["kept"], 2 * A_HEADS + h // 2 + 1)

        @block.vector
        def _(v):
            v.memset(kit.ones[:], 1.0).then_inc(s["set"], 1)
            v.memset(kit.eps[:, 0:1], NORM_EPS).then_inc(s["set"], 1)
            v.memset(kit.eps[:, 1:2], LN_EPS).then_inc(s["set"], 1)
            v.wait_ge(s["loaded"], 64)
            for i in range(2):
                v.wait_ge(s["vec_mm"], i + 1)
                v.tensor_tensor(vec[:, i * T:(i + 1) * T], bank[i][0:A_HEADS + C_HEADS, :],
                                msk[:, i * T:(i + 1) * T], ALU.add).then_inc(s["vec_made"], 1)
            for h in range(A_HEADS):
                v.wait_ge(s["turned"], 2 * h + 1)
                v.tensor_copy(kit.biasA[:, h, :], bank[2 + h % 2][:]).then_inc(s["kept"], 1)
                v.wait_ge(s["turned"], 2 * h + 2)
                v.tensor_copy(kit.biasK[:, h, :, :],
                              bank[4 + h % 2][:, 0:P].rearrange("p (n c) -> p n c", c=32)[:, :, 0:NCMP]
                              ).then_inc(s["kept"], 1)
            for h in range(0, C_HEADS, 2):
                v.wait_ge(s["turned"], 2 * A_HEADS + h // 2 + 1)
                v.tensor_copy(kit.biasC[:, h:h + 2, :], bank[6 + h // 2 % 2][:]
                              .rearrange("p (a b) -> p a b", a=2)).then_inc(s["kept"], 1)



def phase_project1(kit, l):
    nc, d, bank = kit.nc, kit.d, kit.bank
    with ExitStack() as ctx:
        st = Stream(nc, ctx, "in1", DC)
        hn = ctx.enter_context(nc.sbuf_tensor("hn", [P, DC, T], F32))
        sq = ctx.enter_context(nc.sbuf_tensor("sq1", [P, 2, T], F32))
        rs = ctx.enter_context(nc.sbuf_tensor("rs1", [P, 2, T], F32))
        s = kit.sems("in1", DENSE + ("small", "sq_made", "sq_summed", "ln_made", "rstd_made", "hn_made", "xhi_made",
                                     "xlo_made"), ring=("w_loaded",))
        block = ctx.enter_context(nc.Block())

        @block.sync
        def _(sp):
            load_weights(sp, st, s, d["w_in"], l * N_IN, N_IN)

        @block.scalar
        def _(a):
            a.dma_start(kit.s1[:], d["s1"][bass.ds(l, 1)].rearrange("o p k -> (o p) k")).then_inc(s["small"], 16)
            a.dma_start(kit.w1[:], d["w1"][bass.ds(l, 1)].rearrange("o p k -> (o p) k")).then_inc(s["small"], 16)
            for c in range(DC):
                if c >= 2:
                    a.wait_ge(s["sq_summed"], c - 1)
                a.activation(sq[:, c % 2, :], kit.x[:, c, :], ACT.Square).then_inc(s["sq_made"], 1)
            a.wait_ge(s["sq_summed"], DC)
            a.activation(rs[:, 0, :], bank[2][:], ACT.Ln, bias=kit.eps[:, 0:1], scale=1.0 / D).then_inc(s["ln_made"], 1)
            a.wait_ge(s["ln_made"], 1)
            a.activation(rs[:, 1, :], rs[:, 0, :], ACT.Exp, scale=-0.5).then_inc(s["rstd_made"], 1)
            for c in range(DC):
                a.wait_ge(s["hn_made"], c + 1)
                a.activation(kit.xh[:, c, :], hn[:, c, :], ACT.Copy).then_inc(s["xhi_made"], 1)
            a.sem_inc(s["out_taken"], 2)
            with a.Fori(0, N_IN // UNROLL) as j:
                for u in range(UNROLL):
                    a.wait_ge(s["mm_done"], j * UNROLL + u + 1 + HL_RING)
                    a.activation(kit.proj[:, bass.ds(j * UNROLL + u, 1), :].rearrange("p o t -> p (o t)"), bank[u % 2][:],
                                 ACT.Copy).then_inc(s["out_taken"], 1)
            a.wait_ge(s["small"], 32)

        @block.vector
        def _(v):
            v.sem_inc(s["w_split"], RAW_RING)
            v.wait_ge(s["small"], 32)
            v.wait_ge(s["rstd_made"], 1)
            for c in range(DC):
                v.scalar_tensor_tensor(hn[:, c, :], kit.x[:, c, :], kit.s1[:, S_GPRE + c:S_GPRE + c + 1], rs[:, 1, :],
                                       ALU.mult, ALU.mult).then_inc(s["hn_made"], 1)
                if c >= 1:
                    v.wait_ge(s["xhi_made"], c)
                    v.tensor_tensor(kit.xl[:, c - 1, :], hn[:, c - 1, :], kit.xh[:, c - 1, :].bitcast(F32), ALU.subtract
                                    ).then_inc(s["xlo_made"], 1)
            v.wait_ge(s["xhi_made"], DC)
            v.tensor_tensor(kit.xl[:, DC - 1, :], hn[:, DC - 1, :], kit.xh[:, DC - 1, :].bitcast(F32), ALU.subtract
                            ).then_inc(s["xlo_made"], 1)
            split_weights(v, st, s, N_IN)

        @block.tensor
        def _(pe):
            for c in range(DC):
                pe.wait_ge(s["sq_made"], c + 1)
                pe.matmul(bank[2][:], kit.ones[:], sq[:, c % 2, :], start=c == 0, stop=c == DC - 1
                          ).then_inc(s["sq_summed"], 1)
            pe.sem_inc(s["mm_done"], HL_RING)
            pe.wait_ge(s["xlo_made"], DC)
            dense_products(pe, st, s, N_IN, kit.xh, kit.xl, bank[0:2])

        @block.gpsimd
        def _(g):
            kit.clear(g, "out1")



def phase_prepare(kit):
    nc, bank, proj, s1, k1 = kit.nc, kit.bank, kit.proj, kit.s1, kit.k1
    with ExitStack() as ctx:
        def sb(name, shape):
            return ctx.enter_context(nc.sbuf_tensor(name, shape, F32))
        sq = sb("sq2", [P, 3, T])
        rq = sb("rq", [P, 2, T])
        cn = sb("cn", [P, 3, T])
        tpe = sb("tpe", [P, 2, T])
        hid = sb("hid", [P, 2, 32])
        rot = sb("rot", [P, 2, T])
        ge = sb("ge", [P, NT, 12])
        ident = k1[:, K_ID:K_ID + P]
        cos, sin = k1[64:96, K_TRIG:K_TRIG + T], k1[96:128, K_TRIG:K_TRIG + T]
        s = kit.sems("prep", ("sq_made", "sq_summed", "ln_made", "rstd_made", "cn_made", "tpe_made", "cmp_mm", "hid_made",
                              "cmp2_mm", "turned", "v_kept", "gates", "uq_mm", "uq_kept", "uk_mm", "uk_kept",
                              "uv_mm", "uv_kept", "rot_made", "qk_made", "act_chain", "misc"))
        block = ctx.enter_context(nc.Block())

        @block.scalar
        def _(a):
            for i, c in enumerate((C_CQ, C_CQ + 1, C_CKV)):
                a.activation(sq[:, i, :], proj[:, c, :], ACT.Square).then_inc(s["sq_made"], 1)
            for i, width in enumerate((2 * P, P)):
                a.wait_ge(s["sq_summed"], i + 1)
                a.activation(rq[:, i, :], bank[i][:], ACT.Ln, bias=kit.eps[:, 0:1], scale=1.0 / width).then_inc(s["ln_made"], 1)
            for i in range(2):
                a.wait_ge(s["ln_made"], i + 1)
                a.activation(rq[:, i, :], rq[:, i, :], ACT.Exp, scale=-0.5).then_inc(s["rstd_made"], 1)
            a.wait_ge(s["turned"], 3)
            a.activation(ge[:], bank[4][:, 0:NT * 12].rearrange("p (n c) -> p n c", c=12), ACT.Exp, scale=-1.0
                         ).then_inc(s["gates"], 1)
            a.activation(kit.vr[:], bank[2][:].rearrange("p (n c) -> p n c", c=P), ACT.Copy).then_inc(s["v_kept"], 1)
            a.activation(kit.cv[:], bank[3][:].rearrange("p (n c) -> p n c", c=P)[:, :, 0:HD], ACT.Copy
                         ).then_inc(s["v_kept"], 1)
            a.activation(proj[:, C_QA:C_QA + 2, :], proj[:, C_QA:C_QA + 2, :], ACT.Copy, scale=HD ** -0.5
                         ).then_inc(s["misc"], 1)
            a.activation(proj[:, C_QC:C_QC + 4, :], proj[:, C_QC:C_QC + 4, :], ACT.Copy, scale=HD ** -0.5
                         ).then_inc(s["misc"], 1)
            a.wait_ge(s["cmp_mm"], 2)
            for i in range(2):
                a.activation(hid[:, i, 0:NCMP], bank[5 + i][:, 0:NCMP], ACT.Silu).then_inc(s["hid_made"], 1)
            a.activation(proj[:, C_Z:C_Z + DC, :], proj[:, C_Z:C_Z + DC, :], ACT.Silu).then_inc(s["misc"], 1)
            for h in range(B_HEADS):
                a.wait_ge(s["uk_mm"], h + 1)
                a.activation(kit.kf[0:HD, h, :], bank[h % 2][0:HD, :], ACT.Copy).then_inc(s["uk_kept"], 1)
            a.wait_ge(s["uv_mm"], 4)
            for n in range(NT):
                a.activation(kit.mv[:, n, :], bank[2 + n // 2][:, (n % 2) * 256:(n % 2) * 256 + 256], ACT.Copy
                             ).then_inc(s["uv_kept"], 1)

        @block.tensor
        def _(pe):
            for n in range(NT):
                pe.transpose(bank[2][:, n * P:(n + 1) * P], proj[:, C_V, n * P:(n + 1) * P], ident)
            pe.transpose(bank[3][:, 0:P], proj[:, C_KR, 0:P], ident).then_inc(s["turned"], 1)
            for n in range(1, NT):
                mm = pe.transpose(bank[3][:, n * P:(n + 1) * P], proj[:, C_KR, n * P:(n + 1) * P], ident)
            mm.then_inc(s["turned"], 1)
            for n in range(NT):
                mm = pe.transpose(bank[4][:, n * 12:(n + 1) * 12], proj[0:12, C_GATE, n * P:(n + 1) * P], ident[0:12, 0:12])
            mm.then_inc(s["turned"], 1)
            pe.wait_ge(s["sq_made"], 2)
            pe.matmul(bank[0][:], kit.ones[:], sq[:, 0, :], start=True, stop=False)
            pe.matmul(bank[0][:], kit.ones[:], sq[:, 1, :], start=False, stop=True).then_inc(s["sq_summed"], 1)
            pe.wait_ge(s["sq_made"], 3)
            pe.matmul(bank[1][:], kit.ones[:], sq[:, 2, :], start=True, stop=True).then_inc(s["sq_summed"], 1)
            pe.wait_ge(s["tpe_made"], 2)
            for i in range(CMP_LEN):
                half, at = divmod(i, CMP_STRIDE)
                first = half * CMP_STRIDE + at
                for b in range(2):
                    rows = slice(HD * b, HD * b + HD)
                    mm = pe.matmul(bank[5 + b][:, 0:NCMP], kit.w1[rows, i * P:(i + 1) * P],
                                   tpe[rows, half, first:first + CMP_STRIDE * (NCMP - 1) + 1:CMP_STRIDE],
                                   start=i == 0, stop=i == CMP_LEN - 1)
                    if i == CMP_LEN - 1:
                        mm.then_inc(s["cmp_mm"], 1)
            for h in range(B_HEADS):
                if h == 0:
                    pe.wait_ge(s["cn_made"], 3)
                if h >= 2:
                    pe.wait_ge(s["uq_kept"], h - 1)
                for k in range(2):
                    mm = pe.matmul(bank[(0, 7)[h % 2]][:], s1[:, S_UQ + (k * B_HEADS + h) * P:S_UQ + (k * B_HEADS + h + 1) * P],
                                   cn[:, k, :], start=k == 0, stop=k == 1)
                mm.then_inc(s["uq_mm"], 1)
            pe.wait_ge(s["hid_made"], 2)
            pe.matmul(bank[4][:, 64:64 + NCMP], s1[:, S_W2K:S_W2K + P], hid[:, 0, 0:NCMP], start=True, stop=True)
            pe.matmul(bank[4][0:NCMP, 128:128 + HD], hid[:, 1, 0:NCMP], s1[:, S_W2V:S_W2V + HD], start=True, stop=True
                      ).then_inc(s["cmp2_mm"], 1)
            pe.wait_ge(s["v_kept"], 2)
            for n in range(NT):
                mm = pe.matmul(bank[2 + n // 2][:, (n % 2) * 256:(n % 2) * 256 + 256], cn[:, 2, n * P:(n + 1) * P],
                               s1[:, S_UV:S_UV + B_HEADS * HD], start=True, stop=True)
                mm.then_inc(s["uv_mm"], 1)
            pe.wait_ge(s["uq_kept"], B_HEADS)
            for h in range(B_HEADS):
                if h >= 2:
                    pe.wait_ge(s["uk_kept"], h - 1)
                pe.matmul(bank[h % 2][0:HD, :], s1[:, S_UK + h * HD:S_UK + (h + 1) * HD], cn[:, 2, :], start=True, stop=True
                          ).then_inc(s["uk_mm"], 1)

        @block.vector
        def _(v):
            pe_rows = s1[:, S_PE:S_PE + CMP_LEN]
            for half in range(2):
                v.tensor_tensor(tpe[:, half, :].rearrange("p (b i) -> p b i", i=CMP_STRIDE),
                                proj[:, C_CMP, :].rearrange("p (b i) -> p b i", i=CMP_STRIDE),
                                pe_rows[:, half * CMP_STRIDE:(half + 1) * CMP_STRIDE].unsqueeze(1)
                                .to_broadcast([P, T // CMP_STRIDE, CMP_STRIDE]), ALU.add).then_inc(s["tpe_made"], 1)
            for i, c in enumerate((C_CQ, C_CQ + 1, C_CKV)):
                v.wait_ge(s["rstd_made"], i // 2 + 1)
                v.scalar_tensor_tensor(cn[:, i, :], proj[:, c, :], s1[:, S_QN + i:S_QN + i + 1], rq[:, i // 2, :],
                                       ALU.mult, ALU.mult).then_inc(s["cn_made"], 1)
            v.wait_ge(s["gates"], 1)
            v.tensor_scalar(ge[:], ge[:], 1.0, None, ALU.add).then_inc(s["gates"], 1)
            v.wait_ge(s["gates"], 2)
            v.reciprocal(kit.gate[:], ge[:]).then_inc(s["gates"], 1)
            v.wait_ge(s["gates"], 3)
            v.tensor_scalar(kit.gate[:, 0, 0:12:3], kit.gate[:, 0, 0:12:3], k1[:, K_ROWOK:K_ROWOK + 1], None, ALU.mult
                            ).then_inc(s["gates"], 1)
            v.tensor_scalar(kit.nsink[:], s1[:, S_SINK:S_SINK + C_HEADS], -1.0, None, ALU.mult).then_inc(s["gates"], 1)
            scale = (HD + ROPE) ** -0.5
            for h in range(B_HEADS):
                qb = bank[(0, 7)[h % 2]]
                v.wait_ge(s["uq_mm"], h + 1)
                if h >= 1:
                    v.wait_ge(s["qk_made"], h)
                v.scalar_tensor_tensor(rot[64:96, 0, :], qb[64:96, :], scale, cos, ALU.mult, ALU.mult
                                       ).then_inc(s["rot_made"], 1)
                v.scalar_tensor_tensor(rot[64:96, 1, :], qb[96:128, :], scale, sin, ALU.mult, ALU.mult
                                       ).then_inc(s["rot_made"], 1)
                v.tensor_scalar(kit.qf[0:HD, h, :], qb[0:HD, :], scale, None, ALU.mult).then_inc(s["uq_kept"], 1)
                v.wait_ge(s["rot_made"], 2 * h + 2)
                v.tensor_tensor(kit.qf[64:96, h, :], rot[64:96, 0, :], rot[64:96, 1, :], ALU.add).then_inc(s["qk_made"], 1)
            v.wait_ge(s["qk_made"], B_HEADS)
            v.tensor_tensor(rot[64:96, 0, :], proj[64:96, C_KR, :], cos, ALU.mult).then_inc(s["rot_made"], 1)
            v.tensor_tensor(rot[64:96, 1, :], proj[96:128, C_KR, :], sin, ALU.mult).then_inc(s["rot_made"], 1)
            v.wait_ge(s["rot_made"], 2 * B_HEADS + 2)
            for h in range(B_HEADS):
                v.tensor_tensor(kit.kf[64:96, h, :], rot[64:96, 0, :], rot[64:96, 1, :], ALU.add).then_inc(s["qk_made"], 1)
            v.wait_ge(s["cmp2_mm"], 1)
            v.tensor_copy(kit.kc[:], bank[4][:, 64:64 + NCMP]).then_inc(s["qk_made"], 1)
            v.tensor_copy(kit.vc[:], bank[4][0:NCMP, 128:128 + HD]).then_inc(s["qk_made"], 1)

        @block.gpsimd
        def _(g):
            kit.clear(g, "in1")



def attention_units():
    units = []
    for pair in range(2):
        for n in range(NT):
            for h in (2 * pair, 2 * pair + 1):
                for b, kind in enumerate(("cmp", "slc", "win")):
                    units.append(dict(kind=kind, n=n, h=h, tile=pair, branch=b, first=b == 0, last=b == 2))
    for pair in range(2):
        for n in range(NT):
            for h in (2 * pair, 2 * pair + 1):
                units.append(dict(kind="mla", n=n, h=h, tile=2 + pair, first=True, last=True))
    for pair in range(4):
        for n in range(NT):
            for h in (2 * pair, 2 * pair + 1):
                units.append(dict(kind="swa", n=n, h=h, tile=4 + pair, first=True, last=True))
    for u in units:
        n = u["n"]
        if u["kind"] == "cmp":
            u["width"], u["keys"] = NCMP, [(0, NCMP)]
        else:
            lo = max(n - 1, 0) if u["kind"] == "swa" else 0
            u["width"], u["keys"] = (n + 1 - lo) * P, [(j, P) for j in range(lo, n + 1)]
            u["lo"] = lo
    return units


L_RING = 3
PT_RING = 2


def phase_attention(kit):
    nc, bank, proj = kit.nc, kit.bank, kit.proj
    units = attention_units()
    NU = len(units)
    tile_end = {u["tile"]: i for i, u in enumerate(units)}
    with ExitStack() as ctx:
        def sb(name, shape):
            return ctx.enter_context(nc.sbuf_tensor(name, shape, F32))
        lg = sb("lg", [P, L_RING, T])
        pt = sb("pt", [P, PT_RING, T])
        negm = sb("negm", [P, NU])
        tot = sb("tot", [P, NU])
        es = sb("es", [P, NU])
        inv = sb("inv", [P, NU])
        s = kit.sems("att", ("s_mm", "logits", "exps", "sinks", "inv_made", "dens", "scaled", "turned", "pt_made", "pv_mm", "mixed"))
        SB, TB, OB = bank[0:2], bank[2:4], bank[4:6]
        block = ctx.enter_context(nc.Block())

        def queries(u):
            r = slice(HD * (u["h"] % 2), HD * (u["h"] % 2) + HD)
            t = slice(u["n"] * P, (u["n"] + 1) * P)
            if u["kind"] == "mla":
                return kit.qf[:, u["h"], t]
            return proj[r, (C_QC if u["kind"] == "swa" else C_QA) + u["h"] // 2, t]

        def keys(u):
            r = slice(HD * (u["h"] % 2), HD * (u["h"] % 2) + HD)
            if u["kind"] == "cmp":
                return kit.kc[r, :]
            t = slice(u["lo"] * P, u["lo"] * P + u["width"])
            if u["kind"] == "mla":
                return kit.kf[:, u["h"], t]
            return proj[r, {"slc": C_KSLC, "win": C_KWIN, "swa": C_KC}[u["kind"]], t]

        def values(u, j):
            if u["kind"] == "cmp":
                return kit.vc[:, :]
            if u["kind"] == "mla":
                return kit.mv[:, j, u["h"] * HD:(u["h"] + 1) * HD]
            if u["kind"] == "swa":
                return kit.cv[:, j, :]
            return kit.vr[:, j, 0:HD] if u["kind"] == "slc" else kit.vr[:, j, HD:P]

        def bias(u):
            if u["kind"] == "cmp":
                return kit.biasK[:, u["h"], u["n"], :]
            if u["kind"] == "mla":
                return kit.k1[:, K_CAUSAL + T - u["width"]:K_CAUSAL + T]
            if u["kind"] == "swa":
                return kit.biasC[:, u["h"], 256 - u["width"]:256]
            return kit.biasA[:, u["h"], T - u["width"]:T]

        n_swa = {i: sum(x["kind"] == "swa" for x in units[:i + 1]) for i in range(NU)}

        @block.tensor
        def _(pe):
            def turn(i):
                u = units[i]
                pe.wait_ge(s["scaled"], i + 1)
                if i >= PT_RING:
                    pe.wait_ge(s["pt_made"], i - PT_RING + 1)
                w = P if u["kind"] != "cmp" else NCMP
                for x in range(len(u["keys"])):
                    mm = pe.transpose(TB[i % 2][0:w, x * P:(x + 1) * P], lg[:, i % L_RING, x * P:x * P + w],
                                      kit.k1[:, K_ID:K_ID + P])
                mm.then_inc(s["turned"], 1)

            def weigh(i):
                u = units[i]
                pe.wait_ge(s["pt_made"], i + 1)
                if u["tile"] >= 2:
                    pe.wait_ge(s["mixed"], u["tile"] - 1)
                r = HD * (u["h"] % 2)
                out = OB[u["tile"] % 2][r:r + HD, u["n"] * P:(u["n"] + 1) * P]
                for x, (j, w) in enumerate(u["keys"]):
                    mm = pe.matmul(out, values(u, j), pt[0:w, i % PT_RING, x * P:(x + 1) * P],
                                   start=u["first"] and x == 0, stop=u["last"] and x == len(u["keys"]) - 1)
                mm.then_inc(s["pv_mm"], 1)

            for i in range(NU + 3):
                if i < NU:
                    if i >= 2:
                        pe.wait_ge(s["logits"], i - 1)
                    pe.matmul(SB[i % 2][:, 0:units[i]["width"]], queries(units[i]), keys(units[i]), start=True, stop=True
                              ).then_inc(s["s_mm"], 1)
                if 2 <= i < NU + 2:
                    turn(i - 2)
                if i >= 3:
                    weigh(i - 3)

        @block.vector
        def _(v):
            def scale(i):
                u = units[i]
                v.wait_ge(s["exps"], i + 1)
                if u["kind"] == "swa":
                    v.wait_ge(s["sinks"], n_swa[i])
                    v.tensor_tensor(tot[:, i:i + 1], tot[:, i:i + 1], es[:, i:i + 1], ALU.add).then_inc(s["dens"], 1)
                    v.wait_ge(s["dens"], n_swa[i])
                v.reciprocal(inv[:, i:i + 1], tot[:, i:i + 1]).then_inc(s["inv_made"], 1)
                v.wait_ge(s["inv_made"], i + 1)
                row = lg[:, i % L_RING, 0:u["width"]]
                if "branch" in u:
                    at = u["h"] * 3 + u["branch"]
                    v.tensor_scalar(row, row, inv[:, i:i + 1], kit.gate[:, u["n"], at:at + 1], ALU.mult, ALU.mult
                                    ).then_inc(s["scaled"], 1)
                else:
                    v.tensor_scalar(row, row, inv[:, i:i + 1], None, ALU.mult).then_inc(s["scaled"], 1)

            def mix(tile):
                v.wait_ge(s["pv_mm"], tile_end[tile] + 1)
                z = proj[:, C_Z + tile, :]
                v.tensor_tensor(z, OB[tile % 2][:], z, ALU.mult).then_inc(s["mixed"], 1)

            done = 0
            for i in range(NU + 1):
                if i < NU:
                    u = units[i]
                    v.wait_ge(s["s_mm"], i + 1)
                    if i >= L_RING:
                        v.wait_ge(s["turned"], i - L_RING + 1)
                    start = kit.nsink[:, u["h"]:u["h"] + 1] if u["kind"] == "swa" else 3e38
                    v.tensor_tensor_reduce(lg[:, i % L_RING, 0:u["width"]], SB[i % 2][:, 0:u["width"]], bias(u), -1.0,
                                           start, ALU.add, ALU.min, negm[:, i:i + 1]).then_inc(s["logits"], 1)
                if i >= 1:
                    scale(i - 1)
                while done < 8 and tile_end[done] + 4 <= i:
                    mix(done)
                    done += 1
            while done < 8:
                mix(done)
                done += 1

        @block.scalar
        def _(a):
            def keep(i):
                u = units[i]
                a.wait_ge(s["turned"], i + 1)
                if i >= PT_RING:
                    a.wait_ge(s["pv_mm"], i - PT_RING + 1)
                w = P if u["kind"] != "cmp" else NCMP
                m = len(u["keys"]) * P
                a.activation(pt[0:w, i % PT_RING, 0:m], TB[i % 2][0:w, 0:m], ACT.Copy).then_inc(s["pt_made"], 1)

            for i in range(NU + 2):
                if i < NU:
                    u = units[i]
                    a.wait_ge(s["logits"], i + 1)
                    row = lg[:, i % L_RING, 0:u["width"]]
                    a.activation(row, row, ACT.Exp, bias=negm[:, i:i + 1], scale=-1.0, accum_out=tot[:, i:i + 1]
                                 ).then_inc(s["exps"], 1)
                    if u["kind"] == "swa":
                        a.activation(es[:, i:i + 1], kit.s1[:, S_SINK + u["h"]:S_SINK + u["h"] + 1], ACT.Exp,
                                     bias=negm[:, i:i + 1]).then_inc(s["sinks"], 1)
                if i >= 2:
                    keep(i - 2)

        @block.gpsimd
        def _(g):
            kit.clear(g, "prep")



def phase_out1(kit, l):
    nc, d, bank = kit.nc, kit.d, kit.bank
    with ExitStack() as ctx:
        st = Stream(nc, ctx, "out1", DC)
        y = ctx.enter_context(nc.sbuf_tensor("y1", [P, DC, T], F32))
        sq = ctx.enter_context(nc.sbuf_tensor("sq3", [P, 2, T], F32))
        rs = ctx.enter_context(nc.sbuf_tensor("rs3", [P, 2, T], F32))
        s = kit.sems("out1", OUT1_SEMS, ring=("w_loaded",))
        block = ctx.enter_context(nc.Block())
        mixed = kit.proj[:, C_Z:C_Z + DC, :]

        @block.sync
        def _(sp):
            load_weights(sp, st, s, d["w_out"], l * DC, DC)

        @block.scalar
        def _(a):
            for c in range(DC):
                a.activation(kit.xh[:, c, :], mixed[:, c, :], ACT.Copy).then_inc(s["mhi_made"], 1)
            a.sem_inc(s["out_taken"], 2)
            with a.Fori(0, DC // UNROLL) as j:
                for u in range(UNROLL):
                    a.wait_ge(s["mm_done"], j * UNROLL + u + 1 + HL_RING)
                    a.activation(y[:, bass.ds(j * UNROLL + u, 1), :].rearrange("p o t -> p (o t)"), bank[u % 2][:],
                                 ACT.Copy).then_inc(s["out_taken"], 1)
            a.wait_ge(s["out_taken"], 2 + DC)
            for c in range(DC):
                if c >= 2:
                    a.wait_ge(s["sq_summed"], c - 1)
                a.activation(sq[:, c % 2, :], y[:, c, :], ACT.Square).then_inc(s["sq_made"], 1)
            a.wait_ge(s["sq_summed"], DC)
            a.activation(rs[:, 0, :], bank[2][:], ACT.Ln, bias=kit.eps[:, 0:1], scale=1.0 / D).then_inc(s["ln_made"], 1)
            a.wait_ge(s["ln_made"], 1)
            a.activation(rs[:, 1, :], rs[:, 0, :], ACT.Exp, scale=-0.5).then_inc(s["rstd_made"], 1)

        @block.vector
        def _(v):
            v.sem_inc(s["w_split"], RAW_RING)
            for c in range(DC):
                v.wait_ge(s["mhi_made"], c + 1)
                v.tensor_tensor(kit.xl[:, c, :], mixed[:, c, :], kit.xh[:, c, :].bitcast(F32), ALU.subtract
                                ).then_inc(s["mlo_made"], 1)
            split_weights(v, st, s, DC)
            v.wait_ge(s["rstd_made"], 1)
            for c in range(DC):
                v.scalar_tensor_tensor(y[:, c, :], y[:, c, :], kit.s1[:, S_GPOST + c:S_GPOST + c + 1], rs[:, 1, :],
                                       ALU.mult, ALU.mult).then_inc(s["scaled"], 1)
            for c in range(DC):
                v.wait_ge(s["scaled"], c + 1)
                v.tensor_tensor(kit.x[:, c, :], kit.x[:, c, :], y[:, c, :], ALU.add).then_inc(s["x_made"], 1)

        @block.tensor
        def _(pe):
            pe.sem_inc(s["mm_done"], HL_RING)
            pe.wait_ge(s["mlo_made"], DC)
            dense_products(pe, st, s, DC, kit.xh, kit.xl, bank[0:2])
            for c in range(DC):
                pe.wait_ge(s["sq_made"], c + 1)
                pe.matmul(bank[2][:], kit.ones[:], sq[:, c % 2, :], start=c == 0, stop=c == DC - 1
                          ).then_inc(s["sq_summed"], 1)

        @block.gpsimd
        def _(g):
            kit.clear(g, "att")


def phase_leave(kit, tags):
    with kit.nc.Block() as block:
        @block.gpsimd
        def _(g):
            for tag in tags:
                kit.clear(g, tag)



def phase_split_x(kit):
    nc, d = kit.nc, kit.d
    s = kit.sems("split", ("hi_made", "lo_made", "loaded"))
    with nc.Block() as block:
        @block.sync
        def _(sp):
            sp.dma_start(kit.k2[:], d["k2"]).then_inc(s["loaded"], 16)
            sp.wait_ge(s["loaded"], 16)

        @block.scalar
        def _(a):
            for c in range(DC):
                a.activation(kit.xh[:, c, :], kit.x[:, c, :], ACT.Copy).then_inc(s["hi_made"], 1)

        @block.vector
        def _(v):
            for c in range(DC):
                v.wait_ge(s["hi_made"], c + 1)
                v.tensor_tensor(kit.xl[:, c, :], kit.x[:, c, :], kit.xh[:, c, :].bitcast(F32), ALU.subtract
                                ).then_inc(s["lo_made"], 1)



def phase_ffn_up(kit, l, tag, hh, hl):
    nc, d, bank = kit.nc, kit.d, kit.bank
    n = 2 * FC
    with ExitStack() as ctx:
        st = Stream(nc, ctx, tag, DC)
        sg = ctx.enter_context(nc.sbuf_tensor(f"{tag}_sg", [P, 2, T], F32))
        ub = ctx.enter_context(nc.sbuf_tensor(f"{tag}_ub", [P, 2, T], F32))
        hm = ctx.enter_context(nc.sbuf_tensor(f"{tag}_hm", [P, 2, T], F32))
        s = kit.sems("up", DENSE + ("small", "h_made", "hhi_made", "hlo_made"), ring=("w_loaded",))
        block = ctx.enter_context(nc.Block())

        @block.sync
        def _(sp):
            load_weights(sp, st, s, d[tag], l * n, n)

        @block.scalar
        def _(a):
            a.dma_start(kit.s2[:], d["s2"][bass.ds(l, 1)].rearrange("o p k -> (o p) k")).then_inc(s["small"], 16)
            a.sem_inc(s["out_taken"], 2)
            with a.Fori(0, n // UNROLL) as j:
                for f in range(2):
                    a.wait_ge(s["mm_done"], j * UNROLL + 2 * f + 1 + HL_RING)
                    a.activation(sg[:, f, :], bank[0][:], ACT.Silu).then_inc(s["out_taken"], 1)
                    a.wait_ge(s["mm_done"], j * UNROLL + 2 * f + 2 + HL_RING)
                    a.activation(ub[:, f, :], bank[1][:], ACT.Copy).then_inc(s["out_taken"], 1)
                    a.wait_ge(s["h_made"], j * 2 + f + 1)
                    a.activation(hh[:, bass.ds(j * 2 + f, 1), :].rearrange("p o t -> p (o t)"), hm[:, f, :], ACT.Copy
                                 ).then_inc(s["hhi_made"], 1)
            a.wait_ge(s["small"], 16)

        @block.gpsimd
        def _(g):
            kit.clear(g, "ln")
            with g.Fori(0, n // UNROLL) as j:
                for f in range(2):
                    g.wait_ge(s["out_taken"], j * UNROLL + 2 * f + 4)
                    g.tensor_tensor(hm[:, f, :], sg[:, f, :], ub[:, f, :], ALU.mult).then_inc(s["h_made"], 1)
                    g.wait_ge(s["hhi_made"], j * 2 + f + 1)
                    at = bass.ds(j * 2 + f, 1)
                    g.tensor_tensor(hl[:, at, :].rearrange("p o t -> p (o t)"), hm[:, f, :],
                                    hh[:, at, :].rearrange("p o t -> p (o t)").bitcast(F32), ALU.subtract
                                    ).then_inc(s["hlo_made"], 1)

        @block.vector
        def _(v):
            v.sem_inc(s["w_split"], RAW_RING)
            split_weights(v, st, s, n)

        @block.tensor
        def _(pe):
            pe.sem_inc(s["mm_done"], HL_RING)
            dense_products(pe, st, s, n, kit.xh, kit.xl, bank[0:2])



def phase_dense_ln(kit, l, tag, cleared, xh, xl, kp, pieces, scale, which):
    nc, d, bank, x = kit.nc, kit.d, kit.bank, kit.x
    n = DC * pieces
    per = UNROLL // pieces
    with ExitStack() as ctx:
        st = Stream(nc, ctx, tag, kp)
        yt = ctx.enter_context(nc.sbuf_tensor(f"{tag}_yt", [P, 2, T], F32))
        rs = ctx.enter_context(nc.sbuf_tensor(f"{tag}_rs", [P, 2, T], F32))
        s = kit.sems("ln", LN_SEMS, ring=("w_loaded",))
        block = ctx.enter_context(nc.Block())

        @block.sync
        def _(sp):
            load_weights(sp, st, s, d[tag], l * n, n)

        @block.gpsimd
        def _(g):
            kit.clear(g, cleared)
            for c in range(DC):
                g.tensor_scalar(x[:, c, :], x[:, c, :], ALPHA, None, ALU.mult).then_inc(s["alpha"], 1)
            g.sem_inc(s["r_made"], 2)
            g.wait_ge(s["alpha"], DC)
            with g.Fori(0, DC // per) as j:
                for u in range(per):
                    g.wait_ge(s["out_taken"], j * per + u + 3)
                    xc = x[:, bass.ds(j * per + u, 1), :].rearrange("p o t -> p (o t)")
                    g.tensor_tensor(xc, xc, yt[:, u % 2, :], ALU.add).then_inc(s["r_made"], 1)

        @block.scalar
        def _(a):
            a.sem_inc(s["out_taken"], 2)
            with a.Fori(0, DC // per) as j:
                for u in range(per):
                    a.wait_ge(s["mm_done"], j * UNROLL + (u + 1) * pieces + HL_RING)
                    a.wait_ge(s["r_made"], j * per + u + 1)
                    a.activation(yt[:, u % 2, :], bank[u % 2][:], ACT.Copy, scale=scale).then_inc(s["out_taken"], 1)
            a.wait_ge(s["summed"], 1)
            a.activation(rs[:, 0, :], bank[2][:], ACT.Copy, scale=1.0 / D).then_inc(s["mean_made"], 1)
            for c in range(DC):
                a.wait_ge(s["cent_made"], c + 1)
                if c >= 2:
                    a.wait_ge(s["sq_summed"], c - 1)
                a.activation(yt[:, c % 2, :], x[:, c, :], ACT.Square).then_inc(s["sq_made"], 1)
            a.wait_ge(s["sq_summed"], DC)
            a.activation(rs[:, 0, :], bank[3][:], ACT.Ln, bias=kit.eps[:, 1:2], scale=1.0 / D).then_inc(s["ln_made"], 1)
            a.wait_ge(s["ln_made"], 1)
            a.activation(rs[:, 1, :], rs[:, 0, :], ACT.Exp, scale=-0.5).then_inc(s["rstd_made"], 1)
            for c in range(DC):
                b = kit.s2[:, Q_LNB + which * DC + c:Q_LNB + which * DC + c + 1]
                a.wait_ge(s["norm_made"], c + 1)
                a.activation(kit.xh[:, c, :], x[:, c, :], ACT.Identity, bias=b).then_inc(s["xhi_made"], 1)
                a.activation(x[:, c, :], x[:, c, :], ACT.Identity, bias=b).then_inc(s["x_made"], 1)

        @block.vector
        def _(v):
            v.sem_inc(s["w_split"], RAW_RING)
            split_weights(v, st, s, n)
            v.wait_ge(s["mean_made"], 1)
            for c in range(DC):
                v.tensor_tensor(x[:, c, :], x[:, c, :], rs[:, 0, :], ALU.subtract).then_inc(s["cent_made"], 1)
            v.wait_ge(s["rstd_made"], 1)
            for c in range(DC):
                v.scalar_tensor_tensor(x[:, c, :], x[:, c, :], kit.s2[:, Q_LNG + which * DC + c:Q_LNG + which * DC + c + 1],
                                       rs[:, 1, :], ALU.mult, ALU.mult).then_inc(s["norm_made"], 1)
            for c in range(DC):
                v.wait_ge(s["x_made"], c + 1)
                v.tensor_tensor(kit.xl[:, c, :], x[:, c, :], kit.xh[:, c, :].bitcast(F32), ALU.subtract
                                ).then_inc(s["xlo_made"], 1)

        @block.tensor
        def _(pe):
            pe.sem_inc(s["mm_done"], HL_RING)
            dense_products(pe, st, s, n, xh, xl, bank[0:2], pieces)
            for c in range(DC):
                pe.wait_ge(s["r_made"], c + 3)
                mm = pe.matmul(bank[2][:], kit.ones[:], x[:, c, :], start=c == 0, stop=c == DC - 1)
            mm.then_inc(s["summed"], 1)
            for c in range(DC):
                pe.wait_ge(s["sq_made"], c + 1)
                pe.matmul(bank[3][:], kit.ones[:], yt[:, c % 2, :], start=c == 0, stop=c == DC - 1
                          ).then_inc(s["sq_summed"], 1)



def phase_project2(kit, l, p2):
    nc, d, bank = kit.nc, kit.d, kit.bank
    with ExitStack() as ctx:
        st = Stream(nc, ctx, "in2", DC)
        s = kit.sems("in2", DENSE, ring=("w_loaded",))
        block = ctx.enter_context(nc.Block())

        @block.sync
        def _(sp):
            load_weights(sp, st, s, d["w_in_2"], l * N_IN2, N_IN2)

        @block.scalar
        def _(a):
            a.sem_inc(s["out_taken"], 2)
            with a.Fori(0, N_IN2 // UNROLL) as j:
                for u in range(UNROLL):
                    a.wait_ge(s["mm_done"], j * UNROLL + u + 1 + HL_RING)
                    a.activation(p2[:, bass.ds(j * UNROLL + u, 1), :].rearrange("p o t -> p (o t)"), bank[u % 2][:],
                                 ACT.Copy).then_inc(s["out_taken"], 1)

        @block.vector
        def _(v):
            v.sem_inc(s["w_split"], RAW_RING)
            split_weights(v, st, s, N_IN2)

        @block.tensor
        def _(pe):
            pe.sem_inc(s["mm_done"], HL_RING)
            dense_products(pe, st, s, N_IN2, kit.xh, kit.xl, bank[0:2])

        @block.gpsimd
        def _(g):
            kit.clear(g, "ln")



LEVELS = (64, 32, 16, 8, 4, 2, 1)


def phase_mixers(kit, p2):
    nc, bank = kit.nc, kit.bank
    W = HH * T
    with ExitStack() as ctx:
        def sb(name, shape):
            return ctx.enter_context(nc.sbuf_tensor(name, shape, F32))
        bb = sb("bb", [P, W])
        kk = sb("kk", [P, W])
        df = sb("df", [P, 2, W])
        xx = sb("xx", [P, 2, W])
        kr = sb("kr", [P, NT, HH, P])
        vrow = sb("vrow", [P, NT, HH, P])
        at = sb("at", [P, NT, HH, P])
        ad = sb("ad", [P, NT * HH, 32])
        tm = sb("tm", [P, NT * HH, 32])
        sta = sb("sta", [P, 3, HH, P])
        el = sb("el", [P, NT * HH])
        lbv = sb("lbv", [P, 6, HH])
        pl = sb("pl", [P, 2, HH, PADT + T])
        ident = kit.k2[:, 0:P]
        s = kit.sems("mix", ("chain_v", "abs_f", "exp_f", "ln_f", "ls_made", "km_made", "k_made", "a_made", "m_made", "lb_in",
                             "lb_act", "lb_made", "e2", "e3", "e4", "b_made", "sub_made", "exp_made", "x_made", "top_mm",
                             "lev_mm", "acc_made", "at_made", "v_turned", "v_kept", "qe_exp", "qe_made", "kd_made",
                             "k_turned", "k_kept", "kv_mm", "st_made", "o_mm", "o_kept", "osq_made", "o_summed",
                             "oln_made", "orstd_made", "y_made", "g_made", "u_pad", "pool_chain", "pooled", "p_mm",
                             "hi_made", "p_kept", "lo_made", "zeroed"))
        q = p2[:, D_Q:D_Q + HH, :].rearrange("p h t -> p (h t)")
        f = p2[:, D_F:D_F + HH, :].rearrange("p h t -> p (h t)")
        g_in = p2[:, D_G:D_G + HH, :].rearrange("p h t -> p (h t)")
        LNLB, LNOM, DIF = 3, 4, 5
        ot = xx[:, 0, :]
        osq = xx[:, 1, :]
        rst = df[:, 0, :]
        block = ctx.enter_context(nc.Block())

        def halves(ap, m):
            b = ap.rearrange("p (b m) -> p b m", m=2 * m)
            return b[:, :, 0:m], b[:, :, m:2 * m]

        def cols(h, n, a=0, b=P):
            return slice(h * T + n * P + a, h * T + n * P + b)

        @block.scalar
        def _(a):
            a.wait_ge(s["lb_in"], 1)
            a.activation(lbv[:, 1, :], lbv[:, 0, :], ACT.Abs).then_inc(s["lb_act"], 1)
            a.wait_ge(s["lb_act"], 1)
            a.activation(lbv[:, 1, :], lbv[:, 1, :], ACT.Exp, scale=-1.0).then_inc(s["lb_act"], 1)
            a.activation(df[:, 0, :], f, ACT.Abs).then_inc(s["abs_f"], 1)
            a.wait_ge(s["abs_f"], 1)
            a.activation(df[:, 0, :], df[:, 0, :], ACT.Exp, scale=-1.0).then_inc(s["exp_f"], 1)
            a.wait_ge(s["lb_act"], 2)
            a.activation(lbv[:, 1, :], lbv[:, 1, :], ACT.Ln, bias=kit.ones[:, 0:1]).then_inc(s["lb_act"], 1)
            a.wait_ge(s["exp_f"], 1)
            a.activation(df[:, 0, :], df[:, 0, :], ACT.Ln, bias=kit.ones[:, 0:1]).then_inc(s["ln_f"], 1)
            a.wait_ge(s["lb_made"], 1)
            for h in range(HH):
                a.wait_ge(s["ls_made"], 1)
                a.activation(df[:, 1, h * T:(h + 1) * T], xx[:, 0, h * T:(h + 1) * T], ACT.Abs,
                             bias=lbv[:, DIF, h:h + 1]).then_inc(s["e2"], 1)
            a.wait_ge(s["e2"], HH)
            a.activation(df[:, 1, :], df[:, 1, :], ACT.Exp, scale=-1.0).then_inc(s["e3"], 1)
            a.wait_ge(s["km_made"], 1)
            for h in range(HH):
                a.activation(kk[:, h * T:(h + 1) * T], xx[:, 1, h * T:(h + 1) * T], ACT.Exp,
                             bias=lbv[:, LNOM, h:h + 1]).then_inc(s["k_made"], 1)
            a.wait_ge(s["e3"], 1)
            a.activation(df[:, 1, :], df[:, 1, :], ACT.Ln, bias=kit.ones[:, 0:1]).then_inc(s["e4"], 1)
            for n in range(NT):
                a.wait_ge(s["v_turned"], n + 1)
                a.activation(vrow[:, n, :, :], bank[6 + n % 2][:].rearrange("p (h c) -> p h c", h=HH), ACT.Copy
                             ).then_inc(s["v_kept"], 1)
            for i, m in enumerate(LEVELS):
                a.wait_ge(s["sub_made"], i + 1)
                left, right = halves(df[:, i % 2, :], m)
                a.activation(right, right, ACT.Exp).then_inc(s["exp_made"], 1)
                a.activation(left, left, ACT.Exp, scale=-1.0).then_inc(s["exp_made"], 1)
            a.wait_ge(s["x_made"], 2 * len(LEVELS))
            a.activation(df[:, 1, :], bb[:], ACT.Exp).then_inc(s["qe_exp"], 1)
            a.activation(el[:], bb[:, P - 1:W:P], ACT.Exp).then_inc(s["qe_exp"], 1)
            a.wait_ge(s["sub_made"], len(LEVELS) + 1)
            a.activation(df[:, 0, :], df[:, 0, :], ACT.Exp).then_inc(s["qe_exp"], 1)
            a.wait_ge(s["zeroed"], 2)
            for n in range(NT):
                a.wait_ge(s["top_mm"], NT + n + 1)
                top = bank[n][:].rearrange("p (h t) -> p h t", h=HH)
                a.activation(at[0:64, n, :, 64:128], top[0:64, :, 64:128], ACT.Copy).then_inc(s["at_made"], 1)
                a.activation(at[0:32, n, :, 32:64], top[0:32, :, 32:64], ACT.Copy).then_inc(s["at_made"], 1)
                a.activation(at[64:96, n, :, 96:128], top[64:96, :, 96:128], ACT.Copy).then_inc(s["at_made"], 1)
            for n in range(NT - 1):
                a.wait_ge(s["k_turned"], n + 1)
                a.activation(kr[:, n, :, :], bank[6 + n % 2][:].rearrange("p (h c) -> p h c", h=HH), ACT.Copy
                             ).then_inc(s["k_kept"], 1)
            for n in range(NT):
                a.wait_ge(s["o_mm"], n + 1)
                a.activation(ot.rearrange("p (h t) -> p h t", h=HH)[:, :, n * P:(n + 1) * P],
                             bank[n][:].rearrange("p (h t) -> p h t", h=HH), ACT.Copy).then_inc(s["o_kept"], 1)
            a.wait_ge(s["o_kept"], NT)
            a.activation(osq, ot, ACT.Square).then_inc(s["osq_made"], 1)
            for h in range(HH):
                a.wait_ge(s["o_summed"], h + 1)
                a.activation(rst[:, h * T:(h + 1) * T], bank[h][:], ACT.Ln, bias=kit.eps[:, 0:1], scale=1.0 / P
                             ).then_inc(s["oln_made"], 1)
            for h in range(HH):
                a.wait_ge(s["oln_made"], h + 1)
                a.activation(rst[:, h * T:(h + 1) * T], rst[:, h * T:(h + 1) * T], ACT.Exp, scale=-0.5
                             ).then_inc(s["orstd_made"], 1)
            a.activation(g_in, g_in, ACT.Silu).then_inc(s["g_made"], 1)
            for c in range(HH):
                a.wait_ge(s["p_mm"], c + 1)
                sc = kit.s2[:, Q_PS + c:Q_PS + c + 1]
                a.activation(p2[:, D_U + c, :], bank[4 + c % 2][:], ACT.Copy, scale=sc).then_inc(s["p_kept"], 1)
                a.activation(kit.xh[:, c, :], bank[4 + c % 2][:], ACT.Copy, scale=sc).then_inc(s["hi_made"], 1)
            for c in range(HH):
                a.wait_ge(s["y_made"], 2 * (c + 1))
                a.activation(kit.xh[:, HH + c, :], ot[:, c * T:(c + 1) * T], ACT.Copy).then_inc(s["hi_made"], 1)

        @block.vector
        def _(v):
            lb = kit.s2[:, Q_LB:Q_LB + 2 * HH].rearrange("p (l h) -> p l h", l=2)
            v.tensor_tensor(lbv[:, 0, :], lb[:, 1, :], lb[:, 0, :], ALU.subtract).then_inc(s["lb_in"], 1)
            v.wait_ge(s["lb_act"], 3)
            link = linker(v, s["chain_v"])
            link(v.scalar_tensor_tensor(lbv[:, 2, :], lbv[:, 0, :], 0.0, lbv[:, 1, :], ALU.min, ALU.subtract))
            link(v.tensor_tensor(lbv[:, LNOM, :], lbv[:, 2, :], lbv[:, 0, :], ALU.subtract))
            link(v.tensor_scalar(lbv[:, LNLB, :], lbv[:, 2, :], kit.s2[:, Q_FIRST:Q_FIRST + 1], None, ALU.add))
            link(v.tensor_scalar(lbv[:, LNOM, :], lbv[:, LNOM, :], kit.s2[:, Q_NOTFIRST:Q_NOTFIRST + 1], None, ALU.mult))
            v.tensor_tensor(lbv[:, DIF, :], lbv[:, LNOM, :], lbv[:, LNLB, :], ALU.subtract).then_inc(s["lb_made"], 1)
            v.wait_ge(s["ln_f"], 1)
            v.scalar_tensor_tensor(xx[:, 0, :], f, 0.0, df[:, 0, :], ALU.min, ALU.subtract).then_inc(s["ls_made"], 1)
            v.wait_ge(s["ls_made"], 1)
            v.tensor_tensor(xx[:, 1, :], xx[:, 0, :], f, ALU.subtract).then_inc(s["km_made"], 1)
            v.wait_ge(s["lb_made"], 1)
            for h in range(HH):
                v.tensor_scalar(df[:, 0, h * T:(h + 1) * T], xx[:, 0, h * T:(h + 1) * T], lbv[:, LNOM, h:h + 1],
                                lbv[:, LNLB, h:h + 1], ALU.add, ALU.max).then_inc(s["m_made"], 1)
            v.wait_ge(s["m_made"], HH)
            v.wait_ge(s["e4"], 1)
            v.tensor_tensor(df[:, 0, :], df[:, 0, :], df[:, 1, :], ALU.add).then_inc(s["a_made"], 1)
            v.wait_ge(s["a_made"], 1)
            for h in range(HH):
                for n in range(NT):
                    v.tensor_tensor_scan(bb[:, cols(h, n)], kit.ones[:], df[:, 0, cols(h, n)], 0.0, ALU.mult, ALU.add
                                         ).then_inc(s["b_made"], 1)
            v.tensor_scalar(q, q, float(P) ** -0.5, None, ALU.mult).then_inc(s["b_made"], 1)
            v.wait_ge(s["b_made"], HH * NT + 1)
            v.wait_ge(s["k_made"], HH)

            def sub(i):
                m = LEVELS[i]
                b3 = bb[:].rearrange("p (b m) -> p b m", m=2 * m)
                v.tensor_tensor(df[:, i % 2, :].rearrange("p (b m) -> p b m", m=2 * m), b3,
                                b3[:, :, m - 1:m].to_broadcast([P, W // (2 * m), 2 * m]), ALU.subtract
                                ).then_inc(s["sub_made"], 1)

            def accumulate(i):
                v.wait_ge(s["lev_mm"], i + 1)
                mask = kit.k2[:, M_MASK + 32 * i:M_MASK + 32 * i + 32].unsqueeze(1).to_broadcast([P, NT * HH, 32])
                lev = bank[4 + i % 2][:].rearrange("p (a t) -> p a t", t=32)
                if i == 0:
                    v.tensor_tensor(ad[:], lev, mask, ALU.mult).then_inc(s["acc_made"], 1)
                else:
                    v.tensor_tensor(tm[:], lev, mask, ALU.mult).then_inc(s["acc_made"], 1)
                    v.wait_ge(s["acc_made"], 2 * i)
                    v.tensor_tensor(ad[:], ad[:], tm[:], ALU.add).then_inc(s["acc_made"], 1)
                    v.wait_ge(s["acc_made"], 2 * i + 1)

            sub(0)
            for i, m in enumerate(LEVELS):
                if i + 1 < len(LEVELS):
                    if i >= 1:
                        v.wait_ge(s["x_made"], 2 * i)
                    sub(i + 1)
                v.wait_ge(s["exp_made"], 2 * i + 2)
                if i == 2:
                    v.wait_ge(s["top_mm"], NT)
                if i == 3:
                    v.wait_ge(s["top_mm"], 2 * NT)
                if i >= 4:
                    v.wait_ge(s["lev_mm"], i - 3)
                el_, er_ = halves(df[:, i % 2, :], m)
                kl_, _ = halves(kk[:], m)
                _, qr_ = halves(q, m)
                xl_, xr_ = halves(xx[:, i % 2, :], m)
                v.tensor_tensor(xl_, el_, kl_, ALU.mult).then_inc(s["x_made"], 1)
                v.tensor_tensor(xr_, er_, qr_, ALU.mult).then_inc(s["x_made"], 1)
                if i >= 3:
                    accumulate(i - 3)
            b3 = bb[:].rearrange("p (b m) -> p b m", m=P)
            v.wait_ge(s["x_made"], 2 * len(LEVELS))
            v.tensor_tensor(df[:, 0, :].rearrange("p (b m) -> p b m", m=P),
                            b3[:, :, P - 1:P].to_broadcast([P, NT * HH, P]), b3, ALU.subtract).then_inc(s["sub_made"], 1)
            for i in range(len(LEVELS) - 3, len(MASKED)):
                accumulate(i)
            v.wait_ge(s["qe_exp"], 2)
            v.tensor_tensor(q, q, df[:, 1, :], ALU.mult).then_inc(s["qe_made"], 1)
            v.wait_ge(s["qe_exp"], 3)
            v.tensor_tensor(kk[:], kk[:], df[:, 0, :], ALU.mult).then_inc(s["kd_made"], 1)
            v.wait_ge(s["zeroed"], 2)
            for b in range(4):
                r = slice(32 * b, 32 * b + 32)
                v.tensor_copy(at[r].rearrange("p n h t -> p (n h) t")[:, :, r], ad[r]).then_inc(s["at_made"], 1)
            v.wait_ge(s["kv_mm"], 1)
            v.tensor_copy(sta[:, 0, :, :], bank[4][:].rearrange("p (h c) -> p h c", h=HH)).then_inc(s["st_made"], 1)
            count = 1
            for n in (1, 2):
                v.wait_ge(s["kv_mm"], n + 1)
                v.wait_ge(s["st_made"], count)
                for h in range(HH):
                    v.scalar_tensor_tensor(sta[:, n, h, :], sta[:, n - 1, h, :], el[:, h * NT + n:h * NT + n + 1],
                                           bank[4 + n % 2][:, h * P:(h + 1) * P], ALU.mult, ALU.add
                                           ).then_inc(s["st_made"], 1)
                    count += 1
            v.wait_ge(s["g_made"], 1)
            for h in range(HH):
                seg = slice(h * T, (h + 1) * T)
                v.wait_ge(s["orstd_made"], h + 1)
                v.scalar_tensor_tensor(ot[:, seg], ot[:, seg], kit.s2[:, Q_HG:Q_HG + 1], rst[:, seg], ALU.mult, ALU.mult
                                       ).then_inc(s["y_made"], 1)
                v.wait_ge(s["y_made"], 2 * h + 1)
                v.tensor_tensor(ot[:, seg], ot[:, seg], g_in[:, seg], ALU.mult).then_inc(s["y_made"], 1)
            for c in range(DC):
                v.wait_ge(s["hi_made"], c + 1)
                full = p2[:, D_U + c, :] if c < HH else ot[:, (c - HH) * T:(c - HH + 1) * T]
                v.wait_ge(s["p_kept"], min(c + 1, HH))
                v.tensor_tensor(kit.xl[:, c, :], full, kit.xh[:, c, :].bitcast(F32), ALU.subtract
                                ).then_inc(s["lo_made"], 1)

        @block.tensor
        def _(pe):
            for n in range(NT):
                if n >= 2:
                    pe.wait_ge(s["v_kept"], n - 1)
                for h in range(HH):
                    mm = pe.transpose(bank[6 + n % 2][:, h * P:(h + 1) * P], p2[:, D_V + h, n * P:(n + 1) * P], ident)
                mm.then_inc(s["v_turned"], 1)
            for i, m in enumerate((64, 32)):
                pe.wait_ge(s["x_made"], 2 * i + 2)
                for n in range(NT):
                    for h in range(HH):
                        for a0 in range(0, P, 2 * m):
                            mm = pe.matmul(bank[n][a0:a0 + m, h * P + a0 + m:h * P + a0 + 2 * m],
                                           xx[:, i % 2, cols(h, n, a0, a0 + m)], xx[:, i % 2, cols(h, n, a0 + m, a0 + 2 * m)],
                                           start=True, stop=True)
                    mm.then_inc(s["top_mm"], 1)
            for i in range(len(MASKED)):
                if i < len(MASKED) - 1:
                    pe.wait_ge(s["x_made"], 2 * (i + 3))
                if i >= 2:
                    pe.wait_ge(s["acc_made"], 2 * i - 3)
                for n in range(NT):
                    for h in range(HH):
                        for b in range(4):
                            c = cols(h, n, 32 * b, 32 * b + 32)
                            if i < len(MASKED) - 1:
                                lhs = rhs = xx[:, i % 2, c]
                            else:
                                lhs, rhs = kk[:, c], q[:, c]
                            at0 = (n * HH + h) * 32
                            mm = pe.matmul(bank[4 + i % 2][32 * b:32 * b + 32, at0:at0 + 32], lhs, rhs, start=True, stop=True)
                mm.then_inc(s["lev_mm"], 1)
            pe.wait_ge(s["kd_made"], 1)
            pe.wait_ge(s["v_kept"], NT)
            for n in range(NT - 1):
                if n >= 2:
                    pe.wait_ge(s["k_kept"], n - 1)
                for h in range(HH):
                    mm = pe.transpose(bank[6 + n % 2][:, h * P:(h + 1) * P], kk[:, cols(h, n)], ident)
                mm.then_inc(s["k_turned"], 1)
            for n in range(NT - 1):
                pe.wait_ge(s["k_kept"], n + 1)
                if n == 2:
                    pe.wait_ge(s["st_made"], 1)
                for h in range(HH):
                    mm = pe.matmul(bank[4 + n % 2][:, h * P:(h + 1) * P], kr[:, n, h, :], vrow[:, n, h, :],
                                   start=True, stop=True)
                mm.then_inc(s["kv_mm"], 1)
            pe.wait_ge(s["at_made"], 3 * NT + 4)
            for n in range(NT):
                if n >= 1:
                    pe.wait_ge(s["st_made"], 1 if n == 1 else 1 + HH * (n - 1))
                for h in range(HH):
                    out = bank[n][:, h * P:(h + 1) * P]
                    mm = pe.matmul(out, vrow[:, n, h, :], at[:, n, h, :], start=True, stop=n == 0)
                    if n:
                        mm = pe.matmul(out, sta[:, n - 1, h, :], q[:, cols(h, n)], start=False, stop=True)
                mm.then_inc(s["o_mm"], 1)
            pe.wait_ge(s["osq_made"], 1)
            for h in range(HH):
                pe.matmul(bank[h][:], kit.ones[:], osq[:, h * T:(h + 1) * T], start=True, stop=True
                          ).then_inc(s["o_summed"], 1)
            pe.wait_ge(s["pooled"], HH)
            for c in range(HH):
                if c >= 2:
                    pe.wait_ge(s["hi_made"], c - 1)
                pe.matmul(bank[4 + c % 2][:], kit.s2[:, Q_PW + c * P:Q_PW + (c + 1) * P], p2[:, D_U + c, :],
                          start=True, stop=True).then_inc(s["p_mm"], 1)

        @block.gpsimd
        def _(g):
            kit.clear(g, "in2")
            g.memset(at[:, 0:2, :, :], 0.0).then_inc(s["zeroed"], 1)
            g.memset(at[:, 2:4, :, :], 0.0).then_inc(s["zeroed"], 1)
            link = linker(g, s["pool_chain"])
            link(g.memset(pl[:, :, :, 0:PADT], 0.0))
            u = p2[:, D_U:D_U + HH, :]
            link(g.tensor_copy(pl[:, 0, :, PADT:], u))
            for i, w in enumerate(POOL_WINDOWS):
                a_, b_ = pl[:, i % 2, i:, :], pl[:, (i + 1) % 2, i:, :]
                link(g.tensor_tensor(b_[:, :, PADT:], a_[:, :, PADT:], a_[:, :, PADT - w // 2:PADT + T - w // 2], ALU.add))
            inv = kit.k2[:, M_INV:M_INV + HH * T].rearrange("p (h t) -> p h t", h=HH)
            for i in range(HH):
                m = pl[:, (i + 1) % 2, i, PADT:]
                link(g.tensor_tensor(m, m, inv[:, i, :], ALU.mult))
                g.tensor_tensor(u[:, i, :], m, u[:, i, :], ALU.subtract).then_inc(s["pooled"], 1)



def phase_store(kit):
    nc, d = kit.nc, kit.d
    s = kit.sems("store", ("stored",))
    with nc.Block() as block:
        @block.sync
        def _(sp):
            sp.dma_start(d["out"], kit.x[:]).then_inc(s["stored"], 16)
            sp.wait_ge(s["stored"], 16)


def hybrid_kernel(nc, dram, stop=None):
    ctx = ExitStack()
    with ctx:
        kit = Kit(nc, ctx, dram)

        def sb(c, name, shape, dt=F32):
            return c.enter_context(nc.sbuf_tensor(name, shape, dt))

        kit.bank = [ctx.enter_context(nc.psum_tensor(f"bank{i}", [P, T], F32)) for i in range(8)]
        kit.x = sb(ctx, "x", [P, DC, T])
        kit.xh = sb(ctx, "xh", [P, DC, T], F32R)
        kit.xl = sb(ctx, "xl", [P, DC, T], F32R)
        kit.ones = sb(ctx, "ones", [P, P])
        kit.eps = sb(ctx, "eps", [P, 2])
        with ExitStack() as c1:
            kit.sem_ctx = c1
            kit.k1 = sb(c1, "k1", [P, N_K1])
            kit.biasA = sb(c1, "biasA", [P, A_HEADS, T])
            kit.biasK = sb(c1, "biasK", [P, A_HEADS, NT, NCMP])
            kit.biasC = sb(c1, "biasC", [P, C_HEADS, 256])
            phase_start(kit)
            kit.s1 = sb(c1, "s1", [P, N_S1])
            kit.proj = sb(c1, "proj", [P, N_IN, T])
            kit.sems("out1", OUT1_SEMS, ring=("w_loaded",))
            with nc.Fori(0, DEPTH) as l:
                with ExitStack() as cw:
                    kit.w1 = sb(cw, "w1", [P, CMP_LEN * P])
                    phase_project1(kit, l)
                    with ExitStack() as c2:
                        kit.qf = sb(c2, "qf", [96, B_HEADS, T])
                        kit.kf = sb(c2, "kf", [96, B_HEADS, T])
                        kit.vr = sb(c2, "vr", [P, NT, P])
                        kit.cv = sb(c2, "cv", [P, NT, HD])
                        kit.mv = sb(c2, "mv", [P, NT, B_HEADS * HD])
                        kit.kc = sb(c2, "kc", [P, NCMP])
                        kit.vc = sb(c2, "vc", [NCMP, HD])
                        kit.gate = sb(c2, "gate", [P, NT, 12])
                        kit.nsink = sb(c2, "nsink", [P, C_HEADS])
                        phase_prepare(kit)
                        phase_attention(kit)
                phase_out1(kit, l)
            phase_leave(kit, ("start", "out1"))
        kit.sem_ctx = ctx
        if stop == "block1":
            phase_store(kit)
            return
        with ExitStack() as c1:
            kit.k2 = sb(c1, "k2", [P, N_K2])
            kit.s2 = sb(c1, "s2", [P, N_S2])
            phase_split_x(kit)
            kit.sems("ln", LN_SEMS, ring=("w_loaded",))
            with nc.Fori(0, DEPTH) as l:
                with ExitStack() as c2:
                    hh = sb(c2, "hh1", [P, FC, T], F32R)
                    hl = sb(c2, "hl1", [P, FC, T], F32R)
                    phase_ffn_up(kit, l, "up1", hh, hl)
                    phase_dense_ln(kit, l, "down1", "up", hh, hl, KH, 2, 0.5, 0)
                with ExitStack() as c2:
                    p2 = sb(c2, "p2", [P, N_IN2, T])
                    phase_project2(kit, l, p2)
                    phase_mixers(kit, p2)
                phase_dense_ln(kit, l, "w_out_2", "mix", kit.xh, kit.xl, DC, 1, 1.0, 1)
                with ExitStack() as c2:
                    hh = sb(c2, "hh2", [P, FC, T], F32R)
                    hl = sb(c2, "hl2", [P, FC, T], F32R)
                    phase_ffn_up(kit, l, "up2", hh, hl)
                    phase_dense_ln(kit, l, "down2", "up", hh, hl, KH, 2, 0.5, 2)
        phase_store(kit)



def in_columns():
    sizes = (A_HEADS * HD, 6 * HD, 3 * A_HEADS, 256, 128, ROPE, C_HEADS * HD, 2 * HD, D)
    o = np.concatenate([[0], np.cumsum(sizes)])
    r = lambda a, n: np.arange(a, a + n)
    pad = lambda n: np.full(n, -1)
    kv = [r(o[1] + i * HD, HD) for i in range(6)]
    kr = r(o[5], ROPE)
    swapped = np.concatenate([kr[ROPE // 2:], kr[:ROPE // 2]])
    ck, cv = r(o[7], HD), r(o[7] + HD, HD)
    parts = [r(o[0], 256), kv[2], kv[2], kv[4], kv[4], kv[3], kv[5], kv[0], kv[1], r(o[3], 256), r(o[4], 128),
             cv, kr, swapped, r(o[6], 512), ck, ck, r(o[2], 12), pad(P - 12), r(o[8], D)]
    cols = np.concatenate(parts)
    assert cols.size == N_IN * P
    return cols


def uq_columns():
    out = []
    for h in range(B_HEADS):
        c = np.arange(h * (HD + ROPE), (h + 1) * (HD + ROPE))
        out += [c, c[HD + ROPE // 2:], c[HD:HD + ROPE // 2]]
    return np.concatenate(out)


def bucket(dist):
    dist = np.maximum(dist, 0)
    exact = BKT // 2
    large = exact + (np.log(np.maximum(dist, 1).astype(np.float32) / np.float32(exact))
                     / np.float32(math.log(T / exact)) * np.float32(BKT - exact)).astype(np.int32)
    return np.where(dist < exact, dist, np.minimum(large, BKT - 1))


def shape_constants():
    f32 = np.float32
    p = np.arange(P)
    k1 = np.zeros((P, N_K1), f32)
    k1[:, K_ID:K_ID + P] = np.eye(P)
    k1[:, K_EX:K_EX + P] = np.eye(P)[::-1]
    half = ROPE // 2
    inv = f32(10000.0) ** (-np.arange(half, dtype=f32) / f32(half))
    ang = np.arange(T, dtype=f32)[None, :] * inv[:, None]
    cos, sin = np.cos(ang), np.sin(ang)
    k1[64:96, K_TRIG:K_TRIG + T] = np.concatenate([cos, cos])
    k1[96:128, K_TRIG:K_TRIG + T] = np.concatenate([-sin, sin])
    k1[:, K_CAUSAL:K_CAUSAL + T] = np.where(T - P + p[:, None] - np.arange(T)[None, :] < 0, NEG, 0)
    k1[:, K_ROWOK] = p >= CMP_LEN - 1
    dist = T - 1 - np.arange(2 * T)
    hot = (bucket(dist)[None, :] == np.arange(BKT)[:, None]).astype(f32)
    msk = np.zeros((A_HEADS + C_HEADS, 2 * T), f32)
    msk[:, dist < 0] = NEG
    msk[A_HEADS:, dist >= SWA_WINDOW] = NEG
    k2 = np.zeros((P, N_K2), f32)
    k2[:, 0:P] = np.eye(P)
    for i, m in enumerate(MASKED):
        a, b = (p % 32)[:, None], np.arange(32)[None, :]
        ok = (a == b) if m == 0 else (a // (2 * m) == b // (2 * m)) & (a % (2 * m) < m) & (b % (2 * m) >= m)
        k2[:, M_MASK + 32 * i:M_MASK + 32 * i + 32] = ok
    for i, w in enumerate(POOL_WINDOWS):
        k2[:, M_INV + i * T:M_INV + (i + 1) * T] = f32(1) / np.minimum(np.arange(T) + 1, w).astype(f32)[None, :]
    flags = np.zeros((DEPTH, P, 2), f32)
    flags[0, :, 0] = NEG
    flags[1:, :, 1] = 1
    return k1, k2, hot, msk, flags


def tiles(w, kp=DC):
    n, k, m = w.shape
    return np.ascontiguousarray(w.reshape(n, k // (kp * P), kp, P, m // P, P).transpose(0, 4, 1, 3, 2, 5)
                                ).reshape(-1, P, kp * P)


def by_partition(v):
    return v.reshape(v.shape[0], -1, P).transpose(0, 2, 1)


def layouts(i):
    k1, k2, hot, msk, flags = shape_constants()
    L = DEPTH
    w_in = np.concatenate([i["w_in"], np.zeros((L, D, 1), np.float32)], axis=2)[:, :, in_columns()]
    pe = i["cmp_pos"].transpose(0, 1, 3, 2).reshape(L, P, CMP_LEN)
    uq = i["mla_w_uq"][:, :, uq_columns()].reshape(L, 2, P, B_HEADS * P).transpose(0, 2, 1, 3).reshape(L, P, -1)
    ukv = i["mla_w_ukv"].reshape(L, P, B_HEADS, 2, HD)
    w2 = i["cmp_w2"]
    s1 = np.concatenate([
        by_partition(i["norm_pre"]), by_partition(i["norm_post"]), by_partition(i["mla_q_norm"]),
        by_partition(i["mla_kv_norm"]), np.broadcast_to(i["swa_sinks"][:, None, :], (L, P, C_HEADS)), pe, uq,
        ukv[:, :, :, 0].reshape(L, P, -1), ukv[:, :, :, 1].reshape(L, P, -1), w2[:, 0], w2[:, 0], w2[:, 1]], axis=2)
    w1 = i["cmp_w1"].reshape(L, 2, CMP_LEN, HD, P).transpose(0, 1, 3, 2, 4).reshape(L, P, CMP_LEN * P)
    lb = by_partition(i["lb_param_2"]).transpose(1, 0, 2).reshape(1, P, -1)
    s2 = np.concatenate([
        by_partition(i["ln_g_2"].reshape(L, -1)), by_partition(i["ln_b_2"].reshape(L, -1)),
        by_partition(i["pool_scale_2"]), by_partition(i["hgrn_norm_g_2"]), np.broadcast_to(lb, (L, P, 2 * HH)), flags,
        i["pool_w_2"].transpose(0, 2, 1, 3).reshape(L, P, -1)], axis=2)
    assert s1.shape[2] == N_S1 and s2.shape[2] == N_S2

    def up(k):
        g = tiles(i[f"ffn{k}_gate_2"]).reshape(L, FC, 1, P, DC * P)
        u = tiles(i[f"ffn{k}_up_2"]).reshape(L, FC, 1, P, DC * P)
        return np.concatenate([g, u], axis=2).reshape(-1, P, DC * P)

    return {
        "x": i["x"][0].T.reshape(DC, P, T).transpose(1, 0, 2), "rel": i["rel_bias"].T, "hot": hot, "msk": msk,
        "k1": k1, "k2": k2, "s1": s1, "s2": s2, "w1": w1, "w_in": tiles(w_in), "w_out": tiles(i["w_out"]),
        "w_in_2": tiles(i["w_in_2"]), "w_out_2": tiles(i["w_out_2"]), "up1": up(1), "up2": up(2),
        "down1": tiles(i["ffn1_down_2"], KH), "down2": tiles(i["ffn2_down_2"], KH),
    }


def program(nc, arrays, stop=None):
    dram = {}
    for name, a in arrays.items():
        dram[name] = nc.dram_tensor(f"in_{name}", a.shape, F32, kind="ExternalInput").ap()
    dram["scratch"] = nc.dram_tensor("bias_by_distance", (A_HEADS + C_HEADS, 2 * T), F32, kind="Internal").ap()
    dram["out"] = nc.dram_tensor("out", (P, DC, T), F32, kind="ExternalOutput").ap()
    hybrid_kernel(nc, dram, stop)


def kernel(**inputs):
    import concourse.bacc as bacc
    from concourse.bass_utils import run_bass_kernel_spmd

    arrays = {k: np.ascontiguousarray(v) for k, v in layouts({k: np.asarray(v) for k, v in inputs.items()}).items()}
    nc = bacc.Bacc("TRN2", target_bir_lowering=False, num_devices=1)
    program(nc, arrays)
    r = run_bass_kernel_spmd(nc, [{f"in_{k}": v for k, v in arrays.items()}], core_ids=[0])
    out = r.results[0]["out"]
    return np.ascontiguousarray(out.transpose(1, 0, 2).reshape(D, T).T).reshape(1, T, D)
```

```python
import math
from contextlib import ExitStack

import numpy as np

import concourse.bass as bass
from concourse import mybir

ALU = mybir.AluOpType
ACT = mybir.ActivationFunctionType
AX_X = mybir.AxisListType.X
F32 = mybir.dt.float32
F32R = mybir.dt.float32r

P = 128
T = 512
D = 1024
DC = D // P
NT = T // P
DEPTH = 2
HD = 64
A_HEADS, B_HEADS, C_HEADS = 4, 4, 8
CMP_LEN, CMP_STRIDE = 32, 16
NCMP = T // CMP_STRIDE - 1
ROPE = 32
BKT = 32
SWA_WINDOW = 128
NEG = -1e30
NORM_EPS = 1e-6
LN_EPS = 1e-5
RMS_EPS = 1e-6
FF = ((8 * D // 3 + 127) // 128) * 128
FC = FF // P
KH = FC // 2
ALPHA = (2.0 * DEPTH) ** 0.25
HH = 4
POOL_WINDOWS = (2, 4, 8, 16)
PADT = max(POOL_WINDOWS)

(C_QA, C_KSLC, C_KWIN, C_V, C_CMP, C_CQ, C_CKV, C_KR, C_QC, C_KC, C_GATE, C_Z, N_IN) = (
    0, 2, 3, 4, 5, 6, 8, 9, 10, 14, 15, 16, 24)
D_U, D_Q, D_F, D_V, D_G, N_IN2 = 0, 4, 8, 12, 16, 20

S_GPRE, S_GPOST, S_QN, S_KVN, S_SINK, S_PE = 0, 8, 16, 18, 19, 27
S_UQ = S_PE + CMP_LEN
S_UK = S_UQ + 2 * B_HEADS * P
S_UV = S_UK + B_HEADS * HD
S_W2K = S_UV + B_HEADS * HD
S_W2V = S_W2K + P
N_S1 = S_W2V + P
Q_LNG, Q_LNB, Q_PS, Q_HG, Q_LB, Q_FIRST, Q_NOTFIRST, Q_PW = 0, 24, 48, 52, 53, 61, 62, 63
N_S2 = Q_PW + HH * P
K_ID, K_EX, K_TRIG, K_CAUSAL, K_ROWOK = 0, P, 2 * P, 2 * P + T, 2 * P + 2 * T
N_K1 = K_ROWOK + 1
MASKED = (16, 8, 4, 2, 1, 0)
M_MASK = P
M_INV = M_MASK + 32 * len(MASKED)
N_K2 = M_INV + HH * PADT

RAW_RING = 4
HL_RING = 2
UNROLL = 4



class Stream:

    def __init__(self, nc, ctx, tag, phases, dram, width):
        self.nc, self.tag, self.width = nc, tag, width
        self.raw = ctx.enter_context(nc.sbuf_tensor(f"{tag}_raw", [P, RAW_RING, width], F32))
        self.w_loaded = [ctx.enter_context(nc.semaphore(f"{tag}_w_loaded{u}")) for u in range(RAW_RING)]
        self.hi_made, self.w_split, self.mm_done = (ctx.enter_context(nc.semaphore(f"{tag}_{x}"))
                                                    for x in ("hi_made", "w_split", "mm_done"))
        self.dram = dram
        self.n = dict(phases)
        self.names = [name for name, _ in phases]
        self.base, at = {}, 0
        for name, n in phases:
            self.base[name] = at
            at += n
        self.per_layer = at

    def allocate_parts(self, ctx, tag=""):
        self.hi = ctx.enter_context(self.nc.sbuf_tensor(f"{self.tag}{tag}_hi", [P, HL_RING, self.width], F32R))
        self.lo = ctx.enter_context(self.nc.sbuf_tensor(f"{self.tag}{tag}_lo", [P, HL_RING, self.width], F32R))

    def split_after(self, l, i):
        return l * self.per_layer + i + 1 + RAW_RING

    def done_after(self, l, i):
        return l * self.per_layer + i + 1 + HL_RING

    def fetch(self, sp, name, layer, i, u):
        src = self.dram[name]
        w = src.shape[2]
        sp.dma_start(self.raw[:, u, 0:w], src[bass.ds(layer * self.n[name] + i, 1)].rearrange("o p k -> (o p) k")
                     ).then_inc(self.w_loaded[u], 16)

    def start(self, sp):
        for u in range(RAW_RING):
            self.fetch(sp, self.names[0], 0, u, u)


def load_weights(sp, st, l, name):
    n, base = st.n[name], st.base[name]
    with sp.Fori(1, n // UNROLL) as j:
        for u in range(UNROLL):
            sp.wait_ge(st.w_split, l * st.per_layer + base + j * UNROLL + u + 1)
            st.fetch(sp, name, l, j * UNROLL + u, u)
    after = st.names.index(name) + 1
    nxt, layer = (st.names[after], l) if after < len(st.names) else (st.names[0], l * -1 + (DEPTH - 1))
    for u in range(UNROLL):
        sp.wait_ge(st.w_split, l * st.per_layer + base + n + u + 1)
        st.fetch(sp, nxt, layer, u, u)


def split_tile(v, st, l, i, j, u, w):
    g, r = l * st.per_layer + i + j * UNROLL + u, (i + u) % RAW_RING
    h = (i + u) % HL_RING
    first = (i + u) // RAW_RING * RAW_RING
    v.wait_ge(st.w_loaded[r], (l * (st.per_layer // RAW_RING) + first // RAW_RING + j + 1) * 16)
    v.wait_ge(st.mm_done, g + 1)
    v.tensor_copy(st.hi[:, h, 0:w], st.raw[:, r, 0:w]).then_inc(st.hi_made, 1)
    v.wait_ge(st.hi_made, g + 1)
    v.tensor_tensor(st.lo[:, h, 0:w], st.raw[:, r, 0:w], st.hi[:, h, 0:w].bitcast(F32), ALU.subtract
                    ).then_inc(st.w_split, 1)


def split_weights(v, st, l, name, first, kp, kp_next):
    n, at = st.n[name], st.base[name] + first
    with v.Fori(0, n // UNROLL - 1) as j:
        for u in range(UNROLL):
            split_tile(v, st, l, at, j, u, kp * P)
    for u in range(UNROLL):
        split_tile(v, st, l, at + n - UNROLL, 0, u, (kp if u < UNROLL - first else kp_next) * P)


def three_products(pe, st, out, slot, k, xh, xl, kx, start, stop, low=None):
    wh = st.hi[:, slot, k * P:(k + 1) * P]
    wl = st.lo[:, slot, k * P:(k + 1) * P]
    if low in (None, False):
        pe.matmul(out[:], wh, xh[:, kx, :], start=start, stop=False)
        pe.matmul(out[:], wl, xh[:, kx, :], start=False, stop=False)
    if low in (None, True):
        return pe.matmul(out[:], wh, xl[:, kx, :], start=False, stop=stop)


def dense_tile(pe, st, out_taken, l, name, kp, xh, xl, banks, pieces, j, u):
    base = st.base[name]
    out, h = banks[(u // pieces) % len(banks)], u % pieces
    pe.wait_ge(st.w_split, st.split_after(l, base + j * UNROLL + u))
    if h == 0:
        pe.wait_ge(out_taken, j * (UNROLL // pieces) + u // pieces + 1)
    for k in range(kp):
        kx = h * kp + k
        mm = three_products(pe, st, out, u % HL_RING, k, xh, xl, kx, kx == 0, kx == pieces * kp - 1)
    mm.then_inc(st.mm_done, 1)


def dense_products(pe, st, out_taken, l, name, kp, xh, xl, banks, pieces=1, first=0):
    with pe.Fori(first // UNROLL, st.n[name] // UNROLL) as j:
        for u in range(UNROLL):
            dense_tile(pe, st, out_taken, l, name, kp, xh, xl, banks, pieces, j, u)


def dense_on_arrival(pe, st, s, l, name, kp, xh, xl, banks):
    base = st.base[name]
    pe.wait_ge(st.w_split, st.split_after(l, base + 1))
    pe.wait_ge(s["out_taken"], 2)
    for k in range(kp):
        pe.wait_ge(s["xhi_made"], k + 1)
        for u in range(2):
            three_products(pe, st, banks[u], u, k, xh, xl, k, k == 0, k == kp - 1, low=False)
        pe.wait_ge(s["xlo_made"], k + 1)
        for u in range(2):
            mm = three_products(pe, st, banks[u], u, k, xh, xl, k, k == 0, k == kp - 1, low=True)
            if k == kp - 1:
                mm.then_inc(st.mm_done, 1)
    for u in range(2, UNROLL):
        dense_tile(pe, st, s["out_taken"], l, name, kp, xh, xl, banks, 1, 0, u)


def linker(eng, sem):
    count = [0]

    def link(ins):
        count[0] += 1
        ins.then_inc(sem, 1)
        eng.wait_ge(sem, count[0])
    return link


class Kit:

    def __init__(self, nc, ctx, dram):
        self.nc, self.sem_ctx, self.d = nc, ctx, dram
        self.groups = {}

    def q_swa(self, h):
        return self.xh[:, h, :]

    def q_nsa(self, h):
        return self.xl[:, h, :]

    def k_hi(self, kind):
        return {"slc": self.xl[:, 4, :], "win": self.xl[:, 6, :], "swa": self.k2c[:, 0, :]}[kind]

    def k_lo(self, kind):
        return {"slc": self.xl[:, 5, :], "win": self.xl[:, 7, :], "swa": self.k2c[:, 1, :]}[kind]

    def sems(self, tag, names):
        if tag not in self.groups:
            g, nums = {}, []
            for n in names:
                g[n] = self.sem_ctx.enter_context(self.nc.semaphore(f"{tag}_{n}"))
                nums.append(g[n].num)
            runs = []
            for n in sorted(nums):
                if runs and runs[-1].stop == n:
                    runs[-1] = range(runs[-1].start, n + 1)
                else:
                    runs.append(range(n, n + 1))
            self.groups[tag] = (g, runs)
        return self.groups[tag][0]

    def clear(self, pool, tag):
        for run in self.groups[tag][1]:
            pool.sem_clear(run)


DENSE = ("out_taken",)
OUT1_SEMS = DENSE + ("mhi_made", "mlo_made", "sq_made", "sq_summed", "ln_made", "rstd_made", "scaled", "x_made")
LN_SEMS = DENSE + ("alpha", "small", "c0_mm", "c0_made", "shifted", "sum_made", "sqsum_made", "sq_made", "sum_mm",
                   "sqsum_mm", "mean_made", "meansq_made", "var_made", "ln_made", "rstd_made")



def phase_start(kit):
    nc, d = kit.nc, kit.d
    bank = kit.bank
    with ExitStack() as ctx:
        def sb(name, shape):
            return ctx.enter_context(nc.sbuf_tensor(name, shape, F32))
        rel = sb("rel", [BKT, A_HEADS + C_HEADS])
        hot = sb("hot", [BKT, 2 * T])
        msk = sb("msk", [A_HEADS + C_HEADS, 2 * T])
        vec = sb("vec", [A_HEADS + C_HEADS, 2 * T])
        ha = sb("ha", [P, A_HEADS, 896])
        hc = sb("hc", [P, C_HEADS, 256])
        s = kit.sems("start", ("loaded", "x_loaded", "vec_mm", "vec_made", "stored", "read_a", "read_c",
                               "turned", "kept", "set"))
        block = ctx.enter_context(nc.Block())

        @block.sync
        def _(sp):
            for dst, src in ((rel, "rel"), (hot, "hot"), (msk, "msk"), (kit.k1, "k1")):
                sp.dma_start(dst[:], d[src]).then_inc(s["loaded"], 16)
            sp.dma_start(kit.x[:], d["x"]).then_inc(s["x_loaded"], 16)
            kit.stream.start(sp)
            sp.wait_ge(s["vec_made"], 2)
            sp.dma_start(d["scratch"], vec[:]).then_inc(s["stored"], 16)
            sp.wait_ge(s["stored"], 16)
            src = d["scratch"]
            sp.dma_start(ha[:], bass.AP(src.tensor, src.offset, [[1, P], [2 * T, A_HEADS], [1, 896]])
                         ).then_inc(s["read_a"], 16)
            sp.dma_start(hc[:], bass.AP(src.tensor, src.offset + A_HEADS * 2 * T + 256,
                                        [[1, P], [2 * T, C_HEADS], [1, 256]])).then_inc(s["read_c"], 16)
            sp.wait_ge(s["x_loaded"], 16)

        @block.tensor
        def _(pe):
            pe.sem_inc(kit.stream.mm_done, HL_RING)
            pe.wait_ge(s["loaded"], 64)
            for i in range(2):
                pe.matmul(bank[i][0:A_HEADS + C_HEADS, :], rel[:], hot[:, i * T:(i + 1) * T], start=True, stop=True
                          ).then_inc(s["vec_mm"], 1)
            ex = kit.k1[:, K_EX:K_EX + P]
            pe.wait_ge(s["read_a"], 16)
            for h in range(A_HEADS):
                pe.matmul(bank[2 + h % 2][:], ex, ha[:, h, 0:T], start=True, stop=True).then_inc(s["turned"], 1)
                for n in range(NT):
                    at = 415 - P * n
                    mm = pe.matmul(bank[4 + h % 2][:, n * 32:n * 32 + NCMP], ex,
                                   ha[:, h, at:at + CMP_STRIDE * (NCMP - 1) + 1:CMP_STRIDE], start=True, stop=True)
                mm.then_inc(s["turned"], 1)
                pe.wait_ge(s["kept"], 2 * h + 2)
            pe.wait_ge(s["read_c"], 16)
            for h in range(0, C_HEADS, 2):
                pe.matmul(bank[6 + h // 2 % 2][:], ex, hc[:, h:h + 2, :], start=True, stop=True).then_inc(s["turned"], 1)
                pe.wait_ge(s["kept"], 2 * A_HEADS + h // 2 + 1)

        @block.vector
        def _(v):
            v.sem_inc(kit.stream.w_split, RAW_RING)
            v.memset(kit.ones[:], 1.0).then_inc(s["set"], 1)
            v.memset(kit.eps[:, 0:1], NORM_EPS).then_inc(s["set"], 1)
            v.memset(kit.eps[:, 1:2], LN_EPS).then_inc(s["set"], 1)
            v.wait_ge(s["loaded"], 64)
            for i in range(2):
                v.wait_ge(s["vec_mm"], i + 1)
                v.tensor_tensor(vec[:, i * T:(i + 1) * T], bank[i][0:A_HEADS + C_HEADS, :],
                                msk[:, i * T:(i + 1) * T], ALU.add).then_inc(s["vec_made"], 1)
            for h in range(A_HEADS):
                v.wait_ge(s["turned"], 2 * h + 1)
                v.tensor_copy(kit.biasA[:, h, :], bank[2 + h % 2][:]).then_inc(s["kept"], 1)
                v.wait_ge(s["turned"], 2 * h + 2)
                v.tensor_copy(kit.biasK[:, h, :, :],
                              bank[4 + h % 2][:, 0:P].rearrange("p (n c) -> p n c", c=32)[:, :, 0:NCMP]
                              ).then_inc(s["kept"], 1)
            for h in range(0, C_HEADS, 2):
                v.wait_ge(s["turned"], 2 * A_HEADS + h // 2 + 1)
                v.tensor_copy(kit.biasC[:, h:h + 2, :], bank[6 + h // 2 % 2][:]
                              .rearrange("p (a b) -> p a b", a=2)).then_inc(s["kept"], 1)



def phase_project1(kit, l):
    nc, d, bank = kit.nc, kit.d, kit.bank
    with ExitStack() as ctx:
        st = kit.stream
        st.allocate_parts(ctx, "in")
        hn = kit.proj[:, C_Z:C_Z + DC, :]
        sq = ctx.enter_context(nc.sbuf_tensor("sq1", [P, 2, T], F32))
        rs = ctx.enter_context(nc.sbuf_tensor("rs1", [P, 2, T], F32))
        s = kit.sems("in1", DENSE + ("small", "sq_made", "sq_summed", "ln_made", "rstd_made", "hn_made", "xhi_made",
                                     "xlo_made"))
        block = ctx.enter_context(nc.Block())

        @block.sync
        def _(sp):
            load_weights(sp, st, l, "w_in")

        @block.scalar
        def _(a):
            a.dma_start(kit.s1[:], d["s1"][bass.ds(l, 1)].rearrange("o p k -> (o p) k")).then_inc(s["small"], 16)
            a.dma_start(kit.w1[:], d["w1"][bass.ds(l, 1)].rearrange("o p k -> (o p) k")).then_inc(s["small"], 16)
            for c in range(DC):
                if c >= 2:
                    a.wait_ge(s["sq_summed"], c - 1)
                a.activation(sq[:, c % 2, :], kit.x[:, c, :], ACT.Square).then_inc(s["sq_made"], 1)
            a.wait_ge(s["sq_summed"], DC)
            a.activation(rs[:, 0, :], bank[2][:], ACT.Ln, bias=kit.eps[:, 0:1], scale=1.0 / D).then_inc(s["ln_made"], 1)
            a.wait_ge(s["ln_made"], 1)
            a.activation(rs[:, 1, :], rs[:, 0, :], ACT.Exp, scale=-0.5).then_inc(s["rstd_made"], 1)
            for c in range(DC):
                a.wait_ge(s["hn_made"], c + 1)
                a.activation(kit.xh[:, c, :], hn[:, c, :], ACT.Copy).then_inc(s["xhi_made"], 1)
            a.sem_inc(s["out_taken"], 2)
            with a.Fori(0, N_IN // UNROLL) as j:
                for u in range(UNROLL):
                    a.wait_ge(st.mm_done, st.done_after(l, st.base["w_in"] + j * UNROLL + u))
                    a.activation(kit.proj[:, bass.ds(j * UNROLL + u, 1), :].rearrange("p o t -> p (o t)"), bank[u % 2][:],
                                 ACT.Copy).then_inc(s["out_taken"], 1)
            a.wait_ge(s["small"], 32)

        @block.vector
        def _(v):
            v.wait_ge(s["small"], 32)
            v.wait_ge(s["rstd_made"], 1)
            for c in range(DC):
                v.scalar_tensor_tensor(hn[:, c, :], kit.x[:, c, :], kit.s1[:, S_GPRE + c:S_GPRE + c + 1], rs[:, 1, :],
                                       ALU.mult, ALU.mult).then_inc(s["hn_made"], 1)
                if c >= 1:
                    v.wait_ge(s["xhi_made"], c)
                    v.tensor_tensor(kit.xl[:, c - 1, :], hn[:, c - 1, :], kit.xh[:, c - 1, :].bitcast(F32), ALU.subtract
                                    ).then_inc(s["xlo_made"], 1)
            v.wait_ge(s["xhi_made"], DC)
            v.tensor_tensor(kit.xl[:, DC - 1, :], hn[:, DC - 1, :], kit.xh[:, DC - 1, :].bitcast(F32), ALU.subtract
                            ).then_inc(s["xlo_made"], 1)
            split_weights(v, st, l, "w_in", 0, DC, DC)

        @block.tensor
        def _(pe):
            for c in range(DC):
                pe.wait_ge(s["sq_made"], c + 1)
                pe.matmul(bank[2][:], kit.ones[:], sq[:, c % 2, :], start=c == 0, stop=c == DC - 1
                          ).then_inc(s["sq_summed"], 1)
            pe.wait_ge(s["xlo_made"], DC)
            dense_products(pe, st, s["out_taken"], l, "w_in", DC, kit.xh, kit.xl, bank[0:2])

        @block.gpsimd
        def _(g):
            kit.clear(g, "out1")



def phase_prepare(kit):
    nc, bank, proj, s1, k1 = kit.nc, kit.bank, kit.proj, kit.s1, kit.k1
    with ExitStack() as ctx:
        def sb(name, shape):
            return ctx.enter_context(nc.sbuf_tensor(name, shape, F32))
        rq = sb("rq", [P, 2, T])
        cn = sq = sb("cn", [P, 3, T])
        tpe = sb("tpe", [P, 2, T])
        hid = sb("hid", [P, 2, 32])
        rot = sb("rot", [P, 2, T])
        ge = sb("ge", [P, NT, 12])
        ident = k1[:, K_ID:K_ID + P]
        cos, sin = k1[64:96, K_TRIG:K_TRIG + T], k1[96:128, K_TRIG:K_TRIG + T]
        s = kit.sems("prep", ("sq_made", "sq_summed", "ln_made", "rstd_made", "cn_made", "tpe_made", "cmp_mm", "hid_made",
                              "cmp2_mm", "turned", "v_kept", "gates", "uq_mm", "uq_kept", "uk_mm", "uk_kept",
                              "uv_mm", "uv_kept", "rot_made", "qk_made", "qk_hi", "qk_lo", "misc"))
        block = ctx.enter_context(nc.Block())

        @block.scalar
        def _(a):
            for i, c in enumerate((C_CQ, C_CQ + 1, C_CKV)):
                a.activation(sq[:, i, :], proj[:, c, :], ACT.Square).then_inc(s["sq_made"], 1)
            for i, width in enumerate((2 * P, P)):
                a.wait_ge(s["sq_summed"], i + 1)
                a.activation(rq[:, i, :], bank[i][:], ACT.Ln, bias=kit.eps[:, 0:1], scale=1.0 / width).then_inc(s["ln_made"], 1)
            for i in range(2):
                a.wait_ge(s["ln_made"], i + 1)
                a.activation(rq[:, i, :], rq[:, i, :], ACT.Exp, scale=-0.5).then_inc(s["rstd_made"], 1)
            a.wait_ge(s["turned"], 3)
            a.activation(ge[:], bank[4][:, 0:NT * 12].rearrange("p (n c) -> p n c", c=12), ACT.Exp, scale=-1.0
                         ).then_inc(s["gates"], 1)
            a.activation(kit.vr[:], bank[2][:].rearrange("p (n c) -> p n c", c=P), ACT.Copy).then_inc(s["v_kept"], 1)
            a.activation(kit.cv[:], bank[3][:].rearrange("p (n c) -> p n c", c=P), ACT.Copy
                         ).then_inc(s["v_kept"], 1)
            for c0, n, q in ((C_QA, 2, kit.xl), (C_QC, 4, kit.xh)):
                for par in range(2):
                    r = slice(HD * par, HD * par + HD)
                    a.activation(q[r, par:2 * n:2, :], proj[r, c0:c0 + n, :], ACT.Copy, scale=HD ** -0.5
                                 ).then_inc(s["qk_hi"], 1)
            for c, kind in ((C_KSLC, "slc"), (C_KWIN, "win"), (C_KC, "swa")):
                a.activation(kit.k_hi(kind), proj[:, c, :], ACT.Copy).then_inc(s["qk_hi"], 1)
            a.wait_ge(s["cmp_mm"], 2)
            for i in range(2):
                a.activation(hid[:, i, 0:NCMP], bank[5 + i][:, 0:NCMP], ACT.Silu).then_inc(s["hid_made"], 1)
            a.activation(proj[:, C_Z:C_Z + DC, :], proj[:, C_Z:C_Z + DC, :], ACT.Silu).then_inc(s["misc"], 1)
            for h in range(B_HEADS):
                a.wait_ge(s["uk_mm"], h + 1)
                a.activation(kit.kf[0:HD, h, :], bank[h % 2][0:HD, :], ACT.Copy).then_inc(s["uk_kept"], 1)
            a.wait_ge(s["uv_mm"], 4)
            for n in range(NT):
                a.activation(kit.mv[:, n, :], bank[2 + n // 2][:, (n % 2) * 256:(n % 2) * 256 + 256], ACT.Copy
                             ).then_inc(s["uv_kept"], 1)

        @block.tensor
        def _(pe):
            for n in range(NT):
                pe.transpose(bank[2][:, n * P:(n + 1) * P], proj[:, C_V, n * P:(n + 1) * P], ident)
            pe.transpose(bank[3][:, 0:P], proj[:, C_KR, 0:P], ident).then_inc(s["turned"], 1)
            for n in range(1, NT):
                mm = pe.transpose(bank[3][:, n * P:(n + 1) * P], proj[:, C_KR, n * P:(n + 1) * P], ident)
            mm.then_inc(s["turned"], 1)
            for n in range(NT):
                mm = pe.transpose(bank[4][:, n * 12:(n + 1) * 12], proj[0:12, C_GATE, n * P:(n + 1) * P], ident[0:12, 0:12])
            mm.then_inc(s["turned"], 1)
            pe.wait_ge(s["sq_made"], 2)
            pe.matmul(bank[0][:], kit.ones[:], sq[:, 0, :], start=True, stop=False)
            pe.matmul(bank[0][:], kit.ones[:], sq[:, 1, :], start=False, stop=True).then_inc(s["sq_summed"], 1)
            pe.wait_ge(s["sq_made"], 3)
            pe.matmul(bank[1][:], kit.ones[:], sq[:, 2, :], start=True, stop=True).then_inc(s["sq_summed"], 1)
            pe.wait_ge(s["tpe_made"], 2)
            for i in range(CMP_LEN):
                half, at = divmod(i, CMP_STRIDE)
                first = half * CMP_STRIDE + at
                for b in range(2):
                    rows = slice(HD * b, HD * b + HD)
                    mm = pe.matmul(bank[5 + b][:, 0:NCMP], kit.w1[rows, i * P:(i + 1) * P],
                                   tpe[rows, half, first:first + CMP_STRIDE * (NCMP - 1) + 1:CMP_STRIDE],
                                   start=i == 0, stop=i == CMP_LEN - 1)
                    if i == CMP_LEN - 1:
                        mm.then_inc(s["cmp_mm"], 1)
            for h in range(B_HEADS):
                if h == 0:
                    pe.wait_ge(s["cn_made"], 3)
                if h >= 2:
                    pe.wait_ge(s["uq_kept"], h - 1)
                for k in range(2):
                    mm = pe.matmul(bank[(0, 7)[h % 2]][:], s1[:, S_UQ + (k * B_HEADS + h) * P:S_UQ + (k * B_HEADS + h + 1) * P],
                                   cn[:, k, :], start=k == 0, stop=k == 1)
                mm.then_inc(s["uq_mm"], 1)
            pe.wait_ge(s["hid_made"], 2)
            pe.matmul(bank[4][:, 64:64 + NCMP], s1[:, S_W2K:S_W2K + P], hid[:, 0, 0:NCMP], start=True, stop=True)
            pe.matmul(bank[4][0:NCMP, P:2 * P], hid[:, 1, 0:NCMP], s1[:, S_W2V:S_W2V + P], start=True, stop=True
                      ).then_inc(s["cmp2_mm"], 1)
            pe.wait_ge(s["v_kept"], 2)
            for n in range(NT):
                mm = pe.matmul(bank[2 + n // 2][:, (n % 2) * 256:(n % 2) * 256 + 256], cn[:, 2, n * P:(n + 1) * P],
                               s1[:, S_UV:S_UV + B_HEADS * HD], start=True, stop=True)
                mm.then_inc(s["uv_mm"], 1)
            pe.wait_ge(s["uq_kept"], B_HEADS)
            for h in range(B_HEADS):
                if h >= 2:
                    pe.wait_ge(s["uk_kept"], h - 1)
                pe.matmul(bank[h % 2][0:HD, :], s1[:, S_UK + h * HD:S_UK + (h + 1) * HD], cn[:, 2, :], start=True, stop=True
                          ).then_inc(s["uk_mm"], 1)

        @block.vector
        def _(v):
            pe_rows = s1[:, S_PE:S_PE + CMP_LEN]
            for half in range(2):
                v.tensor_tensor(tpe[:, half, :].rearrange("p (b i) -> p b i", i=CMP_STRIDE),
                                proj[:, C_CMP, :].rearrange("p (b i) -> p b i", i=CMP_STRIDE),
                                pe_rows[:, half * CMP_STRIDE:(half + 1) * CMP_STRIDE].unsqueeze(1)
                                .to_broadcast([P, T // CMP_STRIDE, CMP_STRIDE]), ALU.add).then_inc(s["tpe_made"], 1)
            for i, c in enumerate((C_CQ, C_CQ + 1, C_CKV)):
                v.wait_ge(s["rstd_made"], i // 2 + 1)
                v.scalar_tensor_tensor(cn[:, i, :], proj[:, c, :], s1[:, S_QN + i:S_QN + i + 1], rq[:, i // 2, :],
                                       ALU.mult, ALU.mult).then_inc(s["cn_made"], 1)
            for i, (c0, n, q) in enumerate(((C_QA, 2, kit.xl), (C_QC, 4, kit.xh))):
                for par in range(2):
                    r, o = slice(HD * par, HD * par + HD), slice(HD - HD * par, 2 * HD - HD * par)
                    v.wait_ge(s["qk_hi"], 2 * i + par + 1)
                    for c in range(n):
                        h = 2 * c + par
                        v.scalar_tensor_tensor(q[o, h, :], proj[r, c0 + c, :], HD ** -0.5, q[r, h, :].bitcast(F32),
                                               ALU.mult, ALU.subtract).then_inc(s["qk_lo"], 1)
            for i, (c, kind) in enumerate(((C_KSLC, "slc"), (C_KWIN, "win"), (C_KC, "swa"))):
                v.wait_ge(s["qk_hi"], 5 + i)
                v.tensor_tensor(kit.k_lo(kind), proj[:, c, :], kit.k_hi(kind).bitcast(F32), ALU.subtract
                                ).then_inc(s["qk_lo"], 1)
            v.wait_ge(s["gates"], 1)
            v.tensor_scalar(ge[:], ge[:], 1.0, None, ALU.add).then_inc(s["gates"], 1)
            v.wait_ge(s["gates"], 2)
            v.reciprocal(kit.gate[:], ge[:]).then_inc(s["gates"], 1)
            v.wait_ge(s["gates"], 3)
            v.tensor_scalar(kit.gate[:, 0, 0:12:3], kit.gate[:, 0, 0:12:3], k1[:, K_ROWOK:K_ROWOK + 1], None, ALU.mult
                            ).then_inc(s["gates"], 1)
            v.tensor_scalar(kit.nsink[:], s1[:, S_SINK:S_SINK + C_HEADS], -1.0, None, ALU.mult).then_inc(s["gates"], 1)
            scale = (HD + ROPE) ** -0.5
            for h in range(B_HEADS):
                qb = bank[(0, 7)[h % 2]]
                v.wait_ge(s["uq_mm"], h + 1)
                if h >= 1:
                    v.wait_ge(s["qk_made"], h)
                v.scalar_tensor_tensor(rot[64:96, 0, :], qb[64:96, :], scale, cos, ALU.mult, ALU.mult
                                       ).then_inc(s["rot_made"], 1)
                v.scalar_tensor_tensor(rot[64:96, 1, :], qb[96:128, :], scale, sin, ALU.mult, ALU.mult
                                       ).then_inc(s["rot_made"], 1)
                v.tensor_scalar(kit.qf[0:HD, h, :], qb[0:HD, :], scale, None, ALU.mult).then_inc(s["uq_kept"], 1)
                v.wait_ge(s["rot_made"], 2 * h + 2)
                v.tensor_tensor(kit.qf[64:96, h, :], rot[64:96, 0, :], rot[64:96, 1, :], ALU.add).then_inc(s["qk_made"], 1)
            v.wait_ge(s["qk_made"], B_HEADS)
            v.tensor_tensor(rot[64:96, 0, :], proj[64:96, C_KR, :], cos, ALU.mult).then_inc(s["rot_made"], 1)
            v.tensor_tensor(rot[64:96, 1, :], proj[96:128, C_KR, :], sin, ALU.mult).then_inc(s["rot_made"], 1)
            v.wait_ge(s["rot_made"], 2 * B_HEADS + 2)
            for h in range(B_HEADS):
                v.tensor_tensor(kit.kf[64:96, h, :], rot[64:96, 0, :], rot[64:96, 1, :], ALU.add).then_inc(s["qk_made"], 1)
            v.wait_ge(s["cmp2_mm"], 1)
            v.tensor_scalar(kit.kc[:], bank[4][:, 64:64 + NCMP], HD ** -0.5, None, ALU.mult).then_inc(s["qk_made"], 1)
            v.tensor_copy(kit.vc[:], bank[4][0:NCMP, P:2 * P]).then_inc(s["qk_made"], 1)

        @block.gpsimd
        def _(g):
            kit.clear(g, "in1")



def attention_units():
    units = []
    for pair in range(2):
        for n in range(NT):
            for h in (2 * pair, 2 * pair + 1):
                for b, kind in enumerate(("cmp", "slc", "win")):
                    units.append(dict(kind=kind, n=n, h=h, tile=pair, branch=b, first=b == 0, last=b == 2))
    for pair in range(2):
        for n in range(NT):
            for h in (2 * pair, 2 * pair + 1):
                units.append(dict(kind="mla", n=n, h=h, tile=2 + pair, first=True, last=True))
    for pair in range(4):
        for n in range(NT):
            for h in (2 * pair, 2 * pair + 1):
                units.append(dict(kind="swa", n=n, h=h, tile=4 + pair, first=True, last=True))
    for u in units:
        n = u["n"]
        if u["kind"] == "cmp":
            u["width"], u["keys"] = NCMP, [(0, NCMP)]
        else:
            lo = max(n - 1, 0) if u["kind"] == "swa" else 0
            u["width"], u["keys"] = (n + 1 - lo) * P, [(j, P) for j in range(lo, n + 1)]
            u["lo"] = lo
    return units


L_RING = 4
PT_RING = 3
TURN_LAG, WEIGH_LAG, FINISH_LAG = 2, 3, 4


def phase_attention(kit):
    nc, bank, proj = kit.nc, kit.bank, kit.proj
    units = attention_units()
    NU = len(units)
    by_v = [i % 3 == 0 for i in range(NU)]
    n_v = [sum(by_v[:i + 1]) for i in range(NU)]
    n_a = [i + 1 - n_v[i] for i in range(NU)]
    n_swa = [sum(x["kind"] == "swa" for x in units[:i + 1]) for i in range(NU)]
    n_es = [sum(x.get("branch", 0) > 0 for x in units[:i + 1]) for i in range(NU)]
    rows = []
    for i, u in enumerate(units):
        if not rows or rows[-1][:2] != (u["tile"], u["n"]):
            rows.append((u["tile"], u["n"], i))
        rows[-1] = (u["tile"], u["n"], i)
    row_of = {i: r for r, (_, _, end) in enumerate(rows) for i in range((rows[r - 1][2] + 1) if r else 0, end + 1)}
    ends = {end: r for r, (_, _, end) in enumerate(rows)}
    with ExitStack() as ctx:
        def sb(name, shape):
            return ctx.enter_context(nc.sbuf_tensor(name, shape, F32))
        lg = sb("lg", [P, L_RING, T])
        pt = sb("pt", [P, PT_RING, T])
        orow = sb("orow", [P, 2, P])
        negm = sb("negm", [P, NU])
        tot = sb("tot", [P, NU])
        es = sb("es", [P, NU])
        inv = sb("inv", [P, NU])
        s = kit.sems("att", ("s_mm", "logits", "exps", "sinks", "inv_made", "dens", "turned", "pt_by_v", "pt_by_a",
                             "pv_mm", "out_read", "rows_turned", "mixed", "gated"))
        SB, TB, OB, XB = bank[0:2], bank[2:4], bank[4:6], bank[6:8]
        ident = kit.k1[:, K_ID:K_ID + P]
        block = ctx.enter_context(nc.Block())

        def logits(pe, u, out):
            t = slice(u["n"] * P, (u["n"] + 1) * P)
            if u["kind"] == "cmp":
                r = slice(HD * (u["h"] % 2), HD * (u["h"] % 2) + HD)
                return pe.matmul(out[:, 0:NCMP], proj[r, C_QA + u["h"] // 2, t], kit.kc[r, :], start=True, stop=True)
            if u["kind"] == "mla":
                return pe.matmul(out[:, 0:u["width"]], kit.qf[:, u["h"], t], kit.kf[:, u["h"], 0:u["width"]],
                                 start=True, stop=True)
            q = kit.q_swa(u["h"]) if u["kind"] == "swa" else kit.q_nsa(u["h"])
            w = max(u["width"], 2 * P)
            kt = slice(u["lo"] * P, u["lo"] * P + w)
            pe.matmul(out[:, 0:w], q[:, t], kit.k_hi(u["kind"])[:, kt], start=True, stop=False)
            return pe.matmul(out[:, 0:w], q[:, t], kit.k_lo(u["kind"])[:, kt], start=False, stop=True)

        def values(u, j):
            if u["kind"] == "cmp":
                return kit.vc[:, :], 0
            if u["kind"] == "mla":
                pair = u["h"] // 2
                return kit.mv[:, j, pair * P:(pair + 1) * P], HD * (u["h"] % 2)
            if u["kind"] == "swa":
                return kit.cv[:, j, :], 0
            return kit.vr[:, j, :], 0 if u["kind"] == "slc" else HD

        def bias(u):
            if u["kind"] == "cmp":
                return kit.biasK[:, u["h"], u["n"], :]
            if u["kind"] == "mla":
                return kit.k1[:, K_CAUSAL + T - u["width"]:K_CAUSAL + T]
            if u["kind"] == "swa":
                return kit.biasC[:, u["h"], 256 - u["width"]:256]
            return kit.biasA[:, u["h"], T - u["width"]:T]

        def wait_turned_copy(eng, i):
            if n_v[i]:
                eng.wait_ge(s["pt_by_v"], n_v[i])
            if n_a[i]:
                eng.wait_ge(s["pt_by_a"], n_a[i])

        def copy_shape(u):
            return (P if u["kind"] != "cmp" else NCMP), len(u["keys"]) * P

        @block.tensor
        def _(pe):
            for i in range(NU + FINISH_LAG + 2):
                if i < NU:
                    if i >= 2:
                        pe.wait_ge(s["logits"], i - 1)
                    logits(pe, units[i], SB[i % 2]).then_inc(s["s_mm"], 1)
                x = i - TURN_LAG
                if 0 <= x < NU:
                    u = units[x]
                    pe.wait_ge(s["exps"], x + 1)
                    if x >= 2:
                        wait_turned_copy(pe, x - 2)
                    w, _ = copy_shape(u)
                    for y in range(len(u["keys"])):
                        mm = pe.transpose(TB[x % 2][0:w, y * P:(y + 1) * P], lg[:, x % L_RING, y * P:y * P + w], ident)
                    mm.then_inc(s["turned"], 1)
                x = i - WEIGH_LAG
                if 0 <= x < NU:
                    u = units[x]
                    wait_turned_copy(pe, x)
                    if x >= 2:
                        pe.wait_ge(s["out_read"], x - 1)
                    w, _ = copy_shape(u)
                    for y, (j, _) in enumerate(u["keys"]):
                        mm = pe.matmul(OB[x % 2][:, 0:P], pt[0:w, x % PT_RING, y * P:(y + 1) * P], values(u, j)[0],
                                       start=y == 0, stop=y == len(u["keys"]) - 1)
                    mm.then_inc(s["pv_mm"], 1)
                x = i - FINISH_LAG - 1
                if x in ends:
                    tile, n, end = rows[ends[x]]
                    pe.wait_ge(s["out_read"], end + 1)
                    if tile >= 2:
                        pe.wait_ge(s["mixed"], tile - 1)
                    pe.transpose(XB[tile % 2][:, n * P:(n + 1) * P], orow[:, ends[x] % 2, :], ident
                                 ).then_inc(s["rows_turned"], 1)

        @block.vector
        def _(v):
            for i in range(NU + FINISH_LAG + 2):
                if i < NU:
                    u = units[i]
                    v.wait_ge(s["s_mm"], i + 1)
                    if i >= L_RING:
                        v.wait_ge(s["turned"], i - L_RING + 1)
                    start = kit.nsink[:, u["h"]:u["h"] + 1] if u["kind"] == "swa" else 3e38
                    v.tensor_tensor_reduce(lg[:, i % L_RING, 0:u["width"]], SB[i % 2][:, 0:u["width"]], bias(u), -1.0,
                                           start, ALU.add, ALU.min, negm[:, i:i + 1]).then_inc(s["logits"], 1)
                x = i - TURN_LAG
                if 0 <= x < NU and by_v[x]:
                    w, m = copy_shape(units[x])
                    v.wait_ge(s["turned"], x + 1)
                    if x >= PT_RING:
                        v.wait_ge(s["pv_mm"], x - PT_RING + 1)
                    v.tensor_copy(pt[0:w, x % PT_RING, 0:m], TB[x % 2][0:w, 0:m]).then_inc(s["pt_by_v"], 1)
                x = i - FINISH_LAG
                if 0 <= x < NU:
                    u = units[x]
                    den = tot[:, x:x + 1]
                    v.wait_ge(s["exps"], x + 1)
                    if u["kind"] == "swa":
                        v.wait_ge(s["sinks"], n_swa[x])
                        v.tensor_tensor(den, den, es[:, x:x + 1], ALU.add).then_inc(s["dens"], 1)
                        v.wait_ge(s["dens"], n_swa[x])
                    v.reciprocal(inv[:, x:x + 1], den).then_inc(s["inv_made"], 1)
                    v.wait_ge(s["inv_made"], x + 1)
                    v.wait_ge(s["pv_mm"], x + 1)
                    at = values(u, 0)[1]
                    rows_in = OB[x % 2][:, at:at + HD]
                    r = row_of[x]
                    dst = orow[:, r % 2, HD * (u["h"] % 2):HD * (u["h"] % 2) + HD]
                    if r >= 2:
                        v.wait_ge(s["rows_turned"], r - 1)
                    if "branch" not in u:
                        v.tensor_scalar(dst, rows_in, inv[:, x:x + 1], None, ALU.mult).then_inc(s["out_read"], 1)
                    else:
                        b = u["h"] * 3 + u["branch"]
                        gate = kit.gate[:, u["n"], b:b + 1]
                        if u["branch"] == 0:
                            v.tensor_scalar(dst, rows_in, inv[:, x:x + 1], gate, ALU.mult, ALU.mult
                                            ).then_inc(s["out_read"], 1)
                        else:
                            v.tensor_tensor(es[:, x:x + 1], inv[:, x:x + 1], gate, ALU.mult).then_inc(s["gated"], 1)
                            v.wait_ge(s["gated"], n_es[x])
                            v.wait_ge(s["out_read"], x)
                            v.scalar_tensor_tensor(dst, rows_in, es[:, x:x + 1], dst, ALU.mult, ALU.add
                                                   ).then_inc(s["out_read"], 1)
                x = i - FINISH_LAG - 2
                if x in ends and rows[ends[x]][1] == NT - 1:
                    tile = rows[ends[x]][0]
                    v.wait_ge(s["rows_turned"], ends[x] + 1)
                    z = proj[:, C_Z + tile, :]
                    v.tensor_tensor(z, XB[tile % 2][:], z, ALU.mult).then_inc(s["mixed"], 1)
            last = NU - 1
            assert last in ends

        @block.scalar
        def _(a):
            for i in range(NU + TURN_LAG):
                if i < NU:
                    u = units[i]
                    a.wait_ge(s["logits"], i + 1)
                    row = lg[:, i % L_RING, 0:u["width"]]
                    a.activation(row, row, ACT.Exp, bias=negm[:, i:i + 1], scale=-1.0, accum_out=tot[:, i:i + 1]
                                 ).then_inc(s["exps"], 1)
                    if u["kind"] == "swa":
                        a.activation(es[:, i:i + 1], kit.s1[:, S_SINK + u["h"]:S_SINK + u["h"] + 1], ACT.Exp,
                                     bias=negm[:, i:i + 1]).then_inc(s["sinks"], 1)
                x = i - TURN_LAG
                if 0 <= x < NU and not by_v[x]:
                    w, m = copy_shape(units[x])
                    a.wait_ge(s["turned"], x + 1)
                    if x >= PT_RING:
                        a.wait_ge(s["pv_mm"], x - PT_RING + 1)
                    a.activation(pt[0:w, x % PT_RING, 0:m], TB[x % 2][0:w, 0:m], ACT.Copy).then_inc(s["pt_by_a"], 1)

        @block.gpsimd
        def _(g):
            kit.clear(g, "prep")



def phase_out1(kit, l):
    nc, d, bank = kit.nc, kit.d, kit.bank
    with ExitStack() as ctx:
        st = kit.stream
        st.allocate_parts(ctx, "out")
        y = ctx.enter_context(nc.sbuf_tensor("y1", [P, DC, T], F32))
        sq = ctx.enter_context(nc.sbuf_tensor("sq3", [P, 2, T], F32))
        rs = ctx.enter_context(nc.sbuf_tensor("rs3", [P, 2, T], F32))
        s = kit.sems("out1", OUT1_SEMS)
        block = ctx.enter_context(nc.Block())
        mixed = kit.proj[:, C_Z:C_Z + DC, :]

        @block.sync
        def _(sp):
            load_weights(sp, st, l, "w_out")

        @block.scalar
        def _(a):
            for c in range(DC):
                a.activation(kit.xh[:, c, :], mixed[:, c, :], ACT.Copy).then_inc(s["mhi_made"], 1)
            a.sem_inc(s["out_taken"], 2)
            with a.Fori(0, DC // UNROLL) as j:
                for u in range(UNROLL):
                    a.wait_ge(st.mm_done, st.done_after(l, st.base["w_out"] + j * UNROLL + u))
                    a.activation(y[:, bass.ds(j * UNROLL + u, 1), :].rearrange("p o t -> p (o t)"), bank[u % 2][:],
                                 ACT.Copy).then_inc(s["out_taken"], 1)
            a.wait_ge(s["out_taken"], 2 + DC)
            for c in range(DC):
                if c >= 2:
                    a.wait_ge(s["sq_summed"], c - 1)
                a.activation(sq[:, c % 2, :], y[:, c, :], ACT.Square).then_inc(s["sq_made"], 1)
            a.wait_ge(s["sq_summed"], DC)
            a.activation(rs[:, 0, :], bank[2][:], ACT.Ln, bias=kit.eps[:, 0:1], scale=1.0 / D).then_inc(s["ln_made"], 1)
            a.wait_ge(s["ln_made"], 1)
            a.activation(rs[:, 1, :], rs[:, 0, :], ACT.Exp, scale=-0.5).then_inc(s["rstd_made"], 1)

        @block.vector
        def _(v):
            for c in range(DC):
                v.wait_ge(s["mhi_made"], c + 1)
                v.tensor_tensor(kit.xl[:, c, :], mixed[:, c, :], kit.xh[:, c, :].bitcast(F32), ALU.subtract
                                ).then_inc(s["mlo_made"], 1)
            split_weights(v, st, l, "w_out", 0, DC, DC)
            v.wait_ge(s["rstd_made"], 1)
            for c in range(DC):
                v.scalar_tensor_tensor(y[:, c, :], y[:, c, :], kit.s1[:, S_GPOST + c:S_GPOST + c + 1], rs[:, 1, :],
                                       ALU.mult, ALU.mult).then_inc(s["scaled"], 1)
            for c in range(DC):
                v.wait_ge(s["scaled"], c + 1)
                v.tensor_tensor(kit.x[:, c, :], kit.x[:, c, :], y[:, c, :], ALU.add).then_inc(s["x_made"], 1)

        @block.tensor
        def _(pe):
            pe.wait_ge(s["mlo_made"], DC)
            dense_products(pe, st, s["out_taken"], l, "w_out", DC, kit.xh, kit.xl, bank[0:2])
            for c in range(DC):
                pe.wait_ge(s["sq_made"], c + 1)
                pe.matmul(bank[2][:], kit.ones[:], sq[:, c % 2, :], start=c == 0, stop=c == DC - 1
                          ).then_inc(s["sq_summed"], 1)

        @block.gpsimd
        def _(g):
            kit.clear(g, "att")


def phase_leave(kit, tags):
    st = kit.stream
    with kit.nc.Block() as block:
        @block.sync
        def _(sp):
            wait_stream_end(sp, st)
    with kit.nc.Block() as block:
        @block.gpsimd
        def _(g):
            for tag in tags:
                kit.clear(g, tag)
            for sem in st.w_loaded + [st.hi_made, st.w_split, st.mm_done]:
                g.sem_clear(sem)


def wait_stream_end(sp, st):
    for u in range(RAW_RING):
        sp.wait_ge(st.w_loaded[u], (DEPTH * st.per_layer // RAW_RING + 1) * 16)



MEAN, RSTD = 0, 1


def phase_enter2(kit):
    nc, d, st = kit.nc, kit.d, kit.stream
    s = kit.sems("enter2", ("loaded", "set"))
    with nc.Block() as block:
        @block.sync
        def _(sp):
            st.start(sp)
            sp.dma_start(kit.s2[:], d["s2"][0]).then_inc(s["loaded"], 16)
            sp.dma_start(kit.k2[:], d["k2"]).then_inc(s["loaded"], 16)
            sp.wait_ge(s["loaded"], 32)

        @block.tensor
        def _(pe):
            pe.sem_inc(st.mm_done, HL_RING)

        @block.vector
        def _(v):
            v.sem_inc(st.w_split, RAW_RING)
            v.memset(kit.ln[:, MEAN, :], 0.0).then_inc(s["set"], 1)
            v.memset(kit.ln[:, RSTD, :], 1.0).then_inc(s["set"], 1)
            for u in range(HL_RING):
                split_tile(v, st, 0, 0, 0, u, DC * P)


APPLY_SEMS = ("cent_made", "norm_made", "x_made", "xhi_made", "xlo_made")


def apply_vector(v, kit, s, which):
    x, g = kit.x, Q_LNG + which * DC
    for c in range(DC):
        v.tensor_tensor(x[:, c, :], x[:, c, :], kit.ln[:, MEAN, :], ALU.subtract).then_inc(s["cent_made"], 1)
        v.wait_ge(s["cent_made"], c + 1)
        v.scalar_tensor_tensor(x[:, c, :], x[:, c, :], kit.s2[:, g + c:g + c + 1], kit.ln[:, RSTD, :], ALU.mult, ALU.mult
                               ).then_inc(s["norm_made"], 1)


def apply_scalar(a, kit, s, which):
    x, b = kit.x, Q_LNB + which * DC
    for c in range(DC):
        a.wait_ge(s["norm_made"], c + 1)
        off = kit.s2[:, b + c:b + c + 1]
        a.activation(kit.xh[:, c, :], x[:, c, :], ACT.Identity, bias=off).then_inc(s["xhi_made"], 1)
        a.activation(x[:, c, :], x[:, c, :], ACT.Identity, bias=off).then_inc(s["x_made"], 1)


def apply_gpsimd(g, kit, s):
    for c in range(DC):
        g.wait_ge(s["x_made"], c + 1)
        g.tensor_tensor(kit.xl[:, c, :], kit.x[:, c, :], kit.xh[:, c, :].bitcast(F32), ALU.subtract
                        ).then_inc(s["xlo_made"], 1)



def phase_ffn_up(kit, l, tag, hh, hl, which):
    nc, d, bank = kit.nc, kit.d, kit.bank
    n, base = 2 * FC, kit.stream.base[tag]
    with ExitStack() as ctx:
        st = kit.stream
        sg = ctx.enter_context(nc.sbuf_tensor(f"{tag}_sg", [P, 2, T], F32))
        ub = ctx.enter_context(nc.sbuf_tensor(f"{tag}_ub", [P, 2, T], F32))
        hm = ctx.enter_context(nc.sbuf_tensor(f"{tag}_hm", [P, 2, T], F32))
        s = kit.sems("up", DENSE + APPLY_SEMS + ("h_made", "hhi_made", "hlo_made"))
        block = ctx.enter_context(nc.Block())

        @block.sync
        def _(sp):
            load_weights(sp, st, l, tag)

        @block.scalar
        def _(a):
            a.sem_inc(s["out_taken"], 2)
            apply_scalar(a, kit, s, which)
            with a.Fori(0, n // UNROLL) as j:
                for f in range(2):
                    a.wait_ge(st.mm_done, st.done_after(l, base + j * UNROLL + 2 * f))
                    a.activation(sg[:, f, :], bank[0][:], ACT.Silu).then_inc(s["out_taken"], 1)
                    a.wait_ge(st.mm_done, st.done_after(l, base + j * UNROLL + 2 * f + 1))
                    a.activation(ub[:, f, :], bank[1][:], ACT.Copy).then_inc(s["out_taken"], 1)
                    a.wait_ge(s["h_made"], j * 2 + f + 1)
                    a.activation(hh[:, bass.ds(j * 2 + f, 1), :].rearrange("p o t -> p (o t)"), hm[:, f, :], ACT.Copy
                                 ).then_inc(s["hhi_made"], 1)

        @block.gpsimd
        def _(g):
            kit.clear(g, "ln")
            apply_gpsimd(g, kit, s)
            with g.Fori(0, n // UNROLL) as j:
                for f in range(2):
                    g.wait_ge(s["out_taken"], j * UNROLL + 2 * f + 4)
                    g.tensor_tensor(hm[:, f, :], sg[:, f, :], ub[:, f, :], ALU.mult).then_inc(s["h_made"], 1)
                    g.wait_ge(s["hhi_made"], j * 2 + f + 1)
                    at = bass.ds(j * 2 + f, 1)
                    g.tensor_tensor(hl[:, at, :].rearrange("p o t -> p (o t)"), hm[:, f, :],
                                    hh[:, at, :].rearrange("p o t -> p (o t)").bitcast(F32), ALU.subtract
                                    ).then_inc(s["hlo_made"], 1)

        @block.vector
        def _(v):
            apply_vector(v, kit, s, which)
            split_weights(v, st, l, tag, HL_RING, DC, KH)

        @block.tensor
        def _(pe):
            dense_on_arrival(pe, st, s, l, tag, DC, kit.xh, kit.xl, bank[0:2])
            dense_products(pe, st, s["out_taken"], l, tag, DC, kit.xh, kit.xl, bank[0:2], first=UNROLL)



def phase_dense_ln(kit, l, tag, cleared, xh, xl, kp, kp_next, pieces, scale, next_small=False):
    nc, d, bank, x = kit.nc, kit.d, kit.bank, kit.x
    n, base = DC * pieces, kit.stream.base[tag]
    last = DC - 1
    with ExitStack() as ctx:
        st = kit.stream
        sq = ctx.enter_context(nc.sbuf_tensor(f"{tag}_sq", [P, 2, T], F32))
        acc = ctx.enter_context(nc.sbuf_tensor(f"{tag}_acc", [P, 2, T], F32))
        c0 = ctx.enter_context(nc.sbuf_tensor(f"{tag}_c0", [P, T], F32))
        s = kit.sems("ln", LN_SEMS)
        block = ctx.enter_context(nc.Block())

        def shifted(c):
            return (2, 1)[c] if c < 2 else c + 1

        @block.sync
        def _(sp):
            load_weights(sp, st, l, tag)

        @block.gpsimd
        def _(g):
            kit.clear(g, cleared)
            for c in range(DC):
                g.tensor_scalar(x[:, c, :], x[:, c, :], ALPHA, None, ALU.mult).then_inc(s["alpha"], 1)

            def shift(c):
                g.tensor_tensor(x[:, c, :], x[:, c, :], c0[:], ALU.subtract).then_inc(s["shifted"], 1)
            g.wait_ge(s["alpha"], DC)
            g.wait_ge(s["c0_made"], 1)
            shift(1)
            shift(0)
            for c in range(1, last):
                shift(c + 1)
                g.wait_ge(s["out_taken"], c + 3)
                g.wait_ge(s["shifted"], max(2, shifted(c)))
                if c > 1:
                    g.wait_ge(s["sum_made"], c - 1)
                g.tensor_tensor(acc[:, 0, :], x[:, 0, :] if c == 1 else acc[:, 0, :], x[:, c, :], ALU.add
                                ).then_inc(s["sum_made"], 1)
                g.wait_ge(s["sq_made"], c + 1)
                if c > 1:
                    g.wait_ge(s["sqsum_made"], c - 1)
                g.tensor_tensor(acc[:, 1, :], sq[:, 0, :] if c == 1 else acc[:, 1, :], sq[:, c % 2, :], ALU.add
                                ).then_inc(s["sqsum_made"], 1)

        @block.scalar
        def _(a):
            if next_small:
                a.dma_start(kit.s2[:], d["s2"][bass.ds(l + 1, 1)].rearrange("o p k -> (o p) k")).then_inc(s["small"], 16)
            a.wait_ge(s["c0_mm"], 1)
            a.activation(c0[:], bank[2][:], ACT.Copy, scale=1.0 / P).then_inc(s["c0_made"], 1)
            for c in range(DC):
                if c == 0:
                    a.wait_ge(s["shifted"], shifted(0))
                else:
                    a.wait_ge(s["out_taken"], c + 3)
                if c >= 2:
                    a.wait_ge(s["sqsum_made"], max(1, c - 2))
                a.activation(sq[:, c % 2, :], x[:, c, :], ACT.Square).then_inc(s["sq_made"], 1)
            a.wait_ge(s["sum_mm"], 1)
            a.activation(c0[:], bank[2][:], ACT.Square, scale=1.0 / D).then_inc(s["meansq_made"], 1)
            a.activation(kit.ln[:, MEAN, :], bank[2][:], ACT.Copy, scale=1.0 / D).then_inc(s["mean_made"], 1)
            a.wait_ge(s["var_made"], 1)
            a.activation(c0[:], c0[:], ACT.Ln, bias=kit.eps[:, 1:2]).then_inc(s["ln_made"], 1)
            a.wait_ge(s["ln_made"], 1)
            a.activation(kit.ln[:, RSTD, :], c0[:], ACT.Exp, scale=-0.5).then_inc(s["rstd_made"], 1)
            if next_small:
                a.wait_ge(s["small"], 16)

        @block.vector
        def _(v):
            def split(i):
                split_tile(v, st, l, base, 0, i, (kp if i < n else kp_next) * P)

            for i in range(n):
                if i < n - 1:
                    split(i + HL_RING)
                if i % pieces == pieces - 1:
                    c = i // pieces
                    v.wait_ge(st.mm_done, st.done_after(l, base + i))
                    if c == 0:
                        v.wait_ge(s["alpha"], 1)
                    else:
                        v.wait_ge(s["shifted"], shifted(c))
                    v.scalar_tensor_tensor(x[:, c, :], bank[c % 2][:], scale, x[:, c, :], ALU.mult, ALU.add
                                           ).then_inc(s["out_taken"], 1)
            split(n + HL_RING - 1)
            v.wait_ge(s["sqsum_mm"], 1)
            v.wait_ge(s["meansq_made"], 1)
            v.scalar_tensor_tensor(c0[:], bank[3][:], 1.0 / D, c0[:], ALU.mult, ALU.subtract).then_inc(s["var_made"], 1)

        @block.tensor
        def _(pe):
            pe.sem_inc(s["out_taken"], 2)
            for u in range(UNROLL):
                dense_tile(pe, st, s["out_taken"], l, tag, kp, xh, xl, bank[0:2], pieces, 0, u)
                if u == pieces:
                    pe.wait_ge(s["out_taken"], 3)
                    pe.matmul(bank[2][:], kit.ones[:], x[:, 0, :], start=True, stop=True).then_inc(s["c0_mm"], 1)
            dense_products(pe, st, s["out_taken"], l, tag, kp, xh, xl, bank[0:2], pieces, first=UNROLL)
            pe.wait_ge(s["sum_made"], last - 1)
            pe.matmul(bank[2][:], kit.ones[:], acc[:, 0, :], start=True, stop=False)
            pe.wait_ge(s["sqsum_made"], last - 1)
            pe.matmul(bank[3][:], kit.ones[:], acc[:, 1, :], start=True, stop=False)
            pe.wait_ge(s["out_taken"], DC + 2)
            pe.matmul(bank[2][:], kit.ones[:], x[:, last, :], start=False, stop=True).then_inc(s["sum_mm"], 1)
            pe.wait_ge(s["sq_made"], DC)
            pe.matmul(bank[3][:], kit.ones[:], sq[:, last % 2, :], start=False, stop=True).then_inc(s["sqsum_mm"], 1)



def phase_project2(kit, l, p2):
    nc, d, bank = kit.nc, kit.d, kit.bank
    with ExitStack() as ctx:
        st = kit.stream
        s = kit.sems("in2", DENSE + APPLY_SEMS)
        block = ctx.enter_context(nc.Block())

        @block.sync
        def _(sp):
            load_weights(sp, st, l, "w_in_2")

        @block.scalar
        def _(a):
            a.sem_inc(s["out_taken"], 2)
            apply_scalar(a, kit, s, 1)
            with a.Fori(0, N_IN2 // UNROLL) as j:
                for u in range(UNROLL):
                    a.wait_ge(st.mm_done, st.done_after(l, st.base["w_in_2"] + j * UNROLL + u))
                    a.activation(p2[:, bass.ds(j * UNROLL + u, 1), :].rearrange("p o t -> p (o t)"), bank[u % 2][:],
                                 ACT.Copy).then_inc(s["out_taken"], 1)

        @block.vector
        def _(v):
            apply_vector(v, kit, s, 1)
            split_weights(v, st, l, "w_in_2", HL_RING, DC, DC)

        @block.tensor
        def _(pe):
            dense_on_arrival(pe, st, s, l, "w_in_2", DC, kit.xh, kit.xl, bank[0:2])
            dense_products(pe, st, s["out_taken"], l, "w_in_2", DC, kit.xh, kit.xl, bank[0:2], first=UNROLL)

        @block.gpsimd
        def _(g):
            kit.clear(g, "ln")
            apply_gpsimd(g, kit, s)



LEVELS = (64, 32, 16, 8, 4, 2, 1)


def phase_mixers(kit, p2):
    nc, bank = kit.nc, kit.bank
    W = HH * T
    with ExitStack() as ctx:
        def sb(name, shape):
            return ctx.enter_context(nc.sbuf_tensor(name, shape, F32))
        bb = sb("bb", [P, W])
        kk = sb("kk", [P, W])
        df = sb("df", [P, 2, W])
        xx = sb("xx", [P, 2, W])
        kr = p2[:, D_F:D_F + HH, :].rearrange("p n (h c) -> p n h c", h=HH)
        vrow = sb("vrow", [P, NT, HH, P])
        at = p2[:, D_V:D_V + HH, :].rearrange("p n (h t) -> p n h t", h=HH)
        pl = p2[:, D_V:D_V + HH, :].rearrange("p n t -> p (n t)")[:, 0:2 * (PADT + T)].rearrange("p (s t) -> p s t", s=2)
        ad, tm = (kit.ln[:, i, :].rearrange("p (a t) -> p a t", t=32) for i in range(2))
        sta = sb("sta", [P, 3, HH, P])
        el = sb("el", [P, NT * HH])
        lbv = sb("lbv", [P, 6, HH])
        ident = kit.k2[:, 0:P]
        s = kit.sems("mix", ("chain_v", "abs_f", "exp_f", "ln_f", "ls_made", "km_made", "k_made", "a_made", "m_made", "lb_in",
                             "lb_act", "lb_made", "e2", "e3", "e4", "b_made", "sub_made", "exp_made", "x_made", "top_mm",
                             "lev_mm", "acc_made", "at_made", "v_turned", "v_kept", "qe_exp", "qe_made", "kd_made",
                             "k_turned", "k_kept", "kv_mm", "st_made", "o_mm", "o_kept", "osq_made", "o_summed",
                             "oln_made", "orstd_made", "y_made", "g_made", "u_pad", "pool_chain", "pooled", "p_mm",
                             "hi_made", "p_kept", "lo_made", "zeroed"))
        q = p2[:, D_Q:D_Q + HH, :].rearrange("p h t -> p (h t)")
        f = p2[:, D_F:D_F + HH, :].rearrange("p h t -> p (h t)")
        g_in = p2[:, D_G:D_G + HH, :].rearrange("p h t -> p (h t)")
        LNLB, LNOM, DIF = 3, 4, 5
        ot = xx[:, 0, :]
        osq = xx[:, 1, :]
        rst = df[:, 0, :]
        block = ctx.enter_context(nc.Block())

        def halves(ap, m):
            b = ap.rearrange("p (b m) -> p b m", m=2 * m)
            return b[:, :, 0:m], b[:, :, m:2 * m]

        def cols(h, n, a=0, b=P):
            return slice(h * T + n * P + a, h * T + n * P + b)

        @block.scalar
        def _(a):
            a.wait_ge(s["lb_in"], 1)
            a.activation(lbv[:, 1, :], lbv[:, 0, :], ACT.Abs).then_inc(s["lb_act"], 1)
            a.wait_ge(s["lb_act"], 1)
            a.activation(lbv[:, 1, :], lbv[:, 1, :], ACT.Exp, scale=-1.0).then_inc(s["lb_act"], 1)
            a.activation(df[:, 0, :], f, ACT.Abs).then_inc(s["abs_f"], 1)
            a.wait_ge(s["abs_f"], 1)
            a.activation(df[:, 0, :], df[:, 0, :], ACT.Exp, scale=-1.0).then_inc(s["exp_f"], 1)
            a.wait_ge(s["lb_act"], 2)
            a.activation(lbv[:, 1, :], lbv[:, 1, :], ACT.Ln, bias=kit.ones[:, 0:1]).then_inc(s["lb_act"], 1)
            a.wait_ge(s["exp_f"], 1)
            a.activation(df[:, 0, :], df[:, 0, :], ACT.Ln, bias=kit.ones[:, 0:1]).then_inc(s["ln_f"], 1)
            a.wait_ge(s["lb_made"], 1)
            for h in range(HH):
                a.wait_ge(s["ls_made"], 1)
                a.activation(df[:, 1, h * T:(h + 1) * T], xx[:, 0, h * T:(h + 1) * T], ACT.Abs,
                             bias=lbv[:, DIF, h:h + 1]).then_inc(s["e2"], 1)
            a.wait_ge(s["e2"], HH)
            a.activation(df[:, 1, :], df[:, 1, :], ACT.Exp, scale=-1.0).then_inc(s["e3"], 1)
            a.wait_ge(s["km_made"], 1)
            for h in range(HH):
                a.activation(kk[:, h * T:(h + 1) * T], xx[:, 1, h * T:(h + 1) * T], ACT.Exp,
                             bias=lbv[:, LNOM, h:h + 1]).then_inc(s["k_made"], 1)
            a.wait_ge(s["e3"], 1)
            a.activation(df[:, 1, :], df[:, 1, :], ACT.Ln, bias=kit.ones[:, 0:1]).then_inc(s["e4"], 1)
            for n in range(NT):
                a.wait_ge(s["v_turned"], n + 1)
                a.activation(vrow[:, n, :, :], bank[6 + n % 2][:].rearrange("p (h c) -> p h c", h=HH), ACT.Copy
                             ).then_inc(s["v_kept"], 1)
            for i, m in enumerate(LEVELS):
                a.wait_ge(s["sub_made"], i + 1)
                left, right = halves(df[:, i % 2, :], m)
                a.activation(right, right, ACT.Exp).then_inc(s["exp_made"], 1)
                a.activation(left, left, ACT.Exp, scale=-1.0).then_inc(s["exp_made"], 1)
            a.wait_ge(s["x_made"], 2 * len(LEVELS))
            a.activation(df[:, 1, :], bb[:], ACT.Exp).then_inc(s["qe_exp"], 1)
            a.activation(el[:], bb[:, P - 1:W:P], ACT.Exp).then_inc(s["qe_exp"], 1)
            a.wait_ge(s["sub_made"], len(LEVELS) + 1)
            a.activation(df[:, 0, :], df[:, 0, :], ACT.Exp).then_inc(s["qe_exp"], 1)
            a.wait_ge(s["zeroed"], 2)
            for n in range(NT):
                a.wait_ge(s["top_mm"], NT + n + 1)
                top = bank[n][:].rearrange("p (h t) -> p h t", h=HH)
                a.activation(at[0:64, n, :, 64:128], top[0:64, :, 64:128], ACT.Copy).then_inc(s["at_made"], 1)
                a.activation(at[0:32, n, :, 32:64], top[0:32, :, 32:64], ACT.Copy).then_inc(s["at_made"], 1)
                a.activation(at[64:96, n, :, 96:128], top[64:96, :, 96:128], ACT.Copy).then_inc(s["at_made"], 1)
            for n in range(NT - 1):
                a.wait_ge(s["k_turned"], n + 1)
                a.activation(kr[:, n, :, :], bank[6 + n % 2][:].rearrange("p (h c) -> p h c", h=HH), ACT.Copy
                             ).then_inc(s["k_kept"], 1)
            for n in range(NT):
                a.wait_ge(s["o_mm"], n + 1)
                a.activation(ot.rearrange("p (h t) -> p h t", h=HH)[:, :, n * P:(n + 1) * P],
                             bank[n][:].rearrange("p (h t) -> p h t", h=HH), ACT.Copy).then_inc(s["o_kept"], 1)
            a.wait_ge(s["o_kept"], NT)
            a.activation(osq, ot, ACT.Square).then_inc(s["osq_made"], 1)
            for h in range(HH):
                a.wait_ge(s["o_summed"], h + 1)
                a.activation(rst[:, h * T:(h + 1) * T], bank[h][:], ACT.Ln, bias=kit.eps[:, 0:1], scale=1.0 / P
                             ).then_inc(s["oln_made"], 1)
            for h in range(HH):
                a.wait_ge(s["oln_made"], h + 1)
                a.activation(rst[:, h * T:(h + 1) * T], rst[:, h * T:(h + 1) * T], ACT.Exp, scale=-0.5
                             ).then_inc(s["orstd_made"], 1)
            a.activation(g_in, g_in, ACT.Silu).then_inc(s["g_made"], 1)
            for c in range(HH):
                a.wait_ge(s["p_mm"], c + 1)
                sc = kit.s2[:, Q_PS + c:Q_PS + c + 1]
                a.activation(p2[:, D_U + c, :], bank[4 + c % 2][:], ACT.Copy, scale=sc).then_inc(s["p_kept"], 1)
                a.activation(kit.xh[:, c, :], bank[4 + c % 2][:], ACT.Copy, scale=sc).then_inc(s["hi_made"], 1)
            for c in range(HH):
                a.wait_ge(s["y_made"], 2 * (c + 1))
                a.activation(kit.xh[:, HH + c, :], ot[:, c * T:(c + 1) * T], ACT.Copy).then_inc(s["hi_made"], 1)

        @block.vector
        def _(v):
            lb = kit.s2[:, Q_LB:Q_LB + 2 * HH].rearrange("p (l h) -> p l h", l=2)
            v.tensor_tensor(lbv[:, 0, :], lb[:, 1, :], lb[:, 0, :], ALU.subtract).then_inc(s["lb_in"], 1)
            v.wait_ge(s["lb_act"], 3)
            link = linker(v, s["chain_v"])
            link(v.scalar_tensor_tensor(lbv[:, 2, :], lbv[:, 0, :], 0.0, lbv[:, 1, :], ALU.min, ALU.subtract))
            link(v.tensor_tensor(lbv[:, LNOM, :], lbv[:, 2, :], lbv[:, 0, :], ALU.subtract))
            link(v.tensor_scalar(lbv[:, LNLB, :], lbv[:, 2, :], kit.s2[:, Q_FIRST:Q_FIRST + 1], None, ALU.add))
            link(v.tensor_scalar(lbv[:, LNOM, :], lbv[:, LNOM, :], kit.s2[:, Q_NOTFIRST:Q_NOTFIRST + 1], None, ALU.mult))
            v.tensor_tensor(lbv[:, DIF, :], lbv[:, LNOM, :], lbv[:, LNLB, :], ALU.subtract).then_inc(s["lb_made"], 1)
            v.wait_ge(s["ln_f"], 1)
            v.scalar_tensor_tensor(xx[:, 0, :], f, 0.0, df[:, 0, :], ALU.min, ALU.subtract).then_inc(s["ls_made"], 1)
            v.wait_ge(s["ls_made"], 1)
            v.tensor_tensor(xx[:, 1, :], xx[:, 0, :], f, ALU.subtract).then_inc(s["km_made"], 1)
            v.wait_ge(s["lb_made"], 1)
            for h in range(HH):
                v.tensor_scalar(df[:, 0, h * T:(h + 1) * T], xx[:, 0, h * T:(h + 1) * T], lbv[:, LNOM, h:h + 1],
                                lbv[:, LNLB, h:h + 1], ALU.add, ALU.max).then_inc(s["m_made"], 1)
            v.wait_ge(s["m_made"], HH)
            v.wait_ge(s["e4"], 1)
            v.tensor_tensor(df[:, 0, :], df[:, 0, :], df[:, 1, :], ALU.add).then_inc(s["a_made"], 1)
            v.wait_ge(s["a_made"], 1)
            for h in range(HH):
                for n in range(NT):
                    v.tensor_tensor_scan(bb[:, cols(h, n)], kit.ones[:], df[:, 0, cols(h, n)], 0.0, ALU.mult, ALU.add
                                         ).then_inc(s["b_made"], 1)
            v.tensor_scalar(q, q, float(P) ** -0.5, None, ALU.mult).then_inc(s["b_made"], 1)
            v.wait_ge(s["b_made"], HH * NT + 1)
            v.wait_ge(s["k_made"], HH)

            def sub(i):
                m = LEVELS[i]
                b3 = bb[:].rearrange("p (b m) -> p b m", m=2 * m)
                v.tensor_tensor(df[:, i % 2, :].rearrange("p (b m) -> p b m", m=2 * m), b3,
                                b3[:, :, m - 1:m].to_broadcast([P, W // (2 * m), 2 * m]), ALU.subtract
                                ).then_inc(s["sub_made"], 1)

            def accumulate(i):
                v.wait_ge(s["lev_mm"], i + 1)
                mask = kit.k2[:, M_MASK + 32 * i:M_MASK + 32 * i + 32].unsqueeze(1).to_broadcast([P, NT * HH, 32])
                lev = bank[4 + i % 2][:].rearrange("p (a t) -> p a t", t=32)
                if i == 0:
                    v.tensor_tensor(ad[:], lev, mask, ALU.mult).then_inc(s["acc_made"], 1)
                else:
                    v.tensor_tensor(tm[:], lev, mask, ALU.mult).then_inc(s["acc_made"], 1)
                    v.wait_ge(s["acc_made"], 2 * i)
                    v.tensor_tensor(ad[:], ad[:], tm[:], ALU.add).then_inc(s["acc_made"], 1)
                    v.wait_ge(s["acc_made"], 2 * i + 1)

            sub(0)
            for i, m in enumerate(LEVELS):
                if i + 1 < len(LEVELS):
                    if i >= 1:
                        v.wait_ge(s["x_made"], 2 * i)
                    sub(i + 1)
                v.wait_ge(s["exp_made"], 2 * i + 2)
                if i == 2:
                    v.wait_ge(s["top_mm"], NT)
                if i == 3:
                    v.wait_ge(s["top_mm"], 2 * NT)
                if i >= 4:
                    v.wait_ge(s["lev_mm"], i - 3)
                el_, er_ = halves(df[:, i % 2, :], m)
                kl_, _ = halves(kk[:], m)
                _, qr_ = halves(q, m)
                xl_, xr_ = halves(xx[:, i % 2, :], m)
                v.tensor_tensor(xl_, el_, kl_, ALU.mult).then_inc(s["x_made"], 1)
                v.tensor_tensor(xr_, er_, qr_, ALU.mult).then_inc(s["x_made"], 1)
                if i >= 3:
                    accumulate(i - 3)
            b3 = bb[:].rearrange("p (b m) -> p b m", m=P)
            v.wait_ge(s["x_made"], 2 * len(LEVELS))
            v.tensor_tensor(df[:, 0, :].rearrange("p (b m) -> p b m", m=P),
                            b3[:, :, P - 1:P].to_broadcast([P, NT * HH, P]), b3, ALU.subtract).then_inc(s["sub_made"], 1)
            for i in range(len(LEVELS) - 3, len(MASKED)):
                accumulate(i)
            v.wait_ge(s["qe_exp"], 2)
            v.tensor_tensor(q, q, df[:, 1, :], ALU.mult).then_inc(s["qe_made"], 1)
            v.wait_ge(s["qe_exp"], 3)
            v.tensor_tensor(kk[:], kk[:], df[:, 0, :], ALU.mult).then_inc(s["kd_made"], 1)
            v.wait_ge(s["zeroed"], 2)
            for b in range(4):
                r = slice(32 * b, 32 * b + 32)
                v.tensor_copy(at[r].rearrange("p n h t -> p (n h) t")[:, :, r], ad[r]).then_inc(s["at_made"], 1)
            v.wait_ge(s["kv_mm"], 1)
            v.tensor_copy(sta[:, 0, :, :], bank[4][:].rearrange("p (h c) -> p h c", h=HH)).then_inc(s["st_made"], 1)
            count = 1
            for n in (1, 2):
                v.wait_ge(s["kv_mm"], n + 1)
                v.wait_ge(s["st_made"], count)
                for h in range(HH):
                    v.scalar_tensor_tensor(sta[:, n, h, :], sta[:, n - 1, h, :], el[:, h * NT + n:h * NT + n + 1],
                                           bank[4 + n % 2][:, h * P:(h + 1) * P], ALU.mult, ALU.add
                                           ).then_inc(s["st_made"], 1)
                    count += 1
            v.wait_ge(s["g_made"], 1)
            for h in range(HH):
                seg = slice(h * T, (h + 1) * T)
                v.wait_ge(s["orstd_made"], h + 1)
                v.scalar_tensor_tensor(ot[:, seg], ot[:, seg], kit.s2[:, Q_HG:Q_HG + 1], rst[:, seg], ALU.mult, ALU.mult
                                       ).then_inc(s["y_made"], 1)
                v.wait_ge(s["y_made"], 2 * h + 1)
                v.tensor_tensor(ot[:, seg], ot[:, seg], g_in[:, seg], ALU.mult).then_inc(s["y_made"], 1)
            for c in range(DC):
                v.wait_ge(s["hi_made"], c + 1)
                full = p2[:, D_U + c, :] if c < HH else ot[:, (c - HH) * T:(c - HH + 1) * T]
                v.wait_ge(s["p_kept"], min(c + 1, HH))
                v.tensor_tensor(kit.xl[:, c, :], full, kit.xh[:, c, :].bitcast(F32), ALU.subtract
                                ).then_inc(s["lo_made"], 1)

        @block.tensor
        def _(pe):
            for n in range(NT):
                if n >= 2:
                    pe.wait_ge(s["v_kept"], n - 1)
                for h in range(HH):
                    mm = pe.transpose(bank[6 + n % 2][:, h * P:(h + 1) * P], p2[:, D_V + h, n * P:(n + 1) * P], ident)
                mm.then_inc(s["v_turned"], 1)
            for i, m in enumerate((64, 32)):
                pe.wait_ge(s["x_made"], 2 * i + 2)
                for n in range(NT):
                    for h in range(HH):
                        for a0 in range(0, P, 2 * m):
                            mm = pe.matmul(bank[n][a0:a0 + m, h * P + a0 + m:h * P + a0 + 2 * m],
                                           xx[:, i % 2, cols(h, n, a0, a0 + m)], xx[:, i % 2, cols(h, n, a0 + m, a0 + 2 * m)],
                                           start=True, stop=True)
                    mm.then_inc(s["top_mm"], 1)
            for i in range(len(MASKED)):
                if i < len(MASKED) - 1:
                    pe.wait_ge(s["x_made"], 2 * (i + 3))
                if i >= 2:
                    pe.wait_ge(s["acc_made"], 2 * i - 3)
                for n in range(NT):
                    for h in range(HH):
                        for b in range(4):
                            c = cols(h, n, 32 * b, 32 * b + 32)
                            if i < len(MASKED) - 1:
                                lhs = rhs = xx[:, i % 2, c]
                            else:
                                lhs, rhs = kk[:, c], q[:, c]
                            at0 = (n * HH + h) * 32
                            mm = pe.matmul(bank[4 + i % 2][32 * b:32 * b + 32, at0:at0 + 32], lhs, rhs, start=True, stop=True)
                mm.then_inc(s["lev_mm"], 1)
            pe.wait_ge(s["kd_made"], 1)
            pe.wait_ge(s["v_kept"], NT)
            for n in range(NT - 1):
                if n >= 2:
                    pe.wait_ge(s["k_kept"], n - 1)
                for h in range(HH):
                    mm = pe.transpose(bank[6 + n % 2][:, h * P:(h + 1) * P], kk[:, cols(h, n)], ident)
                mm.then_inc(s["k_turned"], 1)
            for n in range(NT - 1):
                pe.wait_ge(s["k_kept"], n + 1)
                if n == 2:
                    pe.wait_ge(s["st_made"], 1)
                for h in range(HH):
                    mm = pe.matmul(bank[4 + n % 2][:, h * P:(h + 1) * P], kr[:, n, h, :], vrow[:, n, h, :],
                                   start=True, stop=True)
                mm.then_inc(s["kv_mm"], 1)
            pe.wait_ge(s["at_made"], 3 * NT + 4)
            for n in range(NT):
                if n >= 1:
                    pe.wait_ge(s["st_made"], 1 if n == 1 else 1 + HH * (n - 1))
                for h in range(HH):
                    out = bank[n][:, h * P:(h + 1) * P]
                    mm = pe.matmul(out, vrow[:, n, h, :], at[:, n, h, :], start=True, stop=n == 0)
                    if n:
                        mm = pe.matmul(out, sta[:, n - 1, h, :], q[:, cols(h, n)], start=False, stop=True)
                mm.then_inc(s["o_mm"], 1)
            pe.wait_ge(s["osq_made"], 1)
            for h in range(HH):
                pe.matmul(bank[h][:], kit.ones[:], osq[:, h * T:(h + 1) * T], start=True, stop=True
                          ).then_inc(s["o_summed"], 1)
            pe.wait_ge(s["pooled"], HH)
            for c in range(HH):
                if c >= 2:
                    pe.wait_ge(s["hi_made"], c - 1)
                pe.matmul(bank[4 + c % 2][:], kit.s2[:, Q_PW + c * P:Q_PW + (c + 1) * P], p2[:, D_U + c, :],
                          start=True, stop=True).then_inc(s["p_mm"], 1)

        @block.gpsimd
        def _(g):
            kit.clear(g, "in2")
            g.wait_ge(s["v_turned"], NT)
            link = linker(g, s["pool_chain"])
            link(g.memset(pl[:, :, 0:PADT], 0.0))
            for i, w in enumerate(POOL_WINDOWS):
                u = p2[:, D_U + i, :]
                link(g.tensor_tensor(pl[:, 0, PADT + 1:], u[:, 1:], u[:, :T - 1], ALU.add))
                link(g.tensor_copy(pl[:, 0, PADT:PADT + 1], u[:, 0:1]))
                for j in range(1, i + 1):
                    a_, b_ = pl[:, (j - 1) % 2, :], pl[:, j % 2, :]
                    link(g.tensor_tensor(b_[:, PADT:], a_[:, PADT:], a_[:, PADT - 2 ** j:PADT + T - 2 ** j], ALU.add))
                m = pl[:, i % 2, PADT:]
                link(g.tensor_scalar(m[:, PADT:], m[:, PADT:], 1.0 / w, None, ALU.mult))
                link(g.tensor_tensor(m[:, :PADT], m[:, :PADT], kit.k2[:, M_INV + i * PADT:M_INV + (i + 1) * PADT], ALU.mult))
                g.tensor_tensor(u, m, u, ALU.subtract).then_inc(s["pooled"], 1)
                g.wait_ge(s["pooled"], i + 1)
            g.memset(at[:, 0:2, :, :], 0.0).then_inc(s["zeroed"], 1)
            g.memset(at[:, 2:4, :, :], 0.0).then_inc(s["zeroed"], 1)



def phase_store(kit):
    nc, d = kit.nc, kit.d
    s = kit.sems("store", APPLY_SEMS + ("stored",))
    with nc.Block() as block:
        @block.vector
        def _(v):
            apply_vector(v, kit, s, 0)

        @block.scalar
        def _(a):
            for c in range(DC):
                a.wait_ge(s["norm_made"], c + 1)
                a.activation(kit.x[:, c, :], kit.x[:, c, :], ACT.Identity, bias=kit.s2[:, Q_LNB + c:Q_LNB + c + 1]
                             ).then_inc(s["x_made"], 1)

        @block.sync
        def _(sp):
            for c in range(0, DC, 2):
                sp.wait_ge(s["x_made"], c + 2)
                sp.dma_start(d["out"][:, c:c + 2, :], kit.x[:, c:c + 2, :]).then_inc(s["stored"], 16)
            wait_stream_end(sp, kit.stream)
            sp.wait_ge(s["stored"], 16 * DC // 2)


def phase_store_plain(kit):
    s = kit.sems("store", ("stored",))
    with kit.nc.Block() as block:
        @block.sync
        def _(sp):
            sp.dma_start(kit.d["out"], kit.x[:]).then_inc(s["stored"], 16)
            sp.wait_ge(s["stored"], 16)


def hybrid_kernel(nc, dram, stop=None):
    ctx = ExitStack()
    with ctx:
        kit = Kit(nc, ctx, dram)

        def sb(c, name, shape, dt=F32):
            return c.enter_context(nc.sbuf_tensor(name, shape, dt))

        kit.bank = [ctx.enter_context(nc.psum_tensor(f"bank{i}", [P, T], F32)) for i in range(8)]
        kit.x = sb(ctx, "x", [P, DC, T])
        kit.xh = sb(ctx, "xh", [P, DC, T], F32R)
        kit.xl = sb(ctx, "xl", [P, DC, T], F32R)
        kit.ones = sb(ctx, "ones", [P, P])
        kit.eps = sb(ctx, "eps", [P, 2])
        with ExitStack() as c1:
            kit.sem_ctx = c1
            kit.stream = Stream(nc, c1, "one", (("w_in", N_IN), ("w_out", DC)), dram, DC * P)
            kit.k1 = sb(c1, "k1", [P, N_K1])
            kit.biasA = sb(c1, "biasA", [P, A_HEADS, T])
            kit.biasK = sb(c1, "biasK", [P, A_HEADS, NT, NCMP])
            kit.biasC = sb(c1, "biasC", [P, C_HEADS, 256])
            phase_start(kit)
            kit.s1 = sb(c1, "s1", [P, N_S1])
            kit.proj = sb(c1, "proj", [P, N_IN, T])
            kit.sems("out1", OUT1_SEMS)
            with nc.Fori(0, DEPTH) as l:
                with ExitStack() as cw:
                    kit.w1 = sb(cw, "w1", [P, CMP_LEN * P])
                    phase_project1(kit, l)
                    with ExitStack() as c2:
                        kit.qf = sb(c2, "qf", [96, B_HEADS, T])
                        kit.kf = sb(c2, "kf", [96, B_HEADS, T])
                        kit.vr = sb(c2, "vr", [P, NT, P])
                        kit.cv = sb(c2, "cv", [P, NT, P])
                        kit.k2c = sb(c2, "k2c", [P, 2, T], F32R)
                        kit.mv = sb(c2, "mv", [P, NT, B_HEADS * HD])
                        kit.kc = sb(c2, "kc", [P, NCMP])
                        kit.vc = sb(c2, "vc", [NCMP, P])
                        kit.gate = sb(c2, "gate", [P, NT, 12])
                        kit.nsink = sb(c2, "nsink", [P, C_HEADS])
                        phase_prepare(kit)
                        phase_attention(kit)
                phase_out1(kit, l)
            phase_leave(kit, ("start", "out1"))
        kit.sem_ctx = ctx
        if stop == "block1":
            phase_store_plain(kit)
            return
        with ExitStack() as c1:
            kit.stream = Stream(nc, c1, "two", (("up1", 2 * FC), ("down1", 2 * DC), ("w_in_2", N_IN2), ("w_out_2", DC),
                                                ("up2", 2 * FC), ("down2", 2 * DC)), dram, KH * P)
            kit.k2 = sb(c1, "k2", [P, N_K2])
            kit.s2 = sb(c1, "s2", [P, N_S2])
            kit.ln = sb(c1, "ln", [P, 2, T])
            kit.stream.allocate_parts(c1)
            phase_enter2(kit)
            kit.sems("ln", LN_SEMS)
            with nc.Fori(0, DEPTH) as l:
                with ExitStack() as c2:
                    hh = sb(c2, "hh1", [P, FC, T], F32R)
                    hl = sb(c2, "hl1", [P, FC, T], F32R)
                    phase_ffn_up(kit, l, "up1", hh, hl, 0)
                    phase_dense_ln(kit, l, "down1", "up", hh, hl, KH, DC, 2, 0.5)
                with ExitStack() as c2:
                    p2 = sb(c2, "p2", [P, N_IN2, T])
                    phase_project2(kit, l, p2)
                    phase_mixers(kit, p2)
                phase_dense_ln(kit, l, "w_out_2", "mix", kit.xh, kit.xl, DC, DC, 1, 1.0)
                with ExitStack() as c2:
                    hh = sb(c2, "hh2", [P, FC, T], F32R)
                    hl = sb(c2, "hl2", [P, FC, T], F32R)
                    phase_ffn_up(kit, l, "up2", hh, hl, 2)
                    phase_dense_ln(kit, l, "down2", "up", hh, hl, KH, DC, 2, 0.5, next_small=True)
        phase_store(kit)



def in_columns():
    sizes = (A_HEADS * HD, 6 * HD, 3 * A_HEADS, 256, 128, ROPE, C_HEADS * HD, 2 * HD, D)
    o = np.concatenate([[0], np.cumsum(sizes)])
    r = lambda a, n: np.arange(a, a + n)
    pad = lambda n: np.full(n, -1)
    kv = [r(o[1] + i * HD, HD) for i in range(6)]
    kr = r(o[5], ROPE)
    swapped = np.concatenate([kr[ROPE // 2:], kr[:ROPE // 2]])
    ck, cv = r(o[7], HD), r(o[7] + HD, HD)
    parts = [r(o[0], 256), kv[2], kv[2], kv[4], kv[4], kv[3], kv[5], kv[0], kv[1], r(o[3], 256), r(o[4], 128),
             cv, kr, swapped, r(o[6], 512), ck, ck, r(o[2], 12), pad(P - 12), r(o[8], D)]
    cols = np.concatenate(parts)
    assert cols.size == N_IN * P
    return cols


def uq_columns():
    out = []
    for h in range(B_HEADS):
        c = np.arange(h * (HD + ROPE), (h + 1) * (HD + ROPE))
        out += [c, c[HD + ROPE // 2:], c[HD:HD + ROPE // 2]]
    return np.concatenate(out)


def bucket(dist):
    dist = np.maximum(dist, 0)
    exact = BKT // 2
    large = exact + (np.log(np.maximum(dist, 1).astype(np.float32) / np.float32(exact))
                     / np.float32(math.log(T / exact)) * np.float32(BKT - exact)).astype(np.int32)
    return np.where(dist < exact, dist, np.minimum(large, BKT - 1))


def shape_constants():
    f32 = np.float32
    p = np.arange(P)
    k1 = np.zeros((P, N_K1), f32)
    k1[:, K_ID:K_ID + P] = np.eye(P)
    k1[:, K_EX:K_EX + P] = np.eye(P)[::-1]
    half = ROPE // 2
    inv = f32(10000.0) ** (-np.arange(half, dtype=f32) / f32(half))
    ang = np.arange(T, dtype=f32)[None, :] * inv[:, None]
    cos, sin = np.cos(ang), np.sin(ang)
    k1[64:96, K_TRIG:K_TRIG + T] = np.concatenate([cos, cos])
    k1[96:128, K_TRIG:K_TRIG + T] = np.concatenate([-sin, sin])
    k1[:, K_CAUSAL:K_CAUSAL + T] = np.where(T - P + p[:, None] - np.arange(T)[None, :] < 0, NEG, 0)
    k1[:, K_ROWOK] = p >= CMP_LEN - 1
    dist = T - 1 - np.arange(2 * T)
    hot = (bucket(dist)[None, :] == np.arange(BKT)[:, None]).astype(f32)
    msk = np.zeros((A_HEADS + C_HEADS, 2 * T), f32)
    msk[:, dist < 0] = NEG
    msk[A_HEADS:, dist >= SWA_WINDOW] = NEG
    k2 = np.zeros((P, N_K2), f32)
    k2[:, 0:P] = np.eye(P)
    for i, m in enumerate(MASKED):
        a, b = (p % 32)[:, None], np.arange(32)[None, :]
        ok = (a == b) if m == 0 else (a // (2 * m) == b // (2 * m)) & (a % (2 * m) < m) & (b % (2 * m) >= m)
        k2[:, M_MASK + 32 * i:M_MASK + 32 * i + 32] = ok
    for i, w in enumerate(POOL_WINDOWS):
        k2[:, M_INV + i * PADT:M_INV + (i + 1) * PADT] = f32(1) / np.minimum(np.arange(PADT) + 1, w).astype(f32)[None, :]
    flags = np.zeros((DEPTH, P, 2), f32)
    flags[0, :, 0] = NEG
    flags[1:, :, 1] = 1
    return k1, k2, hot, msk, flags


def tiles(w, kp=DC):
    n, k, m = w.shape
    return np.ascontiguousarray(w.reshape(n, k // (kp * P), kp, P, m // P, P).transpose(0, 4, 1, 3, 2, 5)
                                ).reshape(-1, P, kp * P)


def by_partition(v):
    return v.reshape(v.shape[0], -1, P).transpose(0, 2, 1)


def layouts(i):
    k1, k2, hot, msk, flags = shape_constants()
    L = DEPTH
    w_in = np.concatenate([i["w_in"], np.zeros((L, D, 1), np.float32)], axis=2)[:, :, in_columns()]
    pe = i["cmp_pos"].transpose(0, 1, 3, 2).reshape(L, P, CMP_LEN)
    uq = i["mla_w_uq"][:, :, uq_columns()].reshape(L, 2, P, B_HEADS * P).transpose(0, 2, 1, 3).reshape(L, P, -1)
    ukv = i["mla_w_ukv"].reshape(L, P, B_HEADS, 2, HD)
    w2 = i["cmp_w2"]
    s1 = np.concatenate([
        by_partition(i["norm_pre"]), by_partition(i["norm_post"]), by_partition(i["mla_q_norm"]),
        by_partition(i["mla_kv_norm"]), np.broadcast_to(i["swa_sinks"][:, None, :], (L, P, C_HEADS)), pe, uq,
        ukv[:, :, :, 0].reshape(L, P, -1), ukv[:, :, :, 1].reshape(L, P, -1), w2[:, 0], w2[:, 0], w2[:, 1], w2[:, 1]], axis=2)
    w1 = i["cmp_w1"].reshape(L, 2, CMP_LEN, HD, P).transpose(0, 1, 3, 2, 4).reshape(L, P, CMP_LEN * P)
    lb = by_partition(i["lb_param_2"]).transpose(1, 0, 2).reshape(1, P, -1)

    def ln_sets(v, neutral):
        first = np.full((1, D), neutral, np.float32)
        return np.concatenate([by_partition(np.concatenate([first, v[:-1, 2]])), by_partition(v[:, 0]),
                               by_partition(v[:, 1])], axis=2)

    s2 = np.concatenate([
        ln_sets(i["ln_g_2"], 1), ln_sets(i["ln_b_2"], 0),
        by_partition(i["pool_scale_2"]), by_partition(i["hgrn_norm_g_2"]), np.broadcast_to(lb, (L, P, 2 * HH)), flags,
        i["pool_w_2"].transpose(0, 2, 1, 3).reshape(L, P, -1)], axis=2)
    end = np.zeros((1, P, N_S2), np.float32)
    end[0, :, Q_LNG:Q_LNG + DC] = by_partition(i["ln_g_2"][-1:, 2])[0]
    end[0, :, Q_LNB:Q_LNB + DC] = by_partition(i["ln_b_2"][-1:, 2])[0]
    s2 = np.concatenate([s2, end])
    assert s1.shape[2] == N_S1 and s2.shape[2] == N_S2

    def up(k):
        g = tiles(i[f"ffn{k}_gate_2"]).reshape(L, FC, 1, P, DC * P)
        u = tiles(i[f"ffn{k}_up_2"]).reshape(L, FC, 1, P, DC * P)
        return np.concatenate([g, u], axis=2).reshape(-1, P, DC * P)

    return {
        "x": i["x"][0].T.reshape(DC, P, T).transpose(1, 0, 2), "rel": i["rel_bias"].T, "hot": hot, "msk": msk,
        "k1": k1, "k2": k2, "s1": s1, "s2": s2, "w1": w1, "w_in": tiles(w_in), "w_out": tiles(i["w_out"]),
        "w_in_2": tiles(i["w_in_2"]), "w_out_2": tiles(i["w_out_2"]), "up1": up(1), "up2": up(2),
        "down1": tiles(i["ffn1_down_2"], KH), "down2": tiles(i["ffn2_down_2"], KH),
    }


def program(nc, arrays, stop=None):
    dram = {}
    for name, a in arrays.items():
        dram[name] = nc.dram_tensor(f"in_{name}", a.shape, F32, kind="ExternalInput").ap()
    dram["scratch"] = nc.dram_tensor("bias_by_distance", (A_HEADS + C_HEADS, 2 * T), F32, kind="Internal").ap()
    dram["out"] = nc.dram_tensor("out", (P, DC, T), F32, kind="ExternalOutput").ap()
    hybrid_kernel(nc, dram, stop)


def kernel(**inputs):
    import concourse.bacc as bacc
    from concourse.bass_utils import run_bass_kernel_spmd

    arrays = {k: np.ascontiguousarray(v) for k, v in layouts({k: np.asarray(v) for k, v in inputs.items()}).items()}
    nc = bacc.Bacc("TRN2", target_bir_lowering=False, num_devices=1)
    program(nc, arrays)
    r = run_bass_kernel_spmd(nc, [{f"in_{k}": v for k, v in arrays.items()}], core_ids=[0])
    out = r.results[0]["out"]
    return np.ascontiguousarray(out.transpose(1, 0, 2).reshape(D, T).T).reshape(1, T, D)
```

```python
import math
from contextlib import ExitStack

import numpy as np

import concourse.bass as bass
from concourse import mybir

ALU = mybir.AluOpType
ACT = mybir.ActivationFunctionType
AX_X = mybir.AxisListType.X
F32 = mybir.dt.float32
F32R = mybir.dt.float32r

P = 128
T = 512
D = 1024
DC = D // P
NT = T // P
DEPTH = 2
HD = 64
A_HEADS, B_HEADS, C_HEADS = 4, 4, 8
CMP_LEN, CMP_STRIDE = 32, 16
NCMP = T // CMP_STRIDE - 1
ROPE = 32
BKT = 32
SWA_WINDOW = 128
NEG = -1e30
NORM_EPS = 1e-6
LN_EPS = 1e-5
RMS_EPS = 1e-6
FF = ((8 * D // 3 + 127) // 128) * 128
FC = FF // P
KH = FC // 2
ALPHA = (2.0 * DEPTH) ** 0.25
HH = 4
POOL_WINDOWS = (2, 4, 8, 16)
PADT = max(POOL_WINDOWS)

(C_QA, C_KSLC, C_KWIN, C_V, C_CMP, C_CQ, C_CKV, C_KR, C_QC, C_KC, C_GATE, C_Z, N_IN) = (
    0, 2, 3, 4, 5, 6, 8, 9, 10, 14, 15, 16, 24)
D_F, D_Q, D_V, D_U, D_G, N_IN2 = 0, 4, 8, 12, 16, 20

S_GPOST, S_QN, S_KVN, S_SINK, S_PE = 0, 8, 10, 11, 19
S_UQ = S_PE + CMP_LEN
S_UK = S_UQ + 2 * B_HEADS * P
S_UV = S_UK + B_HEADS * HD
S_W2K = S_UV + B_HEADS * HD
S_W2V = S_W2K + P
N_S1 = S_W2V + P
Q_LNG, Q_LNB, Q_PS, Q_HG, Q_LB, Q_FIRST, Q_NOTFIRST, Q_PW = 0, 24, 48, 52, 53, 61, 62, 63
N_S2 = Q_PW + HH * P
K_ID, K_EX, K_TRIG, K_CAUSAL, K_ROWOK = 0, P, 2 * P, 2 * P + T, 2 * P + 2 * T
N_K1 = K_ROWOK + 1
MASKED = (16, 8, 4, 2, 1, 0)
M_MASK = P
M_INV = M_MASK + 32 * len(MASKED)
N_K2 = M_INV + HH * PADT

RAW_RING = 4
HL_RING = 2
UNROLL = 4



class Stream:

    def __init__(self, nc, ctx, tag, phases, dram, width):
        self.nc, self.tag, self.width = nc, tag, width
        self.raw = ctx.enter_context(nc.sbuf_tensor(f"{tag}_raw", [P, RAW_RING, width], F32))
        self.w_loaded = [ctx.enter_context(nc.semaphore(f"{tag}_w_loaded{u}")) for u in range(RAW_RING)]
        self.hi_made, self.w_split, self.mm_done = (ctx.enter_context(nc.semaphore(f"{tag}_{x}"))
                                                    for x in ("hi_made", "w_split", "mm_done"))
        self.dram = dram
        self.n = dict(phases)
        self.names = [name for name, _ in phases]
        self.base, at = {}, 0
        for name, n in phases:
            self.base[name] = at
            at += n
        self.per_layer = at

    def allocate_parts(self, ctx, tag=""):
        self.hi = ctx.enter_context(self.nc.sbuf_tensor(f"{self.tag}{tag}_hi", [P, HL_RING, self.width], F32R))
        self.lo = ctx.enter_context(self.nc.sbuf_tensor(f"{self.tag}{tag}_lo", [P, HL_RING, self.width], F32R))

    def split_after(self, l, i):
        return l * self.per_layer + i + 1 + RAW_RING

    def done_after(self, l, i):
        return l * self.per_layer + i + 1 + HL_RING

    def fetch(self, sp, name, layer, i, u):
        src = self.dram[name]
        w = src.shape[2]
        sp.dma_start(self.raw[:, u, 0:w], src[bass.ds(layer * self.n[name] + i, 1)].rearrange("o p k -> (o p) k")
                     ).then_inc(self.w_loaded[u], 16)

    def start(self, sp):
        for u in range(RAW_RING):
            self.fetch(sp, self.names[0], 0, u, u)


def load_weights(sp, st, l, name):
    n, base = st.n[name], st.base[name]
    with sp.Fori(1, n // UNROLL) as j:
        for u in range(UNROLL):
            sp.wait_ge(st.w_split, l * st.per_layer + base + j * UNROLL + u + 1)
            st.fetch(sp, name, l, j * UNROLL + u, u)
    after = st.names.index(name) + 1
    nxt, layer = (st.names[after], l) if after < len(st.names) else (st.names[0], l * -1 + (DEPTH - 1))
    for u in range(UNROLL):
        sp.wait_ge(st.w_split, l * st.per_layer + base + n + u + 1)
        st.fetch(sp, nxt, layer, u, u)


def split_tile(v, st, l, i, j, u, w):
    g, r = l * st.per_layer + i + j * UNROLL + u, (i + u) % RAW_RING
    h = (i + u) % HL_RING
    first = (i + u) // RAW_RING * RAW_RING
    v.wait_ge(st.w_loaded[r], (l * (st.per_layer // RAW_RING) + first // RAW_RING + j + 1) * 16)
    v.wait_ge(st.mm_done, g + 1)
    v.tensor_copy(st.hi[:, h, 0:w], st.raw[:, r, 0:w]).then_inc(st.hi_made, 1)
    v.wait_ge(st.hi_made, g + 1)
    v.tensor_tensor(st.lo[:, h, 0:w], st.raw[:, r, 0:w], st.hi[:, h, 0:w].bitcast(F32), ALU.subtract
                    ).then_inc(st.w_split, 1)


def split_ahead(v, st, l, name, kp, kp_next):
    n, at = st.n[name], st.base[name] + HL_RING
    with v.Fori(0, n // UNROLL - 1) as j:
        for u in range(UNROLL):
            split_tile(v, st, l, at, j, u, kp * P)
    for u in range(UNROLL):
        split_tile(v, st, l, at + n - UNROLL, 0, u, (kp if u < UNROLL - HL_RING else kp_next) * P)


def split_rest(v, st, l, name, kp):
    n, at = st.n[name], st.base[name] + HL_RING
    with v.Fori(0, n // UNROLL - 1) as j:
        for u in range(UNROLL):
            split_tile(v, st, l, at, j, u, kp * P)
    for u in range(UNROLL - HL_RING):
        split_tile(v, st, l, at + n - UNROLL, 0, u, kp * P)


def three_products(pe, st, out, slot, k, xh, xl, kx, start, stop, low=None):
    wh = st.hi[:, slot, k * P:(k + 1) * P]
    wl = st.lo[:, slot, k * P:(k + 1) * P]
    if low in (None, False):
        pe.matmul(out[:], wh, xh[:, kx, :], start=start, stop=False)
        pe.matmul(out[:], wl, xh[:, kx, :], start=False, stop=False)
    if low in (None, True):
        return pe.matmul(out[:], wh, xl[:, kx, :], start=False, stop=stop)


def dense_tile(pe, st, out_taken, l, name, kp, xh, xl, banks, pieces, j, u):
    base = st.base[name]
    out, h = banks[(u // pieces) % len(banks)], u % pieces
    pe.wait_ge(st.w_split, st.split_after(l, base + j * UNROLL + u))
    if h == 0:
        pe.wait_ge(out_taken, j * (UNROLL // pieces) + u // pieces + 1)
    for k in range(kp):
        kx = h * kp + k
        mm = three_products(pe, st, out, u % HL_RING, k, xh, xl, kx, kx == 0, kx == pieces * kp - 1)
    mm.then_inc(st.mm_done, 1)


def dense_products(pe, st, out_taken, l, name, kp, xh, xl, banks, pieces=1, first=0, last=None):
    with pe.Fori(first // UNROLL, (last or st.n[name]) // UNROLL) as j:
        for u in range(UNROLL):
            dense_tile(pe, st, out_taken, l, name, kp, xh, xl, banks, pieces, j, u)


def dense_on_arrival(pe, st, s, l, name, kp, xh, xl, banks):
    base = st.base[name]
    pe.wait_ge(st.w_split, st.split_after(l, base + 1))
    pe.wait_ge(s["out_taken"], 2)
    for k in range(kp):
        pe.wait_ge(s["xhi_made"], k + 1)
        for u in range(2):
            three_products(pe, st, banks[u], u, k, xh, xl, k, k == 0, k == kp - 1, low=False)
        pe.wait_ge(s["xlo_made"], k + 1)
        for u in range(2):
            mm = three_products(pe, st, banks[u], u, k, xh, xl, k, k == 0, k == kp - 1, low=True)
            if k == kp - 1:
                mm.then_inc(st.mm_done, 1)
    for u in range(2, UNROLL):
        dense_tile(pe, st, s["out_taken"], l, name, kp, xh, xl, banks, 1, 0, u)


def linker(eng, sem):
    count = [0]

    def link(ins):
        count[0] += 1
        ins.then_inc(sem, 1)
        eng.wait_ge(sem, count[0])
    return link


class Kit:

    def __init__(self, nc, ctx, dram):
        self.nc, self.sem_ctx, self.d = nc, ctx, dram
        self.groups = {}

    def q_swa(self, h):
        return self.xh[:, h, :]

    def q_nsa(self, h):
        return self.xl[:, h, :]

    def k_hi(self, kind):
        return {"slc": self.xl[:, 4, :], "win": self.xl[:, 6, :], "swa": self.k2c[:, 0, :]}[kind]

    def k_lo(self, kind):
        return {"slc": self.xl[:, 5, :], "win": self.xl[:, 7, :], "swa": self.k2c[:, 1, :]}[kind]

    def sems(self, tag, names):
        if tag not in self.groups:
            g, nums = {}, []
            for n in names:
                g[n] = self.sem_ctx.enter_context(self.nc.semaphore(f"{tag}_{n}"))
                nums.append(g[n].num)
            runs = []
            for n in sorted(nums):
                if runs and runs[-1].stop == n:
                    runs[-1] = range(runs[-1].start, n + 1)
                else:
                    runs.append(range(n, n + 1))
            self.groups[tag] = (g, runs)
        return self.groups[tag][0]

    def clear(self, pool, tag):
        for run in self.groups[tag][1]:
            pool.sem_clear(run)


DENSE = ("out_taken",)
OUT1_SEMS = DENSE + ("xhi_made", "xlo_made", "sq_made", "sqsum_made", "sq_summed", "ln_made", "rstd_made", "scaled",
                     "x_made", "xsq_made", "xsq_summed", "gains")
LN_SEMS = DENSE + ("alpha", "small", "c0_mm", "c0_made", "shifted", "sum_made", "sqsum_made", "sq_made", "sum_mm",
                   "sqsum_mm", "mean_made", "meansq_made", "var_made", "ln_made", "rstd_made")



def phase_start(kit):
    nc, d = kit.nc, kit.d
    bank = kit.bank
    with ExitStack() as ctx:
        def sb(name, shape):
            return ctx.enter_context(nc.sbuf_tensor(name, shape, F32))
        rel = sb("rel", [BKT, A_HEADS + C_HEADS])
        hot = sb("hot", [BKT, 2 * T])
        msk = sb("msk", [A_HEADS + C_HEADS, 2 * T])
        vec = sb("vec", [A_HEADS + C_HEADS, 2 * T])
        ha = sb("ha", [P, A_HEADS, 896])
        hc = sb("hc", [P, C_HEADS, 256])
        sq = sb("sq0", [P, DC, T])
        s = kit.sems("start", ("loaded", "x_loaded", "vec_mm", "vec_made", "stored", "read_a", "read_c",
                               "turned", "kept", "set", "sq_made", "sq_summed", "ln_made", "rstd_made"))
        block = ctx.enter_context(nc.Block())

        @block.sync
        def _(sp):
            for dst, src in ((rel, "rel"), (hot, "hot"), (msk, "msk"), (kit.k1, "k1")):
                sp.dma_start(dst[:], d[src]).then_inc(s["loaded"], 16)
            sp.dma_start(kit.x[:], d["x"]).then_inc(s["x_loaded"], 16)
            sp.dma_start(kit.gpre[:], d["gpre"][0]).then_inc(s["x_loaded"], 16)
            kit.stream.start(sp)
            sp.wait_ge(s["vec_made"], 2)
            sp.dma_start(d["scratch"], vec[:]).then_inc(s["stored"], 16)
            sp.wait_ge(s["stored"], 16)
            src = d["scratch"]
            sp.dma_start(ha[:], bass.AP(src.tensor, src.offset, [[1, P], [2 * T, A_HEADS], [1, 896]])
                         ).then_inc(s["read_a"], 16)
            sp.dma_start(hc[:], bass.AP(src.tensor, src.offset + A_HEADS * 2 * T + 256,
                                        [[1, P], [2 * T, C_HEADS], [1, 256]])).then_inc(s["read_c"], 16)
            sp.wait_ge(s["x_loaded"], 32)

        @block.scalar
        def _(a):
            a.wait_ge(s["x_loaded"], 32)
            for c in range(DC):
                a.activation(sq[:, c, :], kit.x[:, c, :], ACT.Square).then_inc(s["sq_made"], 1)
            a.wait_ge(s["sq_summed"], 1)
            a.wait_ge(s["set"], 3)
            a.activation(sq[:, 0, :], bank[0][:], ACT.Ln, bias=kit.eps[:, 0:1], scale=1.0 / D).then_inc(s["ln_made"], 1)
            a.wait_ge(s["ln_made"], 1)
            a.activation(kit.xrstd[:], sq[:, 0, :], ACT.Exp, scale=-0.5).then_inc(s["rstd_made"], 1)

        @block.tensor
        def _(pe):
            pe.sem_inc(kit.stream.mm_done, HL_RING)
            pe.wait_ge(s["loaded"], 64)
            for i in range(2):
                pe.matmul(bank[i][0:A_HEADS + C_HEADS, :], rel[:], hot[:, i * T:(i + 1) * T], start=True, stop=True
                          ).then_inc(s["vec_mm"], 1)
            pe.wait_ge(s["set"], 3)
            pe.wait_ge(s["vec_made"], 1)
            for c in range(DC):
                pe.wait_ge(s["sq_made"], c + 1)
                mm = pe.matmul(bank[0][:], kit.ones[:], sq[:, c, :], start=c == 0, stop=c == DC - 1)
            mm.then_inc(s["sq_summed"], 1)
            ex = kit.k1[:, K_EX:K_EX + P]
            pe.wait_ge(s["read_a"], 16)
            for h in range(A_HEADS):
                if h >= 2:
                    pe.wait_ge(s["kept"], 2 * h - 2)
                pe.matmul(bank[2 + h % 2][:], ex, ha[:, h, 0:T], start=True, stop=True).then_inc(s["turned"], 1)
                for n in range(NT):
                    at = 415 - P * n
                    mm = pe.matmul(bank[4 + h % 2][:, n * 32:n * 32 + NCMP], ex,
                                   ha[:, h, at:at + CMP_STRIDE * (NCMP - 1) + 1:CMP_STRIDE], start=True, stop=True)
                mm.then_inc(s["turned"], 1)
            pe.wait_ge(s["read_c"], 16)
            for h in range(0, C_HEADS, 2):
                if h >= 4:
                    pe.wait_ge(s["kept"], 2 * A_HEADS + h // 2 - 1)
                pe.matmul(bank[6 + h // 2 % 2][:], ex, hc[:, h:h + 2, :], start=True, stop=True).then_inc(s["turned"], 1)

        @block.vector
        def _(v):
            v.sem_inc(kit.stream.w_split, RAW_RING)
            v.memset(kit.ones[:], 1.0).then_inc(s["set"], 1)
            v.memset(kit.eps[:, 0:1], NORM_EPS).then_inc(s["set"], 1)
            v.memset(kit.eps[:, 1:2], LN_EPS).then_inc(s["set"], 1)
            v.wait_ge(s["loaded"], 64)
            for i in range(2):
                v.wait_ge(s["vec_mm"], i + 1)
                v.tensor_tensor(vec[:, i * T:(i + 1) * T], bank[i][0:A_HEADS + C_HEADS, :],
                                msk[:, i * T:(i + 1) * T], ALU.add).then_inc(s["vec_made"], 1)
            for h in range(A_HEADS):
                v.wait_ge(s["turned"], 2 * h + 1)
                v.tensor_copy(kit.biasA[:, h, :], bank[2 + h % 2][:]).then_inc(s["kept"], 1)
                v.wait_ge(s["turned"], 2 * h + 2)
                v.tensor_copy(kit.biasK[:, h, :, :],
                              bank[4 + h % 2][:, 0:P].rearrange("p (n c) -> p n c", c=32)[:, :, 0:NCMP]
                              ).then_inc(s["kept"], 1)
            for h in range(0, C_HEADS, 2):
                v.wait_ge(s["turned"], 2 * A_HEADS + h // 2 + 1)
                v.tensor_copy(kit.biasC[:, h:h + 2, :], bank[6 + h // 2 % 2][:]
                              .rearrange("p (a b) -> p a b", a=2)).then_inc(s["kept"], 1)



def phase_project1(kit, l):
    nc, d, bank = kit.nc, kit.d, kit.bank
    with ExitStack() as ctx:
        st = kit.stream
        st.allocate_parts(ctx, "in")
        hn = kit.proj[:, C_Z:C_Z + DC, :]
        s = kit.sems("in1", DENSE + ("small", "hn_made", "xhi_made", "xlo_made"))
        block = ctx.enter_context(nc.Block())

        @block.sync
        def _(sp):
            load_weights(sp, st, l, "w_in")

        @block.scalar
        def _(a):
            a.dma_start(kit.s1[:], d["s1"][bass.ds(l, 1)].rearrange("o p k -> (o p) k")).then_inc(s["small"], 16)
            a.dma_start(kit.w1[:], d["w1"][bass.ds(l, 1)].rearrange("o p k -> (o p) k")).then_inc(s["small"], 16)
            for c in range(DC):
                a.wait_ge(s["hn_made"], c + 1)
                a.activation(kit.xh[:, c, :], hn[:, c, :], ACT.Copy).then_inc(s["xhi_made"], 1)
            a.sem_inc(s["out_taken"], 2)
            with a.Fori(0, N_IN // UNROLL) as j:
                for u in range(UNROLL):
                    a.wait_ge(st.mm_done, st.done_after(l, st.base["w_in"] + j * UNROLL + u))
                    a.activation(kit.proj[:, bass.ds(j * UNROLL + u, 1), :].rearrange("p o t -> p (o t)"), bank[u % 2][:],
                                 ACT.Copy).then_inc(s["out_taken"], 1)
            a.wait_ge(s["small"], 32)

        @block.vector
        def _(v):
            base = st.base["w_in"]
            for u in range(HL_RING):
                split_tile(v, st, l, base, 0, u, DC * P)
            for c in range(DC):
                v.scalar_tensor_tensor(hn[:, c, :], kit.x[:, c, :], kit.gpre[:, c:c + 1], kit.xrstd[:],
                                       ALU.mult, ALU.mult).then_inc(s["hn_made"], 1)
            split_rest(v, st, l, "w_in", DC)

        @block.tensor
        def _(pe):
            dense_on_arrival(pe, st, s, l, "w_in", DC, kit.xh, kit.xl, bank[0:2])
            dense_products(pe, st, s["out_taken"], l, "w_in", DC, kit.xh, kit.xl, bank[0:2], first=UNROLL)

        @block.gpsimd
        def _(g):
            for c in range(DC):
                g.wait_ge(s["xhi_made"], c + 1)
                g.tensor_tensor(kit.xl[:, c, :], hn[:, c, :], kit.xh[:, c, :].bitcast(F32), ALU.subtract
                                ).then_inc(s["xlo_made"], 1)
            kit.clear(g, "out1")



def phase_prepare(kit):
    nc, bank, proj, s1, k1 = kit.nc, kit.bank, kit.proj, kit.s1, kit.k1
    with ExitStack() as ctx:
        def sb(name, shape):
            return ctx.enter_context(nc.sbuf_tensor(name, shape, F32))
        rq = (sb("rq", [P, T])[:], kit.xrstd[:])
        cn = sq = sb("cn", [P, 3, T])
        tpe = sb("tpe", [P, 2, T])
        hid = sb("hid", [P, 2, 32])
        rot = sb("rot", [P, 2, T])
        ge = sb("ge", [P, NT, 12])
        ident = k1[:, K_ID:K_ID + P]
        cos, sin = k1[64:96, K_TRIG:K_TRIG + T], k1[96:128, K_TRIG:K_TRIG + T]
        s = kit.sems("prep", ("sq_made", "sq_summed", "ln_made", "rstd_made", "cn_made", "tpe_made", "cmp_mm", "hid_made",
                              "cmp2_mm", "turned", "v_kept", "gates", "uq_mm", "uq_kept", "uk_mm", "uk_kept",
                              "uv_mm", "uv_kept", "rot_made", "qk_made", "qk_hi", "qk_lo", "misc"))
        block = ctx.enter_context(nc.Block())

        @block.scalar
        def _(a):
            for i, c in enumerate((C_CQ, C_CQ + 1, C_CKV)):
                a.activation(sq[:, i, :], proj[:, c, :], ACT.Square).then_inc(s["sq_made"], 1)
            for i, width in enumerate((2 * P, P)):
                a.wait_ge(s["sq_summed"], i + 1)
                a.activation(rq[i], bank[i][:], ACT.Ln, bias=kit.eps[:, 0:1], scale=1.0 / width).then_inc(s["ln_made"], 1)
            for i in range(2):
                a.wait_ge(s["ln_made"], i + 1)
                a.activation(rq[i], rq[i], ACT.Exp, scale=-0.5).then_inc(s["rstd_made"], 1)
            a.wait_ge(s["turned"], 3)
            a.activation(ge[:], bank[4][:, 0:NT * 12].rearrange("p (n c) -> p n c", c=12), ACT.Exp, scale=-1.0
                         ).then_inc(s["gates"], 1)
            a.activation(kit.vr[:], bank[2][:].rearrange("p (n c) -> p n c", c=P), ACT.Copy).then_inc(s["v_kept"], 1)
            a.activation(kit.cv[:], bank[3][:].rearrange("p (n c) -> p n c", c=P), ACT.Copy
                         ).then_inc(s["v_kept"], 1)
            for c0, n, q in ((C_QA, 2, kit.xl), (C_QC, 4, kit.xh)):
                for par in range(2):
                    r = slice(HD * par, HD * par + HD)
                    a.activation(q[r, par:2 * n:2, :], proj[r, c0:c0 + n, :], ACT.Copy, scale=HD ** -0.5
                                 ).then_inc(s["qk_hi"], 1)
            for c, kind in ((C_KSLC, "slc"), (C_KWIN, "win"), (C_KC, "swa")):
                a.activation(kit.k_hi(kind), proj[:, c, :], ACT.Copy).then_inc(s["qk_hi"], 1)
            a.wait_ge(s["uv_mm"], 4)
            for n in range(NT):
                a.activation(kit.mv[:, n, :], bank[2 + n // 2][:, (n % 2) * 256:(n % 2) * 256 + 256], ACT.Copy
                             ).then_inc(s["uv_kept"], 1)
            a.activation(proj[:, C_Z:C_Z + DC, :], proj[:, C_Z:C_Z + DC, :], ACT.Silu).then_inc(s["misc"], 1)
            a.wait_ge(s["cmp_mm"], 2)
            for i in range(2):
                a.activation(hid[:, i, 0:NCMP], bank[5 + i][:, 0:NCMP], ACT.Silu).then_inc(s["hid_made"], 1)
            for h in range(B_HEADS):
                a.wait_ge(s["uk_mm"], h + 1)
                a.activation(kit.kf[0:HD, h, :], bank[h % 2][0:HD, :], ACT.Copy).then_inc(s["uk_kept"], 1)

        @block.tensor
        def _(pe):
            for n in range(NT):
                pe.transpose(bank[2][:, n * P:(n + 1) * P], proj[:, C_V, n * P:(n + 1) * P], ident)
            pe.transpose(bank[3][:, 0:P], proj[:, C_KR, 0:P], ident).then_inc(s["turned"], 1)
            for n in range(1, NT):
                mm = pe.transpose(bank[3][:, n * P:(n + 1) * P], proj[:, C_KR, n * P:(n + 1) * P], ident)
            mm.then_inc(s["turned"], 1)
            for n in range(NT):
                mm = pe.transpose(bank[4][:, n * 12:(n + 1) * 12], proj[0:12, C_GATE, n * P:(n + 1) * P], ident[0:12, 0:12])
            mm.then_inc(s["turned"], 1)
            pe.wait_ge(s["sq_made"], 2)
            pe.matmul(bank[0][:], kit.ones[:], sq[:, 0, :], start=True, stop=False)
            pe.matmul(bank[0][:], kit.ones[:], sq[:, 1, :], start=False, stop=True).then_inc(s["sq_summed"], 1)
            pe.wait_ge(s["sq_made"], 3)
            pe.matmul(bank[1][:], kit.ones[:], sq[:, 2, :], start=True, stop=True).then_inc(s["sq_summed"], 1)
            def compress(steps):
                for i in steps:
                    half, at = divmod(i, CMP_STRIDE)
                    first = half * CMP_STRIDE + at
                    for b in range(2):
                        rows = slice(HD * b, HD * b + HD)
                        mm = pe.matmul(bank[5 + b][:, 0:NCMP], kit.w1[rows, i * P:(i + 1) * P],
                                       tpe[rows, half, first:first + CMP_STRIDE * (NCMP - 1) + 1:CMP_STRIDE],
                                       start=i == 0, stop=i == CMP_LEN - 1)
                        if i == CMP_LEN - 1:
                            mm.then_inc(s["cmp_mm"], 1)

            def up_queries(h):
                if h >= 2:
                    pe.wait_ge(s["uq_kept"], h - 1)
                for k in range(2):
                    mm = pe.matmul(bank[(0, 7)[h % 2]][:], s1[:, S_UQ + (k * B_HEADS + h) * P:S_UQ + (k * B_HEADS + h + 1) * P],
                                   cn[:, k, :], start=k == 0, stop=k == 1)
                mm.then_inc(s["uq_mm"], 1)

            pe.wait_ge(s["tpe_made"], 2)
            compress(range(0, 4))
            pe.wait_ge(s["cn_made"], 3)
            up_queries(0)
            up_queries(1)
            compress(range(4, 8))
            up_queries(2)
            compress(range(8, 14))
            up_queries(3)
            pe.wait_ge(s["v_kept"], 2)
            for n in range(NT):
                mm = pe.matmul(bank[2 + n // 2][:, (n % 2) * 256:(n % 2) * 256 + 256], cn[:, 2, n * P:(n + 1) * P],
                               s1[:, S_UV:S_UV + B_HEADS * HD], start=True, stop=True)
                mm.then_inc(s["uv_mm"], 1)
            compress(range(14, CMP_LEN))
            pe.wait_ge(s["uq_kept"], B_HEADS)
            for h in range(B_HEADS):
                if h >= 2:
                    pe.wait_ge(s["uk_kept"], h - 1)
                if h == 2:
                    pe.wait_ge(s["hid_made"], 2)
                    pe.matmul(bank[4][:, 64:64 + NCMP], s1[:, S_W2K:S_W2K + P], hid[:, 0, 0:NCMP], start=True, stop=True)
                    pe.matmul(bank[4][0:NCMP, P:2 * P], hid[:, 1, 0:NCMP], s1[:, S_W2V:S_W2V + P], start=True, stop=True
                              ).then_inc(s["cmp2_mm"], 1)
                pe.matmul(bank[h % 2][0:HD, :], s1[:, S_UK + h * HD:S_UK + (h + 1) * HD], cn[:, 2, :], start=True, stop=True
                          ).then_inc(s["uk_mm"], 1)

        @block.vector
        def _(v):
            pe_rows = s1[:, S_PE:S_PE + CMP_LEN]
            for half in range(2):
                v.tensor_tensor(tpe[:, half, :].rearrange("p (b i) -> p b i", i=CMP_STRIDE),
                                proj[:, C_CMP, :].rearrange("p (b i) -> p b i", i=CMP_STRIDE),
                                pe_rows[:, half * CMP_STRIDE:(half + 1) * CMP_STRIDE].unsqueeze(1)
                                .to_broadcast([P, T // CMP_STRIDE, CMP_STRIDE]), ALU.add).then_inc(s["tpe_made"], 1)
            v.tensor_tensor(rot[64:96, 0, :], proj[64:96, C_KR, :], cos, ALU.mult).then_inc(s["rot_made"], 1)
            v.tensor_tensor(rot[64:96, 1, :], proj[96:128, C_KR, :], sin, ALU.mult).then_inc(s["rot_made"], 1)
            v.wait_ge(s["rot_made"], 2)
            for h in range(B_HEADS):
                v.tensor_tensor(kit.kf[64:96, h, :], rot[64:96, 0, :], rot[64:96, 1, :], ALU.add).then_inc(s["qk_made"], 1)
            for i, c in enumerate((C_CQ, C_CQ + 1, C_CKV)):
                v.wait_ge(s["rstd_made"], i // 2 + 1)
                v.scalar_tensor_tensor(cn[:, i, :], proj[:, c, :], s1[:, S_QN + i:S_QN + i + 1], rq[i // 2],
                                       ALU.mult, ALU.mult).then_inc(s["cn_made"], 1)

            def rope_queries(h):
                scale = (HD + ROPE) ** -0.5
                qb = bank[(0, 7)[h % 2]]
                v.wait_ge(s["uq_mm"], h + 1)
                v.wait_ge(s["qk_made"], B_HEADS + h)
                v.scalar_tensor_tensor(rot[64:96, 0, :], qb[64:96, :], scale, cos, ALU.mult, ALU.mult
                                       ).then_inc(s["rot_made"], 1)
                v.scalar_tensor_tensor(rot[64:96, 1, :], qb[96:128, :], scale, sin, ALU.mult, ALU.mult
                                       ).then_inc(s["rot_made"], 1)
                v.tensor_scalar(kit.qf[0:HD, h, :], qb[0:HD, :], scale, None, ALU.mult).then_inc(s["uq_kept"], 1)
                v.wait_ge(s["rot_made"], 2 * h + 4)
                v.tensor_tensor(kit.qf[64:96, h, :], rot[64:96, 0, :], rot[64:96, 1, :], ALU.add).then_inc(s["qk_made"], 1)

            def low_queries(i, par):
                c0, n, q = ((C_QA, 2, kit.xl), (C_QC, 4, kit.xh))[i]
                r, o = slice(HD * par, HD * par + HD), slice(HD - HD * par, 2 * HD - HD * par)
                v.wait_ge(s["qk_hi"], 2 * i + par + 1)
                for c in range(n):
                    h = 2 * c + par
                    v.scalar_tensor_tensor(q[o, h, :], proj[r, c0 + c, :], HD ** -0.5, q[r, h, :].bitcast(F32),
                                           ALU.mult, ALU.subtract).then_inc(s["qk_lo"], 1)

            rope_queries(0)
            rope_queries(1)
            low_queries(0, 0)
            low_queries(0, 1)
            rope_queries(2)
            low_queries(1, 0)
            rope_queries(3)
            low_queries(1, 1)
            for i, (c, kind) in enumerate(((C_KSLC, "slc"), (C_KWIN, "win"), (C_KC, "swa"))):
                v.wait_ge(s["qk_hi"], 5 + i)
                v.tensor_tensor(kit.k_lo(kind), proj[:, c, :], kit.k_hi(kind).bitcast(F32), ALU.subtract
                                ).then_inc(s["qk_lo"], 1)
            v.wait_ge(s["gates"], 1)
            v.tensor_scalar(ge[:], ge[:], 1.0, None, ALU.add).then_inc(s["gates"], 1)
            v.wait_ge(s["gates"], 2)
            v.reciprocal(kit.gate[:], ge[:]).then_inc(s["gates"], 1)
            v.wait_ge(s["gates"], 3)
            v.tensor_scalar(kit.gate[:, 0, 0:12:3], kit.gate[:, 0, 0:12:3], k1[:, K_ROWOK:K_ROWOK + 1], None, ALU.mult
                            ).then_inc(s["gates"], 1)
            v.tensor_scalar(kit.nsink[:], s1[:, S_SINK:S_SINK + C_HEADS], -1.0, None, ALU.mult).then_inc(s["gates"], 1)
            v.wait_ge(s["cmp2_mm"], 1)
            v.tensor_scalar(kit.kc[:], bank[4][:, 64:64 + NCMP], HD ** -0.5, None, ALU.mult).then_inc(s["qk_made"], 1)
            v.tensor_copy(kit.vc[:], bank[4][0:NCMP, P:2 * P]).then_inc(s["qk_made"], 1)

        @block.gpsimd
        def _(g):
            kit.clear(g, "in1")



def attention_units():
    units = []
    for pair in range(2):
        for n in range(NT):
            for h in (2 * pair, 2 * pair + 1):
                for b, kind in enumerate(("cmp", "slc", "win")):
                    units.append(dict(kind=kind, n=n, h=h, tile=pair, branch=b, first=b == 0, last=b == 2))
    for pair in range(2):
        for n in range(NT):
            for h in (2 * pair, 2 * pair + 1):
                units.append(dict(kind="mla", n=n, h=h, tile=2 + pair, first=True, last=True))
    for pair in range(4):
        for n in range(NT):
            for h in (2 * pair, 2 * pair + 1):
                units.append(dict(kind="swa", n=n, h=h, tile=4 + pair, first=True, last=True))
    for u in units:
        n = u["n"]
        if u["kind"] == "cmp":
            u["width"], u["keys"] = NCMP, [(0, NCMP)]
        else:
            lo = max(n - 1, 0) if u["kind"] == "swa" else 0
            u["width"], u["keys"] = (n + 1 - lo) * P, [(j, P) for j in range(lo, n + 1)]
            u["lo"] = lo
    return units


L_RING = 4
PT_RING = 4
TURN_LAG, WEIGH_LAG, FINISH_LAG = 2, 4, 5


def phase_attention(kit):
    nc, bank, proj = kit.nc, kit.bank, kit.proj
    units = attention_units()
    NU = len(units)
    by_v = [i % 3 == 0 for i in range(NU)]
    n_v = [sum(by_v[:i + 1]) for i in range(NU)]
    n_a = [i + 1 - n_v[i] for i in range(NU)]
    n_swa = [sum(x["kind"] == "swa" for x in units[:i + 1]) for i in range(NU)]
    n_es = [sum(x.get("branch", 0) > 0 for x in units[:i + 1]) for i in range(NU)]
    rows = []
    for i, u in enumerate(units):
        if not rows or rows[-1][:2] != (u["tile"], u["n"]):
            rows.append((u["tile"], u["n"], i))
        rows[-1] = (u["tile"], u["n"], i)
    row_of = {i: r for r, (_, _, end) in enumerate(rows) for i in range((rows[r - 1][2] + 1) if r else 0, end + 1)}
    ends = {end: r for r, (_, _, end) in enumerate(rows)}
    with ExitStack() as ctx:
        def sb(name, shape):
            return ctx.enter_context(nc.sbuf_tensor(name, shape, F32))
        rings = kit.w1[:].rearrange("p (s t) -> p s t", t=T)
        assert L_RING + PT_RING <= 8
        lg, pt = rings[:, 0:L_RING, :], rings[:, L_RING:L_RING + PT_RING, :]
        orow = sb("orow", [P, 2, P])
        negm = sb("negm", [P, NU])
        tot = sb("tot", [P, NU])
        es = sb("es", [P, NU])
        inv = sb("inv", [P, NU])
        s = kit.sems("att", ("s_mm", "logits", "exps", "sinks", "inv_made", "dens", "turned", "pt_by_v", "pt_by_a",
                             "pv_mm", "out_read", "rows_turned", "mixed", "gated"))
        SB, TB, OB, XB = bank[0:3], bank[3:5], bank[5:7], bank[7]
        ident = kit.k1[:, K_ID:K_ID + P]
        block = ctx.enter_context(nc.Block())

        def logits(pe, u, out):
            t = slice(u["n"] * P, (u["n"] + 1) * P)
            if u["kind"] == "cmp":
                r = slice(HD * (u["h"] % 2), HD * (u["h"] % 2) + HD)
                return pe.matmul(out[:, 0:NCMP], proj[r, C_QA + u["h"] // 2, t], kit.kc[r, :], start=True, stop=True)
            if u["kind"] == "mla":
                return pe.matmul(out[:, 0:u["width"]], kit.qf[:, u["h"], t], kit.kf[:, u["h"], 0:u["width"]],
                                 start=True, stop=True)
            q = kit.q_swa(u["h"]) if u["kind"] == "swa" else kit.q_nsa(u["h"])
            w = max(u["width"], 2 * P)
            kt = slice(u["lo"] * P, u["lo"] * P + w)
            pe.matmul(out[:, 0:w], q[:, t], kit.k_hi(u["kind"])[:, kt], start=True, stop=False)
            return pe.matmul(out[:, 0:w], q[:, t], kit.k_lo(u["kind"])[:, kt], start=False, stop=True)

        def values(u, j):
            if u["kind"] == "cmp":
                return kit.vc[:, :], 0
            if u["kind"] == "mla":
                pair = u["h"] // 2
                return kit.mv[:, j, pair * P:(pair + 1) * P], HD * (u["h"] % 2)
            if u["kind"] == "swa":
                return kit.cv[:, j, :], 0
            return kit.vr[:, j, :], 0 if u["kind"] == "slc" else HD

        def bias(u):
            if u["kind"] == "cmp":
                return kit.biasK[:, u["h"], u["n"], :]
            if u["kind"] == "mla":
                return kit.k1[:, K_CAUSAL + T - u["width"]:K_CAUSAL + T]
            if u["kind"] == "swa":
                return kit.biasC[:, u["h"], 256 - u["width"]:256]
            return kit.biasA[:, u["h"], T - u["width"]:T]

        def wait_turned_copy(eng, i):
            if n_v[i]:
                eng.wait_ge(s["pt_by_v"], n_v[i])
            if n_a[i]:
                eng.wait_ge(s["pt_by_a"], n_a[i])

        def copy_shape(u):
            return (P if u["kind"] != "cmp" else NCMP), len(u["keys"]) * P

        @block.tensor
        def _(pe):
            for i in range(NU + FINISH_LAG + 2):
                if i < NU:
                    if i >= 3:
                        pe.wait_ge(s["logits"], i - 2)
                    logits(pe, units[i], SB[i % 3]).then_inc(s["s_mm"], 1)
                x = i - TURN_LAG
                if 0 <= x < NU:
                    u = units[x]
                    pe.wait_ge(s["exps"], x + 1)
                    if x >= 2:
                        wait_turned_copy(pe, x - 2)
                    w, _ = copy_shape(u)
                    for y in range(len(u["keys"])):
                        mm = pe.transpose(TB[x % 2][0:w, y * P:(y + 1) * P], lg[:, x % L_RING, y * P:y * P + w], ident)
                    mm.then_inc(s["turned"], 1)
                x = i - WEIGH_LAG
                if 0 <= x < NU:
                    u = units[x]
                    wait_turned_copy(pe, x)
                    if x >= 2:
                        pe.wait_ge(s["out_read"], x - 1)
                    w, _ = copy_shape(u)
                    for y, (j, _) in enumerate(u["keys"]):
                        mm = pe.matmul(OB[x % 2][:, 0:P], pt[0:w, x % PT_RING, y * P:(y + 1) * P], values(u, j)[0],
                                       start=y == 0, stop=y == len(u["keys"]) - 1)
                    mm.then_inc(s["pv_mm"], 1)
                x = i - FINISH_LAG - 1
                if x in ends:
                    tile, n, end = rows[ends[x]]
                    pe.wait_ge(s["out_read"], end + 1)
                    if tile >= 1:
                        pe.wait_ge(s["mixed"], tile)
                    pe.transpose(XB[:, n * P:(n + 1) * P], orow[:, ends[x] % 2, :], ident
                                 ).then_inc(s["rows_turned"], 1)

        @block.vector
        def _(v):
            for i in range(NU + FINISH_LAG + 2):
                if i < NU:
                    u = units[i]
                    v.wait_ge(s["s_mm"], i + 1)
                    if i >= L_RING:
                        v.wait_ge(s["turned"], i - L_RING + 1)
                    start = kit.nsink[:, u["h"]:u["h"] + 1] if u["kind"] == "swa" else 3e38
                    v.tensor_tensor_reduce(lg[:, i % L_RING, 0:u["width"]], SB[i % 3][:, 0:u["width"]], bias(u), -1.0,
                                           start, ALU.add, ALU.min, negm[:, i:i + 1]).then_inc(s["logits"], 1)
                x = i - TURN_LAG
                if 0 <= x < NU and by_v[x]:
                    w, m = copy_shape(units[x])
                    v.wait_ge(s["turned"], x + 1)
                    if x >= PT_RING:
                        v.wait_ge(s["pv_mm"], x - PT_RING + 1)
                    v.tensor_copy(pt[0:w, x % PT_RING, 0:m], TB[x % 2][0:w, 0:m]).then_inc(s["pt_by_v"], 1)
                x = i - FINISH_LAG
                if 0 <= x < NU:
                    u = units[x]
                    den = tot[:, x:x + 1]
                    v.wait_ge(s["exps"], x + 1)
                    if u["kind"] == "swa":
                        v.wait_ge(s["sinks"], n_swa[x])
                        v.tensor_tensor(den, den, es[:, x:x + 1], ALU.add).then_inc(s["dens"], 1)
                        v.wait_ge(s["dens"], n_swa[x])
                    v.reciprocal(inv[:, x:x + 1], den).then_inc(s["inv_made"], 1)
                    v.wait_ge(s["inv_made"], x + 1)
                    v.wait_ge(s["pv_mm"], x + 1)
                    at = values(u, 0)[1]
                    rows_in = OB[x % 2][:, at:at + HD]
                    r = row_of[x]
                    dst = orow[:, r % 2, HD * (u["h"] % 2):HD * (u["h"] % 2) + HD]
                    if r >= 2:
                        v.wait_ge(s["rows_turned"], r - 1)
                    if "branch" not in u:
                        v.tensor_scalar(dst, rows_in, inv[:, x:x + 1], None, ALU.mult).then_inc(s["out_read"], 1)
                    else:
                        b = u["h"] * 3 + u["branch"]
                        gate = kit.gate[:, u["n"], b:b + 1]
                        if u["branch"] == 0:
                            v.tensor_scalar(dst, rows_in, inv[:, x:x + 1], gate, ALU.mult, ALU.mult
                                            ).then_inc(s["out_read"], 1)
                        else:
                            v.tensor_tensor(es[:, x:x + 1], inv[:, x:x + 1], gate, ALU.mult).then_inc(s["gated"], 1)
                            v.wait_ge(s["gated"], n_es[x])
                            v.wait_ge(s["out_read"], x)
                            v.scalar_tensor_tensor(dst, rows_in, es[:, x:x + 1], dst, ALU.mult, ALU.add
                                                   ).then_inc(s["out_read"], 1)
                x = i - FINISH_LAG - 2
                if x in ends and rows[ends[x]][1] == NT - 1:
                    tile = rows[ends[x]][0]
                    v.wait_ge(s["rows_turned"], ends[x] + 1)
                    z = proj[:, C_Z + tile, :]
                    v.tensor_tensor(z, XB[:], z, ALU.mult).then_inc(s["mixed"], 1)
            last = NU - 1
            assert last in ends

        @block.scalar
        def _(a):
            for i in range(NU + TURN_LAG):
                if i < NU:
                    u = units[i]
                    a.wait_ge(s["logits"], i + 1)
                    row = lg[:, i % L_RING, 0:u["width"]]
                    a.activation(row, row, ACT.Exp, bias=negm[:, i:i + 1], scale=-1.0, accum_out=tot[:, i:i + 1]
                                 ).then_inc(s["exps"], 1)
                    if u["kind"] == "swa":
                        a.activation(es[:, i:i + 1], kit.s1[:, S_SINK + u["h"]:S_SINK + u["h"] + 1], ACT.Exp,
                                     bias=negm[:, i:i + 1]).then_inc(s["sinks"], 1)
                x = i - TURN_LAG
                if 0 <= x < NU and not by_v[x]:
                    w, m = copy_shape(units[x])
                    a.wait_ge(s["turned"], x + 1)
                    if x >= PT_RING:
                        a.wait_ge(s["pv_mm"], x - PT_RING + 1)
                    a.activation(pt[0:w, x % PT_RING, 0:m], TB[x % 2][0:w, 0:m], ACT.Copy).then_inc(s["pt_by_a"], 1)

        @block.gpsimd
        def _(g):
            kit.clear(g, "prep")



def phase_out1(kit, l):
    nc, d, bank = kit.nc, kit.d, kit.bank
    with ExitStack() as ctx:
        st = kit.stream
        st.allocate_parts(ctx, "out")
        y = ctx.enter_context(nc.sbuf_tensor("y1", [P, DC, T], F32))
        sq = ctx.enter_context(nc.sbuf_tensor("sq3", [P, 2, T], F32))
        acc = ctx.enter_context(nc.sbuf_tensor("acc3", [P, T], F32))
        lnv = ctx.enter_context(nc.sbuf_tensor("lnv3", [P, 2, T], F32))
        rs = ctx.enter_context(nc.sbuf_tensor("rs3", [P, T], F32))
        s = kit.sems("out1", OUT1_SEMS)
        block = ctx.enter_context(nc.Block())
        mixed = kit.proj[:, C_Z:C_Z + DC, :]
        base, last = st.base["w_out"], DC - 1

        @block.sync
        def _(sp):
            load_weights(sp, st, l, "w_out")

        @block.scalar
        def _(a):
            a.sem_inc(s["out_taken"], 2)
            for c in range(DC):
                a.activation(kit.xh[:, c, :], mixed[:, c, :], ACT.Copy).then_inc(s["xhi_made"], 1)
            for c in range(DC):
                a.wait_ge(st.mm_done, st.done_after(l, base + c))
                a.activation(y[:, c, :], bank[c % 2][:], ACT.Copy).then_inc(s["out_taken"], 1)
                if c >= 2:
                    a.wait_ge(s["sqsum_made"], max(1, c - 2))
                a.wait_ge(s["out_taken"], c + 3)
                a.activation(sq[:, c % 2, :], y[:, c, :], ACT.Square).then_inc(s["sq_made"], 1)
            a.dma_start(kit.gpre[:], d["gpre"][bass.ds(l + 1, 1)].rearrange("o p k -> (o p) k")).then_inc(s["gains"], 16)
            a.wait_ge(s["sq_summed"], 1)
            a.activation(lnv[:, 0, :], bank[2][:], ACT.Ln, bias=kit.eps[:, 0:1], scale=1.0 / D).then_inc(s["ln_made"], 1)
            a.wait_ge(s["ln_made"], 1)
            a.activation(rs[:], lnv[:, 0, :], ACT.Exp, scale=-0.5).then_inc(s["rstd_made"], 1)
            for c in range(DC):
                a.wait_ge(s["x_made"], c + 1)
                a.activation(y[:, c, :], kit.x[:, c, :], ACT.Square).then_inc(s["xsq_made"], 1)
            a.wait_ge(s["xsq_summed"], 1)
            a.activation(lnv[:, 1, :], bank[3][:], ACT.Ln, bias=kit.eps[:, 0:1], scale=1.0 / D).then_inc(s["ln_made"], 1)
            a.wait_ge(s["ln_made"], 2)
            a.activation(kit.xrstd[:], lnv[:, 1, :], ACT.Exp, scale=-0.5).then_inc(s["rstd_made"], 1)
            a.wait_ge(s["gains"], 16)

        @block.vector
        def _(v):
            for u in range(HL_RING):
                split_tile(v, st, l, base, 0, u, DC * P)
            split_rest(v, st, l, "w_out", DC)
            v.wait_ge(s["rstd_made"], 1)
            for c in range(DC):
                v.scalar_tensor_tensor(y[:, c, :], y[:, c, :], kit.s1[:, S_GPOST + c:S_GPOST + c + 1], rs[:],
                                       ALU.mult, ALU.mult).then_inc(s["scaled"], 1)
                v.wait_ge(s["scaled"], c + 1)
                v.tensor_tensor(kit.x[:, c, :], kit.x[:, c, :], y[:, c, :], ALU.add).then_inc(s["x_made"], 1)

        @block.tensor
        def _(pe):
            dense_on_arrival(pe, st, s, l, "w_out", DC, kit.xh, kit.xl, bank[0:2])
            dense_products(pe, st, s["out_taken"], l, "w_out", DC, kit.xh, kit.xl, bank[0:2], first=UNROLL)
            pe.wait_ge(s["sqsum_made"], last - 1)
            pe.matmul(bank[2][:], kit.ones[:], acc[:], start=True, stop=False)
            pe.wait_ge(s["sq_made"], DC)
            pe.matmul(bank[2][:], kit.ones[:], sq[:, last % 2, :], start=False, stop=True).then_inc(s["sq_summed"], 1)
            for c in range(DC):
                pe.wait_ge(s["xsq_made"], c + 1)
                mm = pe.matmul(bank[3][:], kit.ones[:], y[:, c, :], start=c == 0, stop=c == last)
            mm.then_inc(s["xsq_summed"], 1)

        @block.gpsimd
        def _(g):
            for c in range(DC):
                g.wait_ge(s["xhi_made"], c + 1)
                g.tensor_tensor(kit.xl[:, c, :], mixed[:, c, :], kit.xh[:, c, :].bitcast(F32), ALU.subtract
                                ).then_inc(s["xlo_made"], 1)
            kit.clear(g, "att")
            for c in range(1, last):
                g.wait_ge(s["sq_made"], c + 1)
                if c > 1:
                    g.wait_ge(s["sqsum_made"], c - 1)
                g.tensor_tensor(acc[:], sq[:, 0, :] if c == 1 else acc[:], sq[:, c % 2, :], ALU.add
                                ).then_inc(s["sqsum_made"], 1)


def phase_leave(kit, tags):
    st = kit.stream
    with kit.nc.Block() as block:
        @block.sync
        def _(sp):
            wait_stream_end(sp, st)
    with kit.nc.Block() as block:
        @block.gpsimd
        def _(g):
            for tag in tags:
                kit.clear(g, tag)
            for sem in st.w_loaded + [st.hi_made, st.w_split, st.mm_done]:
                g.sem_clear(sem)


def wait_stream_end(sp, st):
    for u in range(RAW_RING):
        sp.wait_ge(st.w_loaded[u], (DEPTH * st.per_layer // RAW_RING + 1) * 16)



MEAN, RSTD = 0, 1


def phase_enter2(kit):
    nc, d, st = kit.nc, kit.d, kit.stream
    s = kit.sems("enter2", ("loaded", "set"))
    with nc.Block() as block:
        @block.sync
        def _(sp):
            st.start(sp)
            sp.dma_start(kit.s2[:], d["s2"][0]).then_inc(s["loaded"], 16)
            sp.dma_start(kit.k2[:], d["k2"]).then_inc(s["loaded"], 16)
            sp.wait_ge(s["loaded"], 32)

        @block.tensor
        def _(pe):
            pe.sem_inc(st.mm_done, HL_RING)

        @block.vector
        def _(v):
            v.sem_inc(st.w_split, RAW_RING)
            v.memset(kit.ln[:, MEAN, :], 0.0).then_inc(s["set"], 1)
            v.memset(kit.ln[:, RSTD, :], 1.0).then_inc(s["set"], 1)
            for u in range(HL_RING):
                split_tile(v, st, 0, 0, 0, u, DC * P)


APPLY_SEMS = ("cent_made", "norm_made", "x_made", "xhi_made", "xlo_made")


def apply_vector(v, kit, s, which):
    x, g = kit.x, Q_LNG + which * DC
    for c in range(DC):
        v.tensor_tensor(x[:, c, :], x[:, c, :], kit.ln[:, MEAN, :], ALU.subtract).then_inc(s["cent_made"], 1)
        v.wait_ge(s["cent_made"], c + 1)
        v.scalar_tensor_tensor(x[:, c, :], x[:, c, :], kit.s2[:, g + c:g + c + 1], kit.ln[:, RSTD, :], ALU.mult, ALU.mult
                               ).then_inc(s["norm_made"], 1)


def apply_scalar(a, kit, s, which):
    x, b = kit.x, Q_LNB + which * DC
    for c in range(DC):
        a.wait_ge(s["norm_made"], c + 1)
        off = kit.s2[:, b + c:b + c + 1]
        a.activation(kit.xh[:, c, :], x[:, c, :], ACT.Identity, bias=off).then_inc(s["xhi_made"], 1)
        a.activation(x[:, c, :], x[:, c, :], ACT.Identity, bias=off).then_inc(s["x_made"], 1)


def apply_gpsimd(g, kit, s):
    for c in range(DC):
        g.wait_ge(s["x_made"], c + 1)
        g.tensor_tensor(kit.xl[:, c, :], kit.x[:, c, :], kit.xh[:, c, :].bitcast(F32), ALU.subtract
                        ).then_inc(s["xlo_made"], 1)



def phase_ffn_up(kit, l, tag, hh, hl, which):
    nc, d, bank = kit.nc, kit.d, kit.bank
    n, base = 2 * FC, kit.stream.base[tag]
    with ExitStack() as ctx:
        st = kit.stream
        sg = ctx.enter_context(nc.sbuf_tensor(f"{tag}_sg", [P, 2, T], F32))
        ub = ctx.enter_context(nc.sbuf_tensor(f"{tag}_ub", [P, 2, T], F32))
        hm = ctx.enter_context(nc.sbuf_tensor(f"{tag}_hm", [P, 2, T], F32))
        s = kit.sems("up", DENSE + APPLY_SEMS + ("h_made", "hhi_made", "hlo_made"))
        block = ctx.enter_context(nc.Block())

        @block.sync
        def _(sp):
            load_weights(sp, st, l, tag)

        @block.scalar
        def _(a):
            a.sem_inc(s["out_taken"], 2)
            apply_scalar(a, kit, s, which)
            with a.Fori(0, n // UNROLL) as j:
                for f in range(2):
                    a.wait_ge(st.mm_done, st.done_after(l, base + j * UNROLL + 2 * f))
                    a.activation(sg[:, f, :], bank[0][:], ACT.Silu).then_inc(s["out_taken"], 1)
                    a.wait_ge(st.mm_done, st.done_after(l, base + j * UNROLL + 2 * f + 1))
                    a.activation(ub[:, f, :], bank[1][:], ACT.Copy).then_inc(s["out_taken"], 1)
                    a.wait_ge(s["h_made"], j * 2 + f + 1)
                    a.activation(hh[:, bass.ds(j * 2 + f, 1), :].rearrange("p o t -> p (o t)"), hm[:, f, :], ACT.Copy
                                 ).then_inc(s["hhi_made"], 1)

        @block.gpsimd
        def _(g):
            kit.clear(g, "ln")
            apply_gpsimd(g, kit, s)
            with g.Fori(0, n // UNROLL) as j:
                for f in range(2):
                    g.wait_ge(s["out_taken"], j * UNROLL + 2 * f + 4)
                    g.tensor_tensor(hm[:, f, :], sg[:, f, :], ub[:, f, :], ALU.mult).then_inc(s["h_made"], 1)
                    g.wait_ge(s["hhi_made"], j * 2 + f + 1)
                    at = bass.ds(j * 2 + f, 1)
                    g.tensor_tensor(hl[:, at, :].rearrange("p o t -> p (o t)"), hm[:, f, :],
                                    hh[:, at, :].rearrange("p o t -> p (o t)").bitcast(F32), ALU.subtract
                                    ).then_inc(s["hlo_made"], 1)

        @block.vector
        def _(v):
            apply_vector(v, kit, s, which)
            split_ahead(v, st, l, tag, DC, KH)

        @block.tensor
        def _(pe):
            dense_on_arrival(pe, st, s, l, tag, DC, kit.xh, kit.xl, bank[0:2])
            dense_products(pe, st, s["out_taken"], l, tag, DC, kit.xh, kit.xl, bank[0:2], first=UNROLL)



def phase_dense_ln(kit, l, tag, cleared, xh, xl, kp, kp_next, pieces, scale, next_small=False):
    nc, d, bank, x = kit.nc, kit.d, kit.bank, kit.x
    n, base = DC * pieces, kit.stream.base[tag]
    last = DC - 1
    with ExitStack() as ctx:
        st = kit.stream
        sq = ctx.enter_context(nc.sbuf_tensor(f"{tag}_sq", [P, 2, T], F32))
        acc = ctx.enter_context(nc.sbuf_tensor(f"{tag}_acc", [P, 2, T], F32))
        c0 = ctx.enter_context(nc.sbuf_tensor(f"{tag}_c0", [P, T], F32))
        s = kit.sems("ln", LN_SEMS)
        block = ctx.enter_context(nc.Block())

        def shifted(c):
            return (2, 1)[c] if c < 2 else c + 1

        @block.sync
        def _(sp):
            load_weights(sp, st, l, tag)

        @block.gpsimd
        def _(g):
            kit.clear(g, cleared)
            for c in range(DC):
                g.tensor_scalar(x[:, c, :], x[:, c, :], ALPHA, None, ALU.mult).then_inc(s["alpha"], 1)

            def shift(c):
                g.tensor_tensor(x[:, c, :], x[:, c, :], c0[:], ALU.subtract).then_inc(s["shifted"], 1)
            g.wait_ge(s["alpha"], DC)
            g.wait_ge(s["c0_made"], 1)
            shift(1)
            shift(0)
            for c in range(1, last):
                shift(c + 1)
                g.wait_ge(s["out_taken"], c + 3)
                g.wait_ge(s["shifted"], max(2, shifted(c)))
                if c > 1:
                    g.wait_ge(s["sum_made"], c - 1)
                g.tensor_tensor(acc[:, 0, :], x[:, 0, :] if c == 1 else acc[:, 0, :], x[:, c, :], ALU.add
                                ).then_inc(s["sum_made"], 1)
                g.wait_ge(s["sq_made"], c + 1)
                if c > 1:
                    g.wait_ge(s["sqsum_made"], c - 1)
                g.tensor_tensor(acc[:, 1, :], sq[:, 0, :] if c == 1 else acc[:, 1, :], sq[:, c % 2, :], ALU.add
                                ).then_inc(s["sqsum_made"], 1)

        @block.scalar
        def _(a):
            if next_small:
                a.dma_start(kit.s2[:], d["s2"][bass.ds(l + 1, 1)].rearrange("o p k -> (o p) k")).then_inc(s["small"], 16)
            a.wait_ge(s["c0_mm"], 1)
            a.activation(c0[:], bank[2][:], ACT.Copy, scale=1.0 / P).then_inc(s["c0_made"], 1)
            for c in range(DC):
                if c == 0:
                    a.wait_ge(s["shifted"], shifted(0))
                else:
                    a.wait_ge(s["out_taken"], c + 3)
                if c >= 2:
                    a.wait_ge(s["sqsum_made"], max(1, c - 2))
                a.activation(sq[:, c % 2, :], x[:, c, :], ACT.Square).then_inc(s["sq_made"], 1)
            a.wait_ge(s["sum_mm"], 1)
            a.activation(c0[:], bank[2][:], ACT.Square, scale=1.0 / D).then_inc(s["meansq_made"], 1)
            a.activation(kit.ln[:, MEAN, :], bank[2][:], ACT.Copy, scale=1.0 / D).then_inc(s["mean_made"], 1)
            a.wait_ge(s["var_made"], 1)
            a.activation(c0[:], c0[:], ACT.Ln, bias=kit.eps[:, 1:2]).then_inc(s["ln_made"], 1)
            a.wait_ge(s["ln_made"], 1)
            a.activation(kit.ln[:, RSTD, :], c0[:], ACT.Exp, scale=-0.5).then_inc(s["rstd_made"], 1)
            if next_small:
                a.wait_ge(s["small"], 16)

        @block.vector
        def _(v):
            def split(i):
                split_tile(v, st, l, base, 0, i, (kp if i < n else kp_next) * P)

            for i in range(n):
                if i < n - 1:
                    split(i + HL_RING)
                if i % pieces == pieces - 1:
                    c = i // pieces
                    v.wait_ge(st.mm_done, st.done_after(l, base + i))
                    if c == 0:
                        v.wait_ge(s["alpha"], 1)
                    else:
                        v.wait_ge(s["shifted"], shifted(c))
                    v.scalar_tensor_tensor(x[:, c, :], bank[c % 2][:], scale, x[:, c, :], ALU.mult, ALU.add
                                           ).then_inc(s["out_taken"], 1)
            split(n + HL_RING - 1)
            v.wait_ge(s["sqsum_mm"], 1)
            v.wait_ge(s["meansq_made"], 1)
            v.scalar_tensor_tensor(c0[:], bank[3][:], 1.0 / D, c0[:], ALU.mult, ALU.subtract).then_inc(s["var_made"], 1)

        @block.tensor
        def _(pe):
            pe.sem_inc(s["out_taken"], 2)
            for u in range(UNROLL):
                dense_tile(pe, st, s["out_taken"], l, tag, kp, xh, xl, bank[0:2], pieces, 0, u)
                if u == pieces:
                    pe.wait_ge(s["out_taken"], 3)
                    pe.matmul(bank[2][:], kit.ones[:], x[:, 0, :], start=True, stop=True).then_inc(s["c0_mm"], 1)
            dense_products(pe, st, s["out_taken"], l, tag, kp, xh, xl, bank[0:2], pieces, first=UNROLL)
            pe.wait_ge(s["sum_made"], last - 1)
            pe.matmul(bank[2][:], kit.ones[:], acc[:, 0, :], start=True, stop=False)
            pe.wait_ge(s["sqsum_made"], last - 1)
            pe.matmul(bank[3][:], kit.ones[:], acc[:, 1, :], start=True, stop=False)
            pe.wait_ge(s["out_taken"], DC + 2)
            pe.matmul(bank[2][:], kit.ones[:], x[:, last, :], start=False, stop=True).then_inc(s["sum_mm"], 1)
            pe.wait_ge(s["sq_made"], DC)
            pe.matmul(bank[3][:], kit.ones[:], sq[:, last % 2, :], start=False, stop=True).then_inc(s["sqsum_mm"], 1)



LEVELS = (64, 32, 16, 8, 4, 2, 1)


def phase_mixers(kit, l, p2):
    nc, bank = kit.nc, kit.bank
    W = HH * T
    with ExitStack() as ctx:
        def sb(name, shape):
            return ctx.enter_context(nc.sbuf_tensor(name, shape, F32))
        bb = sb("bb", [P, W])
        kk = sb("kk", [P, W])
        df = sb("df", [P, 2, W])
        xx = sb("xx", [P, 2, W])
        vrow = sb("vrow", [P, NT, HH, P])
        v_place = p2[:, D_V:D_V + HH, :].rearrange("p h t -> p (h t)")
        at = v_place.rearrange("p (n h t) -> p n h t", n=NT, h=HH)
        pl = v_place[:, 0:2 * (PADT + T)].rearrange("p (s t) -> p s t", s=2)
        kd = p2[:, D_F:D_F + HH, :].rearrange("p h t -> p (h t)")
        kr = kd.rearrange("p (n h c) -> p n h c", n=NT, h=HH)
        qe = bb[:]
        ad, tm = (kit.ln[:, i, :].rearrange("p (a t) -> p a t", t=32) for i in range(2))
        sta = sb("sta", [P, 3, HH, P])
        el = sb("el", [P, NT * HH])
        lbv = sb("lbv", [P, 6, HH])
        ident = kit.k2[:, 0:P]
        st, base = kit.stream, kit.stream.base["w_in_2"]
        dense_banks = bank[6:8]
        k_banks = (bank[6], bank[7], bank[3])
        s = kit.sems("mix", DENSE + APPLY_SEMS + ("chain_v", "abs_f", "exp_f", "ln_f", "ls_made", "km_made", "k_made", "a_made", "m_made", "lb_in",
                             "lb_act", "lb_made", "e2", "e3", "e4", "b_made", "sub_made", "exp_made", "top_mm", "last_sub", "ke_exp", "sc_kept", "lv_made",
                             "lev_mm", "acc_made", "at_made", "v_turned", "v_kept", "qe_exp", "qe_made", "kd_made",
                             "k_turned", "k_kept", "kv_mm", "st_made", "o_mm", "o_kept", "osq_made", "o_summed",
                             "oln_made", "orstd_made", "y_made", "g_made", "u_pad", "pool_chain", "pooled", "p_mm",
                             "hi_made", "p_kept", "lo_made", "zeroed"))
        q = p2[:, D_Q:D_Q + HH, :].rearrange("p h t -> p (h t)")
        f = p2[:, D_F:D_F + HH, :].rearrange("p h t -> p (h t)")
        g_in = p2[:, D_G:D_G + HH, :].rearrange("p h t -> p (h t)")
        LNLB, LNOM, DIF = 3, 4, 5
        ot = xx[:, 0, :]
        osq = xx[:, 1, :]
        rst = df[:, 0, :]
        block = ctx.enter_context(nc.Block())

        def halves(ap, m):
            b = ap.rearrange("p (b m) -> p b m", m=2 * m)
            return b[:, :, 0:m], b[:, :, m:2 * m]

        def cols(h, n, a=0, b=P):
            return slice(h * T + n * P + a, h * T + n * P + b)

        @block.sync
        def _(sp):
            load_weights(sp, st, l, "w_in_2")

        @block.scalar
        def _(a):
            a.sem_inc(s["out_taken"], 2)
            a.wait_ge(s["lb_in"], 1)
            a.activation(lbv[:, 1, :], lbv[:, 0, :], ACT.Abs).then_inc(s["lb_act"], 1)
            a.wait_ge(s["lb_act"], 1)
            a.activation(lbv[:, 1, :], lbv[:, 1, :], ACT.Exp, scale=-1.0).then_inc(s["lb_act"], 1)
            apply_scalar(a, kit, s, 1)

            def level_exps(i):
                a.wait_ge(s["sub_made"], i + 1)
                left, right = halves(df[:, i % 2, :], LEVELS[i])
                a.activation(right, right, ACT.Exp).then_inc(s["exp_made"], 1)
                a.activation(left, left, ACT.Exp, scale=-1.0).then_inc(s["exp_made"], 1)

            for i in range(N_IN2):
                a.wait_ge(st.mm_done, st.done_after(l, base + i))
                a.activation(p2[:, i, :], dense_banks[i % 2][:], ACT.Copy,
                             scale=float(P) ** -0.5 if D_Q <= i < D_Q + HH else 1.0).then_inc(s["out_taken"], 1)
                if i == 3:
                    a.wait_ge(s["out_taken"], 2 + HH)
                    a.activation(df[:, 0, :], f, ACT.Abs).then_inc(s["abs_f"], 1)
                    a.wait_ge(s["abs_f"], 1)
                    a.activation(df[:, 0, :], df[:, 0, :], ACT.Exp, scale=-1.0).then_inc(s["exp_f"], 1)
                if i == 4:
                    a.wait_ge(s["lb_act"], 2)
                    a.activation(lbv[:, 1, :], lbv[:, 1, :], ACT.Ln, bias=kit.ones[:, 0:1]).then_inc(s["lb_act"], 1)
                    a.wait_ge(s["exp_f"], 1)
                    a.activation(df[:, 0, :], df[:, 0, :], ACT.Ln, bias=kit.ones[:, 0:1]).then_inc(s["ln_f"], 1)
                if i == 5:
                    a.wait_ge(s["lb_made"], 1)
                    a.wait_ge(s["ls_made"], 1)
                    for h in range(HH):
                        a.activation(df[:, 1, h * T:(h + 1) * T], xx[:, 0, h * T:(h + 1) * T], ACT.Abs,
                                     bias=lbv[:, DIF, h:h + 1]).then_inc(s["e2"], 1)
                if i == 6:
                    a.wait_ge(s["e2"], HH)
                    a.activation(df[:, 1, :], df[:, 1, :], ACT.Exp, scale=-1.0).then_inc(s["e3"], 1)
                if i == 7:
                    a.wait_ge(s["km_made"], 1)
                    for h in range(HH):
                        a.activation(kk[:, h * T:(h + 1) * T], xx[:, 1, h * T:(h + 1) * T], ACT.Exp,
                                     bias=lbv[:, LNOM, h:h + 1]).then_inc(s["k_made"], 1)
                if i == 8:
                    a.wait_ge(s["e3"], 1)
                    a.activation(df[:, 1, :], df[:, 1, :], ACT.Ln, bias=kit.ones[:, 0:1]).then_inc(s["e4"], 1)
                if i == 12:
                    level_exps(0)
                    for n in range(NT):
                        a.wait_ge(s["v_turned"], n + 1)
                        a.activation(vrow[:, n, :, :], bank[n][:].rearrange("p (h c) -> p h c", h=HH), ACT.Copy
                                     ).then_inc(s["v_kept"], 1)
                if i == 13:
                    level_exps(1)
                if i == 14:
                    a.wait_ge(s["last_sub"], 1)
                    a.activation(v_place, v_place, ACT.Exp).then_inc(s["ke_exp"], 1)
                    a.activation(el[:], bb[:, P - 1:W:P], ACT.Exp).then_inc(s["ke_exp"], 1)
                if i == 15:
                    level_exps(2)
                if i == 17:
                    level_exps(3)
                if i == 19:
                    level_exps(4)
            for c in range(HH):
                a.wait_ge(s["p_mm"], c + 1)
                a.activation(p2[:, D_U + c, :], bank[4 + c % 2][:], ACT.Copy, scale=kit.s2[:, Q_PS + c:Q_PS + c + 1]
                             ).then_inc(s["p_kept"], 1)
            level_exps(5)
            a.wait_ge(s["zeroed"], 2)
            for n in range(NT):
                a.wait_ge(s["top_mm"], NT + n + 1)
                top = bank[n][:].rearrange("p (h t) -> p h t", h=HH)
                a.activation(at[0:64, n, :, 64:128], top[0:64, :, 64:128], ACT.Copy).then_inc(s["at_made"], 1)
                a.activation(at[0:32, n, :, 32:64], top[0:32, :, 32:64], ACT.Copy).then_inc(s["at_made"], 1)
                a.activation(at[64:96, n, :, 96:128], top[64:96, :, 96:128], ACT.Copy).then_inc(s["at_made"], 1)
            level_exps(6)
            a.activation(qe, bb[:], ACT.Exp).then_inc(s["qe_exp"], 1)
            a.wait_ge(s["k_turned"], NT - 1)
            for n in range(NT - 1):
                a.activation(kr[:, n, :, :], k_banks[n][:].rearrange("p (h c) -> p h c", h=HH), ACT.Copy
                             ).then_inc(s["k_kept"], 1)
            for c in range(HH):
                a.wait_ge(s["p_kept"], c + 1)
                a.activation(kit.xh[:, c, :], p2[:, D_U + c, :], ACT.Copy).then_inc(s["hi_made"], 1)
            a.wait_ge(s["out_taken"], 2 + N_IN2)
            a.activation(g_in, g_in, ACT.Silu).then_inc(s["g_made"], 1)
            for h in range(HH):
                a.wait_ge(s["o_mm"], h + 1)
                a.activation(osq[:, h * T:(h + 1) * T], bank[h][:], ACT.Square).then_inc(s["osq_made"], 1)
            for h in range(HH):
                a.wait_ge(s["o_summed"], h + 1)
                a.activation(rst[:, h * T:(h + 1) * T], bank[4 + h][:], ACT.Ln, bias=kit.eps[:, 0:1], scale=1.0 / P
                             ).then_inc(s["oln_made"], 1)
            for h in range(HH):
                a.wait_ge(s["oln_made"], h + 1)
                a.activation(rst[:, h * T:(h + 1) * T], rst[:, h * T:(h + 1) * T], ACT.Exp, scale=-0.5
                             ).then_inc(s["orstd_made"], 1)
            for c in range(HH):
                a.wait_ge(s["y_made"], c + 1)
                a.activation(kit.xh[:, HH + c, :], ot[:, c * T:(c + 1) * T], ACT.Copy).then_inc(s["hi_made"], 1)

        @block.vector
        def _(v):
            lb = kit.s2[:, Q_LB:Q_LB + 2 * HH].rearrange("p (l h) -> p l h", l=2)
            v.tensor_tensor(lbv[:, 0, :], lb[:, 1, :], lb[:, 0, :], ALU.subtract).then_inc(s["lb_in"], 1)
            apply_vector(v, kit, s, 1)

            def sub(i):
                m = LEVELS[i]
                if i >= 2:
                    v.wait_ge(s["lv_made"], 2 * (i - 1))
                b3 = bb[:].rearrange("p (b m) -> p b m", m=2 * m)
                v.tensor_tensor(df[:, i % 2, :].rearrange("p (b m) -> p b m", m=2 * m), b3,
                                b3[:, :, m - 1:m].to_broadcast([P, W // (2 * m), 2 * m]), ALU.subtract
                                ).then_inc(s["sub_made"], 1)

            def level(i):
                m = LEVELS[i]
                v.wait_ge(s["exp_made"], 2 * i + 2)
                if i == 2:
                    v.wait_ge(s["top_mm"], NT)
                if i == 3:
                    v.wait_ge(s["top_mm"], 2 * NT)
                if i >= 4:
                    v.wait_ge(s["lev_mm"], i - 3)
                el_, er_ = halves(df[:, i % 2, :], m)
                kl_, _ = halves(kk[:], m)
                _, qr_ = halves(q, m)
                xl_, xr_ = halves(xx[:, i % 2, :], m)
                v.tensor_tensor(xl_, el_, kl_, ALU.mult).then_inc(s["lv_made"], 1)
                v.tensor_tensor(xr_, er_, qr_, ALU.mult).then_inc(s["lv_made"], 1)

            def accumulate(i):
                v.wait_ge(s["lev_mm"], i + 1)
                mask = kit.k2[:, M_MASK + 32 * i:M_MASK + 32 * i + 32].unsqueeze(1).to_broadcast([P, NT * HH, 32])
                lev = bank[4 + i % 2][:].rearrange("p (a t) -> p a t", t=32)
                if i == 0:
                    v.tensor_tensor(ad, lev, mask, ALU.mult).then_inc(s["acc_made"], 1)
                else:
                    v.tensor_tensor(tm, lev, mask, ALU.mult).then_inc(s["acc_made"], 1)
                    v.wait_ge(s["acc_made"], 2 * i)
                    v.tensor_tensor(ad, ad, tm, ALU.add).then_inc(s["acc_made"], 1)
                    v.wait_ge(s["acc_made"], 2 * i + 1)

            for i in range(N_IN2):
                split_tile(v, st, l, base + HL_RING, 0, i, DC * P)
                if i == 5:
                    v.wait_ge(s["lb_act"], 3)
                    link = linker(v, s["chain_v"])
                    link(v.scalar_tensor_tensor(lbv[:, 2, :], lbv[:, 0, :], 0.0, lbv[:, 1, :], ALU.min, ALU.subtract))
                    link(v.tensor_tensor(lbv[:, LNOM, :], lbv[:, 2, :], lbv[:, 0, :], ALU.subtract))
                    link(v.tensor_scalar(lbv[:, LNLB, :], lbv[:, 2, :], kit.s2[:, Q_FIRST:Q_FIRST + 1], None, ALU.add))
                    link(v.tensor_scalar(lbv[:, LNOM, :], lbv[:, LNOM, :], kit.s2[:, Q_NOTFIRST:Q_NOTFIRST + 1], None,
                                         ALU.mult))
                    v.tensor_tensor(lbv[:, DIF, :], lbv[:, LNOM, :], lbv[:, LNLB, :], ALU.subtract
                                    ).then_inc(s["lb_made"], 1)
                    v.wait_ge(s["ln_f"], 1)
                    v.scalar_tensor_tensor(xx[:, 0, :], f, 0.0, df[:, 0, :], ALU.min, ALU.subtract
                                           ).then_inc(s["ls_made"], 1)
                if i == 6:
                    v.wait_ge(s["ls_made"], 1)
                    v.tensor_tensor(xx[:, 1, :], xx[:, 0, :], f, ALU.subtract).then_inc(s["km_made"], 1)
                if i == 7:
                    v.wait_ge(s["lb_made"], 1)
                    for h in range(HH):
                        v.tensor_scalar(df[:, 0, h * T:(h + 1) * T], xx[:, 0, h * T:(h + 1) * T], lbv[:, LNOM, h:h + 1],
                                        lbv[:, LNLB, h:h + 1], ALU.add, ALU.max).then_inc(s["m_made"], 1)
                if i == 9:
                    v.wait_ge(s["m_made"], HH)
                    v.wait_ge(s["e4"], 1)
                    v.tensor_tensor(df[:, 0, :], df[:, 0, :], df[:, 1, :], ALU.add).then_inc(s["a_made"], 1)
                if i == 10:
                    v.wait_ge(s["a_made"], 1)
                    for h in range(HH):
                        for n in range(NT):
                            v.tensor_tensor_scan(bb[:, cols(h, n)], kit.ones[:], df[:, 0, cols(h, n)], 0.0,
                                                 ALU.mult, ALU.add).then_inc(s["b_made"], 1)
                if i == 11:
                    v.wait_ge(s["b_made"], HH * NT)
                    v.wait_ge(s["k_made"], HH)
                    sub(0)
                if i == 12:
                    sub(1)
                if i == 13:
                    v.wait_ge(s["out_taken"], 2 + D_Q + HH)
                    level(0)
                if i == 14:
                    sub(2)
                if i == 15:
                    level(1)
                if i == 16:
                    sub(3)
                if i == 17:
                    level(2)
                if i == 18:
                    sub(4)
                if i == 19:
                    level(3)
            sub(5)
            level(4)
            accumulate(0)
            sub(6)
            level(5)
            accumulate(1)
            level(6)
            accumulate(2)
            accumulate(3)
            v.wait_ge(s["kv_mm"], 1)
            v.tensor_copy(sta[:, 0, :, :], bank[0][:].rearrange("p (h c) -> p h c", h=HH)).then_inc(s["st_made"], 1)
            count = 1
            for n in (1, 2):
                v.wait_ge(s["kv_mm"], n + 1)
                v.wait_ge(s["st_made"], count)
                for h in range(HH):
                    v.scalar_tensor_tensor(sta[:, n, h, :], sta[:, n - 1, h, :], el[:, h * NT + n:h * NT + n + 1],
                                           bank[n][:, h * P:(h + 1) * P], ALU.mult, ALU.add
                                           ).then_inc(s["st_made"], 1)
                    count += 1
            accumulate(4)
            accumulate(5)
            v.wait_ge(s["zeroed"], 2)
            for b in range(4):
                r = slice(32 * b, 32 * b + 32)
                v.tensor_copy(at[r].rearrange("p n h t -> p (n h) t")[:, :, r], ad[r]).then_inc(s["at_made"], 1)
            v.wait_ge(s["g_made"], 1)
            for h in range(HH):
                seg = slice(h * T, (h + 1) * T)
                v.wait_ge(s["osq_made"], h + 1)
                v.tensor_tensor(ot[:, seg], bank[h][:], g_in[:, seg], ALU.mult).then_inc(s["o_kept"], 1)
            for h in range(HH):
                seg = slice(h * T, (h + 1) * T)
                v.wait_ge(s["orstd_made"], h + 1)
                v.wait_ge(s["o_kept"], h + 1)
                v.scalar_tensor_tensor(ot[:, seg], ot[:, seg], kit.s2[:, Q_HG:Q_HG + 1], rst[:, seg], ALU.mult, ALU.mult
                                       ).then_inc(s["y_made"], 1)
            for c in range(HH, DC):
                v.wait_ge(s["hi_made"], c + 1)
                v.tensor_tensor(kit.xl[:, c, :], ot[:, (c - HH) * T:(c - HH + 1) * T], kit.xh[:, c, :].bitcast(F32),
                                ALU.subtract).then_inc(s["lo_made"], 1)

        @block.tensor
        def _(pe):
            def dense(i):
                dense_tile(pe, st, s["out_taken"], l, "w_in_2", DC, kit.xh, kit.xl, dense_banks, 1, i // UNROLL, i % UNROLL)

            def top_level(i):
                m = LEVELS[i]
                pe.wait_ge(s["lv_made"], 2 * i + 2)
                for n in range(NT):
                    for h in range(HH):
                        for a0 in range(0, P, 2 * m):
                            mm = pe.matmul(bank[n][a0:a0 + m, h * P + a0 + m:h * P + a0 + 2 * m],
                                           xx[:, i % 2, cols(h, n, a0, a0 + m)], xx[:, i % 2, cols(h, n, a0 + m, a0 + 2 * m)],
                                           start=True, stop=True)
                    mm.then_inc(s["top_mm"], 1)

            def masked_level(i):
                if i < len(MASKED) - 1:
                    pe.wait_ge(s["lv_made"], 2 * (i + 3))
                if i >= 2:
                    pe.wait_ge(s["acc_made"], 2 * i - 3)
                for n in range(NT):
                    for h in range(HH):
                        for b in range(4):
                            c = cols(h, n, 32 * b, 32 * b + 32)
                            if i < len(MASKED) - 1:
                                lhs = rhs = xx[:, i % 2, c]
                            else:
                                lhs, rhs = kk[:, c], q[:, c]
                            at0 = (n * HH + h) * 32
                            mm = pe.matmul(bank[4 + i % 2][32 * b:32 * b + 32, at0:at0 + 32], lhs, rhs, start=True, stop=True)
                mm.then_inc(s["lev_mm"], 1)

            def pool_product(c):
                pe.wait_ge(s["pooled"], c + 1)
                if c >= 2:
                    pe.wait_ge(s["p_kept"], c - 1)
                pe.matmul(bank[4 + c % 2][:], kit.s2[:, Q_PW + c * P:Q_PW + (c + 1) * P], p2[:, D_U + c, :],
                          start=True, stop=True).then_inc(s["p_mm"], 1)

            dense_on_arrival(pe, st, s, l, "w_in_2", DC, kit.xh, kit.xl, dense_banks)
            dense_products(pe, st, s["out_taken"], l, "w_in_2", DC, kit.xh, kit.xl, dense_banks, first=D_Q, last=D_U)
            dense(D_U)
            pe.wait_ge(s["out_taken"], 2 + D_V + HH)
            for n in range(NT):
                for h in range(HH):
                    mm = pe.transpose(bank[n][:, h * P:(h + 1) * P], p2[:, D_V + h, n * P:(n + 1) * P], ident)
                mm.then_inc(s["v_turned"], 1)
            for i in range(D_U + 1, D_G):
                dense(i)
            pe.wait_ge(s["v_kept"], NT)
            top_level(0)
            dense(D_G)
            dense(D_G + 1)
            top_level(1)
            dense(D_G + 2)
            dense(D_G + 3)
            for c in range(HH):
                pool_product(c)
            pe.wait_ge(s["p_kept"], HH)
            masked_level(0)
            masked_level(1)
            pe.wait_ge(s["kd_made"], 1)
            pe.wait_ge(s["out_taken"], 2 + N_IN2)
            pe.wait_ge(s["at_made"], 3 * NT)
            for n in range(NT - 1):
                for h in range(HH):
                    mm = pe.transpose(k_banks[n][:, h * P:(h + 1) * P], kd[:, cols(h, n)], ident)
                mm.then_inc(s["k_turned"], 1)
            masked_level(2)
            masked_level(3)
            for n in range(NT - 1):
                pe.wait_ge(s["k_kept"], n + 1)
                for h in range(HH):
                    mm = pe.matmul(bank[n][:, h * P:(h + 1) * P], kr[:, n, h, :], vrow[:, n, h, :],
                                   start=True, stop=True)
                mm.then_inc(s["kv_mm"], 1)
            masked_level(4)
            masked_level(5)
            pe.wait_ge(s["st_made"], 1 + 2 * HH)
            pe.wait_ge(s["qe_made"], 1)
            pe.wait_ge(s["at_made"], 3 * NT + 4)
            for h in range(HH):
                for n in range(NT):
                    out = bank[h][:, n * P:(n + 1) * P]
                    mm = pe.matmul(out, vrow[:, n, h, :], at[:, n, h, :], start=True, stop=n == 0)
                    if n:
                        mm = pe.matmul(out, sta[:, n - 1, h, :], qe[:, cols(h, n)], start=False, stop=True)
                mm.then_inc(s["o_mm"], 1)
                if h:
                    pe.wait_ge(s["osq_made"], h)
                    pe.matmul(bank[4 + h - 1][:], kit.ones[:], osq[:, (h - 1) * T:h * T], start=True, stop=True
                              ).then_inc(s["o_summed"], 1)
            pe.wait_ge(s["osq_made"], HH)
            pe.matmul(bank[4 + HH - 1][:], kit.ones[:], osq[:, (HH - 1) * T:HH * T], start=True, stop=True
                      ).then_inc(s["o_summed"], 1)

        @block.gpsimd
        def _(g):
            kit.clear(g, "ln")
            apply_gpsimd(g, kit, s)
            g.wait_ge(s["b_made"], HH * NT)
            g.wait_ge(s["v_turned"], NT)
            b3 = bb[:].rearrange("p (b m) -> p b m", m=P)
            g.tensor_tensor(v_place.rearrange("p (b m) -> p b m", m=P),
                            b3[:, :, P - 1:P].to_broadcast([P, NT * HH, P]), b3, ALU.subtract).then_inc(s["last_sub"], 1)
            g.wait_ge(s["ke_exp"], 1)
            g.tensor_tensor(kd, kk[:], v_place, ALU.mult).then_inc(s["kd_made"], 1)
            link = linker(g, s["pool_chain"])
            g.wait_ge(s["kd_made"], 1)
            link(g.memset(pl[:, :, 0:PADT], 0.0))
            for i, w in enumerate(POOL_WINDOWS):
                u = p2[:, D_U + i, :]
                g.wait_ge(s["out_taken"], 2 + D_U + i + 1)
                link(g.tensor_tensor(pl[:, 0, PADT + 1:], u[:, 1:], u[:, :T - 1], ALU.add))
                link(g.tensor_copy(pl[:, 0, PADT:PADT + 1], u[:, 0:1]))
                for j in range(1, i + 1):
                    a_, b_ = pl[:, (j - 1) % 2, :], pl[:, j % 2, :]
                    link(g.tensor_tensor(b_[:, PADT:], a_[:, PADT:], a_[:, PADT - 2 ** j:PADT + T - 2 ** j], ALU.add))
                m = pl[:, i % 2, PADT:]
                link(g.tensor_scalar(m[:, PADT:], m[:, PADT:], 1.0 / w, None, ALU.mult))
                link(g.tensor_tensor(m[:, :PADT], m[:, :PADT], kit.k2[:, M_INV + i * PADT:M_INV + (i + 1) * PADT], ALU.mult))
                g.tensor_tensor(u, m, u, ALU.subtract).then_inc(s["pooled"], 1)
                g.wait_ge(s["pooled"], i + 1)
            g.memset(at[:, 0:2, :, :], 0.0).then_inc(s["zeroed"], 1)
            g.memset(at[:, 2:4, :, :], 0.0).then_inc(s["zeroed"], 1)
            g.wait_ge(s["qe_exp"], 1)
            g.tensor_tensor(qe, qe, q, ALU.mult).then_inc(s["qe_made"], 1)
            for c in range(HH):
                g.wait_ge(s["hi_made"], c + 1)
                g.tensor_tensor(kit.xl[:, c, :], p2[:, D_U + c, :], kit.xh[:, c, :].bitcast(F32), ALU.subtract
                                ).then_inc(s["lo_made"], 1)



def phase_store(kit):
    nc, d = kit.nc, kit.d
    s = kit.sems("store", APPLY_SEMS + ("stored",))
    with nc.Block() as block:
        @block.vector
        def _(v):
            apply_vector(v, kit, s, 0)

        @block.scalar
        def _(a):
            for c in range(DC):
                a.wait_ge(s["norm_made"], c + 1)
                a.activation(kit.x[:, c, :], kit.x[:, c, :], ACT.Identity, bias=kit.s2[:, Q_LNB + c:Q_LNB + c + 1]
                             ).then_inc(s["x_made"], 1)

        @block.sync
        def _(sp):
            for c in range(0, DC, 2):
                sp.wait_ge(s["x_made"], c + 2)
                sp.dma_start(d["out"][:, c:c + 2, :], kit.x[:, c:c + 2, :]).then_inc(s["stored"], 16)
            wait_stream_end(sp, kit.stream)
            sp.wait_ge(s["stored"], 16 * DC // 2)


def phase_store_plain(kit):
    s = kit.sems("store", ("stored",))
    with kit.nc.Block() as block:
        @block.sync
        def _(sp):
            sp.dma_start(kit.d["out"], kit.x[:]).then_inc(s["stored"], 16)
            sp.wait_ge(s["stored"], 16)


def hybrid_kernel(nc, dram, stop=None):
    ctx = ExitStack()
    with ctx:
        kit = Kit(nc, ctx, dram)

        def sb(c, name, shape, dt=F32):
            return c.enter_context(nc.sbuf_tensor(name, shape, dt))

        kit.bank = [ctx.enter_context(nc.psum_tensor(f"bank{i}", [P, T], F32)) for i in range(8)]
        kit.x = sb(ctx, "x", [P, DC, T])
        kit.xh = sb(ctx, "xh", [P, DC, T], F32R)
        kit.xl = sb(ctx, "xl", [P, DC, T], F32R)
        kit.ones = sb(ctx, "ones", [P, P])
        kit.eps = sb(ctx, "eps", [P, 2])
        with ExitStack() as c1:
            kit.sem_ctx = c1
            kit.stream = Stream(nc, c1, "one", (("w_in", N_IN), ("w_out", DC)), dram, DC * P)
            kit.k1 = sb(c1, "k1", [P, N_K1])
            kit.biasA = sb(c1, "biasA", [P, A_HEADS, T])
            kit.biasK = sb(c1, "biasK", [P, A_HEADS, NT, NCMP])
            kit.biasC = sb(c1, "biasC", [P, C_HEADS, 256])
            kit.gpre = sb(c1, "gpre", [P, DC])
            kit.xrstd = sb(c1, "xrstd", [P, T])
            phase_start(kit)
            kit.s1 = sb(c1, "s1", [P, N_S1])
            kit.proj = sb(c1, "proj", [P, N_IN, T])
            kit.sems("out1", OUT1_SEMS)
            with nc.Fori(0, DEPTH) as l:
                with ExitStack() as cw:
                    kit.w1 = sb(cw, "w1", [P, CMP_LEN * P])
                    phase_project1(kit, l)
                    with ExitStack() as c2:
                        kit.qf = sb(c2, "qf", [96, B_HEADS, T])
                        kit.kf = sb(c2, "kf", [96, B_HEADS, T])
                        kit.vr = sb(c2, "vr", [P, NT, P])
                        kit.cv = sb(c2, "cv", [P, NT, P])
                        kit.k2c = sb(c2, "k2c", [P, 2, T], F32R)
                        kit.mv = sb(c2, "mv", [P, NT, B_HEADS * HD])
                        kit.kc = sb(c2, "kc", [P, NCMP])
                        kit.vc = sb(c2, "vc", [NCMP, P])
                        kit.gate = sb(c2, "gate", [P, NT, 12])
                        kit.nsink = sb(c2, "nsink", [P, C_HEADS])
                        phase_prepare(kit)
                        phase_attention(kit)
                phase_out1(kit, l)
            phase_leave(kit, ("start", "out1"))
        kit.sem_ctx = ctx
        if stop == "block1":
            phase_store_plain(kit)
            return
        with ExitStack() as c1:
            kit.stream = Stream(nc, c1, "two", (("up1", 2 * FC), ("down1", 2 * DC), ("w_in_2", N_IN2), ("w_out_2", DC),
                                                ("up2", 2 * FC), ("down2", 2 * DC)), dram, KH * P)
            kit.k2 = sb(c1, "k2", [P, N_K2])
            kit.s2 = sb(c1, "s2", [P, N_S2])
            kit.ln = sb(c1, "ln", [P, 2, T])
            kit.stream.allocate_parts(c1)
            phase_enter2(kit)
            kit.sems("ln", LN_SEMS)
            with nc.Fori(0, DEPTH) as l:
                with ExitStack() as c2:
                    hh = sb(c2, "hh1", [P, FC, T], F32R)
                    hl = sb(c2, "hl1", [P, FC, T], F32R)
                    phase_ffn_up(kit, l, "up1", hh, hl, 0)
                    phase_dense_ln(kit, l, "down1", "up", hh, hl, KH, DC, 2, 0.5)
                with ExitStack() as c2:
                    p2 = sb(c2, "p2", [P, N_IN2, T])
                    phase_mixers(kit, l, p2)
                phase_dense_ln(kit, l, "w_out_2", "mix", kit.xh, kit.xl, DC, DC, 1, 1.0)
                with ExitStack() as c2:
                    hh = sb(c2, "hh2", [P, FC, T], F32R)
                    hl = sb(c2, "hl2", [P, FC, T], F32R)
                    phase_ffn_up(kit, l, "up2", hh, hl, 2)
                    phase_dense_ln(kit, l, "down2", "up", hh, hl, KH, DC, 2, 0.5, next_small=True)
        phase_store(kit)



def in_columns():
    sizes = (A_HEADS * HD, 6 * HD, 3 * A_HEADS, 256, 128, ROPE, C_HEADS * HD, 2 * HD, D)
    o = np.concatenate([[0], np.cumsum(sizes)])
    r = lambda a, n: np.arange(a, a + n)
    pad = lambda n: np.full(n, -1)
    kv = [r(o[1] + i * HD, HD) for i in range(6)]
    kr = r(o[5], ROPE)
    swapped = np.concatenate([kr[ROPE // 2:], kr[:ROPE // 2]])
    ck, cv = r(o[7], HD), r(o[7] + HD, HD)
    parts = [r(o[0], 256), kv[2], kv[2], kv[4], kv[4], kv[3], kv[5], kv[0], kv[1], r(o[3], 256), r(o[4], 128),
             cv, kr, swapped, r(o[6], 512), ck, ck, r(o[2], 12), pad(P - 12), r(o[8], D)]
    cols = np.concatenate(parts)
    assert cols.size == N_IN * P
    return cols


def in2_columns():
    w = HH * P
    return np.concatenate([np.arange(i * w, (i + 1) * w) for i in (2, 1, 3, 0, 4)])


def uq_columns():
    out = []
    for h in range(B_HEADS):
        c = np.arange(h * (HD + ROPE), (h + 1) * (HD + ROPE))
        out += [c, c[HD + ROPE // 2:], c[HD:HD + ROPE // 2]]
    return np.concatenate(out)


def bucket(dist):
    dist = np.maximum(dist, 0)
    exact = BKT // 2
    large = exact + (np.log(np.maximum(dist, 1).astype(np.float32) / np.float32(exact))
                     / np.float32(math.log(T / exact)) * np.float32(BKT - exact)).astype(np.int32)
    return np.where(dist < exact, dist, np.minimum(large, BKT - 1))


def shape_constants():
    f32 = np.float32
    p = np.arange(P)
    k1 = np.zeros((P, N_K1), f32)
    k1[:, K_ID:K_ID + P] = np.eye(P)
    k1[:, K_EX:K_EX + P] = np.eye(P)[::-1]
    half = ROPE // 2
    inv = f32(10000.0) ** (-np.arange(half, dtype=f32) / f32(half))
    ang = np.arange(T, dtype=f32)[None, :] * inv[:, None]
    cos, sin = np.cos(ang), np.sin(ang)
    k1[64:96, K_TRIG:K_TRIG + T] = np.concatenate([cos, cos])
    k1[96:128, K_TRIG:K_TRIG + T] = np.concatenate([-sin, sin])
    k1[:, K_CAUSAL:K_CAUSAL + T] = np.where(T - P + p[:, None] - np.arange(T)[None, :] < 0, NEG, 0)
    k1[:, K_ROWOK] = p >= CMP_LEN - 1
    dist = T - 1 - np.arange(2 * T)
    hot = (bucket(dist)[None, :] == np.arange(BKT)[:, None]).astype(f32)
    msk = np.zeros((A_HEADS + C_HEADS, 2 * T), f32)
    msk[:, dist < 0] = NEG
    msk[A_HEADS:, dist >= SWA_WINDOW] = NEG
    k2 = np.zeros((P, N_K2), f32)
    k2[:, 0:P] = np.eye(P)
    for i, m in enumerate(MASKED):
        a, b = (p % 32)[:, None], np.arange(32)[None, :]
        ok = (a == b) if m == 0 else (a // (2 * m) == b // (2 * m)) & (a % (2 * m) < m) & (b % (2 * m) >= m)
        k2[:, M_MASK + 32 * i:M_MASK + 32 * i + 32] = ok
    for i, w in enumerate(POOL_WINDOWS):
        k2[:, M_INV + i * PADT:M_INV + (i + 1) * PADT] = f32(1) / np.minimum(np.arange(PADT) + 1, w).astype(f32)[None, :]
    flags = np.zeros((DEPTH, P, 2), f32)
    flags[0, :, 0] = NEG
    flags[1:, :, 1] = 1
    return k1, k2, hot, msk, flags


def tiles(w, kp=DC):
    n, k, m = w.shape
    return np.ascontiguousarray(w.reshape(n, k // (kp * P), kp, P, m // P, P).transpose(0, 4, 1, 3, 2, 5)
                                ).reshape(-1, P, kp * P)


def by_partition(v):
    return v.reshape(v.shape[0], -1, P).transpose(0, 2, 1)


def layouts(i):
    k1, k2, hot, msk, flags = shape_constants()
    L = DEPTH
    w_in = np.concatenate([i["w_in"], np.zeros((L, D, 1), np.float32)], axis=2)[:, :, in_columns()]
    pe = i["cmp_pos"].transpose(0, 1, 3, 2).reshape(L, P, CMP_LEN)
    uq = i["mla_w_uq"][:, :, uq_columns()].reshape(L, 2, P, B_HEADS * P).transpose(0, 2, 1, 3).reshape(L, P, -1)
    ukv = i["mla_w_ukv"].reshape(L, P, B_HEADS, 2, HD)
    w2 = i["cmp_w2"]
    s1 = np.concatenate([
        by_partition(i["norm_post"]), by_partition(i["mla_q_norm"]),
        by_partition(i["mla_kv_norm"]), np.broadcast_to(i["swa_sinks"][:, None, :], (L, P, C_HEADS)), pe, uq,
        ukv[:, :, :, 0].reshape(L, P, -1), ukv[:, :, :, 1].reshape(L, P, -1), w2[:, 0], w2[:, 0], w2[:, 1], w2[:, 1]], axis=2)
    gpre = np.concatenate([by_partition(i["norm_pre"]), np.ones((1, P, DC), np.float32)])
    w1 = i["cmp_w1"].reshape(L, 2, CMP_LEN, HD, P).transpose(0, 1, 3, 2, 4).reshape(L, P, CMP_LEN * P)
    lb = by_partition(i["lb_param_2"]).transpose(1, 0, 2).reshape(1, P, -1)

    def ln_sets(v, neutral):
        first = np.full((1, D), neutral, np.float32)
        return np.concatenate([by_partition(np.concatenate([first, v[:-1, 2]])), by_partition(v[:, 0]),
                               by_partition(v[:, 1])], axis=2)

    s2 = np.concatenate([
        ln_sets(i["ln_g_2"], 1), ln_sets(i["ln_b_2"], 0),
        by_partition(i["pool_scale_2"]), by_partition(i["hgrn_norm_g_2"]), np.broadcast_to(lb, (L, P, 2 * HH)), flags,
        i["pool_w_2"].transpose(0, 2, 1, 3).reshape(L, P, -1)], axis=2)
    end = np.zeros((1, P, N_S2), np.float32)
    end[0, :, Q_LNG:Q_LNG + DC] = by_partition(i["ln_g_2"][-1:, 2])[0]
    end[0, :, Q_LNB:Q_LNB + DC] = by_partition(i["ln_b_2"][-1:, 2])[0]
    s2 = np.concatenate([s2, end])
    assert s1.shape[2] == N_S1 and s2.shape[2] == N_S2

    def up(k):
        g = tiles(i[f"ffn{k}_gate_2"]).reshape(L, FC, 1, P, DC * P)
        u = tiles(i[f"ffn{k}_up_2"]).reshape(L, FC, 1, P, DC * P)
        return np.concatenate([g, u], axis=2).reshape(-1, P, DC * P)

    return {
        "x": i["x"][0].T.reshape(DC, P, T).transpose(1, 0, 2), "rel": i["rel_bias"].T, "hot": hot, "msk": msk,
        "k1": k1, "k2": k2, "s1": s1, "s2": s2, "w1": w1, "gpre": gpre, "w_in": tiles(w_in), "w_out": tiles(i["w_out"]),
        "w_in_2": tiles(i["w_in_2"][:, :, in2_columns()]), "w_out_2": tiles(i["w_out_2"]), "up1": up(1), "up2": up(2),
        "down1": tiles(i["ffn1_down_2"], KH), "down2": tiles(i["ffn2_down_2"], KH),
    }


def program(nc, arrays, stop=None):
    dram = {}
    for name, a in arrays.items():
        dram[name] = nc.dram_tensor(f"in_{name}", a.shape, F32, kind="ExternalInput").ap()
    dram["scratch"] = nc.dram_tensor("bias_by_distance", (A_HEADS + C_HEADS, 2 * T), F32, kind="Internal").ap()
    dram["out"] = nc.dram_tensor("out", (P, DC, T), F32, kind="ExternalOutput").ap()
    hybrid_kernel(nc, dram, stop)


def kernel(**inputs):
    import concourse.bacc as bacc
    from concourse.bass_utils import run_bass_kernel_spmd

    arrays = {k: np.ascontiguousarray(v) for k, v in layouts({k: np.asarray(v) for k, v in inputs.items()}).items()}
    nc = bacc.Bacc("TRN2", target_bir_lowering=False, num_devices=1)
    program(nc, arrays)
    r = run_bass_kernel_spmd(nc, [{f"in_{k}": v for k, v in arrays.items()}], core_ids=[0])
    out = r.results[0]["out"]
    return np.ascontiguousarray(out.transpose(1, 0, 2).reshape(D, T).T).reshape(1, T, D)
```
